# Optimizing a Trainium2 kernel written in Bass

```python
import math
import jax, jax.numpy as jnp
from jax import lax
import numpy as np

D_MODEL = 1024
BATCH = 1
SEQ = 128
DEPTH = 2
DEC_BATCH = 1
DEC_SEQ = 512
PAST_LEN = 128

GRID_W = 64
POS_BASE = 10000.0
N_EVEN = (DEPTH + 1) // 2
N_ODD = DEPTH // 2
N_DIR = 2
A_HEADS = 12
A_HEAD_DIM = 64
D_A = A_HEADS * A_HEAD_DIM
DECAY_LORA = 64
AAA_LORA = 64
GATE_LORA = 128
B_GROUPS = 4
B_GROUP_DIM = 64
D_B = B_GROUPS * B_GROUP_DIM
D_C = 512
CONV_WIDTH = 31
D_HEADS = 4
D_HEAD_DIM = 128
D_D = D_HEADS * D_HEAD_DIM
CHUNK = 128
N_EXPERTS = 16
D_EXPERT = 1024
EC_FACTOR = 2
RMS_EPS = 1e-6
LN_EPS = 1e-5
GN_EPS = 64e-5

kernel_name = 'hybrid_rwkv7_fnet_conformer_gmlp_ec_moe_diffusion_step'

def rmsnorm(x, g):
    xf = x.astype(jnp.float32)
    y = xf * lax.rsqrt(jnp.mean(xf * xf, axis=-1, keepdims=True) + RMS_EPS)
    return (y * g.astype(jnp.float32)).astype(x.dtype)

def layernorm(x, g, b):
    xf = x.astype(jnp.float32)
    mu = jnp.mean(xf, axis=-1, keepdims=True)
    var = jnp.mean(jnp.square(xf - mu), axis=-1, keepdims=True)
    y = (xf - mu) * lax.rsqrt(var + LN_EPS) * g.astype(jnp.float32) + b.astype(jnp.float32)
    return y.astype(x.dtype)

def centred_shift(x):
    xp = jnp.pad(x, ((0, 0), (1, 1), (0, 0)))
    return 0.5 * (xp[:, :-2] + xp[:, 2:])

def modulation(cvec, w_mod, b_mod):
    m = jax.nn.silu(cvec) @ w_mod + b_mod
    return jnp.split(m[:, None, :], 6, axis=-1)

def grid_posemb(n_tokens, dtype):
    rows = n_tokens // GRID_W
    row = jnp.repeat(jnp.arange(rows, dtype=jnp.float32), GRID_W)
    col = jnp.tile(jnp.arange(GRID_W, dtype=jnp.float32), rows)
    quarter = D_MODEL // 4
    freq = 1.0 / (POS_BASE ** (jnp.arange(quarter, dtype=jnp.float32) / quarter))
    ar = row[:, None] * freq[None, :]
    ac = col[:, None] * freq[None, :]
    return jnp.concatenate([jnp.sin(ar), jnp.cos(ar), jnp.sin(ac), jnp.cos(ac)], axis=-1).astype(dtype)

def wkv7_scan(r, w, k, v, kk, a, s0):
    def step(S, inp):
        r_t, w_t, k_t, v_t, kk_t, a_t = inp
        s_kk = jnp.einsum('zbhvk,zbhk->zbhv', S, kk_t)
        S = (S * w_t[..., None, :] - s_kk[..., None] * (kk_t * a_t)[..., None, :]
             + v_t[..., :, None] * k_t[..., None, :])
        return S, jnp.einsum('zbhvk,zbhk->zbhv', S, r_t)
    xs = tuple(jnp.moveaxis(z, 2, 0) for z in (r, w, k, v, kk, a))
    s_fin, ys = lax.scan(step, s0, xs)
    return jnp.moveaxis(ys, 0, 2), s_fin

def rwkv7_mixer(h, r, k, v, s0, mu_rkv, mu_wag, w0, w1, w2, a0, a1, a2, g1, g2,
                k_k, k_a, r_k, gn_w, gn_b):
    B_, L, _ = h.shape
    f32 = jnp.float32
    heads = lambda z: z.reshape(z.shape[:-1] + (A_HEADS, A_HEAD_DIM))
    r = r + (centred_shift(r) - r) * mu_rkv[0]
    k = k + (centred_shift(k) - k) * mu_rkv[1]
    v = v + (centred_shift(v) - v) * mu_rkv[2]
    dh = centred_shift(h) - h
    xw = h + dh * mu_wag[0]
    xa = h + dh * mu_wag[1]
    xg = h + dh * mu_wag[2]
    w_pre = w0[:, None, None, :] + jnp.einsum('zblr,zrc->zblc', jnp.tanh(jnp.einsum('bld,zdr->zblr', xw, w1)), w2)
    decay = jnp.exp(-jnp.exp(-jax.nn.softplus(-w_pre.astype(f32)) - 0.5))
    icl = jax.nn.sigmoid((a0[:, None, None, :] + jnp.einsum('zblr,zrc->zblc', jnp.einsum('bld,zdr->zblr', xa, a1), a2)).astype(f32))
    gate = jax.nn.sigmoid(xg @ g1) @ g2
    kf = k.astype(f32)
    kk = heads(kf * k_k)
    kk = kk / jnp.maximum(jnp.linalg.norm(kk, axis=-1, keepdims=True), 1e-12)
    k_dir = heads(kf[None] * (1.0 + (icl - 1.0) * k_a))
    rh = heads(r.astype(f32))
    vh = heads(v.astype(f32))
    both = lambda z: jnp.stack([z, jnp.flip(z, axis=1)])
    align = lambda z: jnp.stack([z[0], jnp.flip(z[1], axis=1)])
    ys, s_fin = wkv7_scan(both(rh), align(heads(decay)), align(k_dir), both(vh), both(kk),
                          align(heads(icl)), jnp.swapaxes(s0.astype(f32), 0, 1))
    y = ys[0] + jnp.flip(ys[1], axis=1)
    mu = jnp.mean(y, axis=-1, keepdims=True)
    var = jnp.mean(jnp.square(y - mu), axis=-1, keepdims=True)
    y = (y - mu) * lax.rsqrt(var + GN_EPS) * heads(gn_w.astype(f32)) + heads(gn_b.astype(f32))
    bonus = jnp.sum(rh * heads(kf) * r_k, axis=-1, keepdims=True) * vh
    out = ((y + bonus).reshape(B_, L, D_A) * gate).astype(h.dtype)
    return out, jnp.swapaxes(s_fin, 0, 1)

def fourier_mixer(u):
    B_, L, _ = u.shape
    ug = u.reshape(B_, L, B_GROUPS, B_GROUP_DIM).astype(jnp.float32)
    f = jnp.fft.fft2(ug, axes=(1, 3), norm='ortho').real
    return f.reshape(B_, L, D_B).astype(u.dtype)

def conformer_conv(p, conv_w, conv_b, ln_g, ln_b):
    a, b = jnp.split(p, 2, axis=-1)
    x = a * jax.nn.sigmoid(b)
    pad = CONV_WIDTH // 2
    y = lax.conv_general_dilated(x, conv_w[:, None, :].astype(x.dtype), window_strides=(1,),
                                 padding=[(pad, pad)], dimension_numbers=('NWC', 'WIO', 'NWC'),
                                 feature_group_count=D_C) + conv_b
    return jax.nn.silu(layernorm(y, ln_g, ln_b))

def chunk_gating(p, ln_g, ln_b, w_s, b_s):
    p = jax.nn.gelu(p)
    u, v = jnp.split(p, 2, axis=-1)
    v = layernorm(v, ln_g, ln_b)
    B_, L, _ = v.shape
    vc = v.reshape(B_, L // CHUNK, CHUNK, D_HEADS, D_HEAD_DIM)
    mixed = jnp.einsum('hij,bnjhc->bnihc', w_s, vc) + b_s.T[None, None, :, :, None]
    return u * mixed.reshape(B_, L, D_D)

def expert_choice_ffn(h, w_router, b_router, w_gate, w_up, w_down):
    B_, L, D = h.shape
    cap = EC_FACTOR * L // N_EXPERTS
    logits = (h @ w_router).astype(jnp.float32) + b_router.astype(jnp.float32)
    aff = jax.nn.softmax(logits, axis=-1)
    vals, idx = lax.top_k(jnp.swapaxes(aff, 1, 2), cap)
    xs = jax.vmap(lambda hb, ib: hb[ib])(h, idx)
    hid = jax.nn.silu(jnp.einsum('becd,edf->becf', xs, w_gate)) * jnp.einsum('becd,edf->becf', xs, w_up)
    ys = (jnp.einsum('becf,efd->becd', hid, w_down) * vals[..., None]).astype(h.dtype)
    return jax.vmap(lambda ib, yb: jnp.zeros((L, D), yb.dtype).at[ib.reshape(-1)].add(yb.reshape(-1, D)))(idx, ys)

def run_trunk(x, cvec, s_init, P):
    states = []
    for l in range(DEPTH):
        j = l // 2
        sh1, sc1, gt1, sh2, sc2, gt2 = modulation(cvec, P['mod_w'][l], P['mod_b'][l])
        h = rmsnorm(x, P['norm_mix'][l]) * (1.0 + sc1) + sh1
        if l % 2 == 0:
            proj = h @ P['ev_w_in'][j]
            r, k, v, u = jnp.split(proj, [D_A, 2 * D_A, 3 * D_A], axis=-1)
            o_a, s_fin = rwkv7_mixer(h, r, k, v, s_init[:, j], P['ev_mu_rkv'][j], P['ev_mu_wag'][j],
                                     P['ev_w0'][j], P['ev_w1'][j], P['ev_w2'][j],
                                     P['ev_a0'][j], P['ev_a1'][j], P['ev_a2'][j],
                                     P['ev_g1'][j], P['ev_g2'][j], P['ev_k_k'][j], P['ev_k_a'][j],
                                     P['ev_r_k'][j], P['ev_gn_w'][j], P['ev_gn_b'][j])
            o_b = fourier_mixer(u)
            mixed = jnp.concatenate([o_a, o_b.astype(o_a.dtype)], axis=-1) @ P['ev_w_out'][j]
            states.append(s_fin)
        else:
            proj = h @ P['od_w_in'][j]
            pc, pd = jnp.split(proj, [2 * D_C], axis=-1)
            o_c = conformer_conv(pc, P['od_conv_w'][j], P['od_conv_b'][j], P['od_cln_g'][j], P['od_cln_b'][j])
            o_d = chunk_gating(pd, P['od_vln_g'][j], P['od_vln_b'][j], P['od_w_s'][j], P['od_b_s'][j])
            mixed = jnp.concatenate([o_c, o_d], axis=-1) @ P['od_w_out'][j]
        x = x + gt1 * mixed
        h2 = rmsnorm(x, P['norm_ffn'][l]) * (1.0 + sc2) + sh2
        x = x + gt2 * expert_choice_ffn(h2, P['moe_router'][l], P['moe_router_b'][l],
                                        P['moe_w_gate'][l], P['moe_w_up'][l], P['moe_w_down'][l])
    return rmsnorm(x, P['final_norm']), jnp.stack(states, axis=1)

def setup_inputs(seed: int = 0) -> dict:
    key = jax.random.key(seed)
    keys = jax.random.split(key, 48)

    def nrm(i, shape, scale):
        return jax.random.normal(keys[i], shape, jnp.float32) * scale

    def uni(i, shape, lo, hi):
        return jax.random.uniform(keys[i], shape, jnp.float32, lo, hi)

    D = D_MODEL
    return {
        'x_prompt': nrm(0, (BATCH, SEQ, D), 1.0),
        'x_sample': nrm(1, (DEC_BATCH, DEC_SEQ, D), 1.0),
        'state_wkv': nrm(2, (DEC_BATCH, N_EVEN, N_DIR, A_HEADS, A_HEAD_DIM, A_HEAD_DIM), 1.0),
        'c': nrm(3, (DEC_BATCH, D), 1.0),
        'c_ctx': nrm(4, (D,), 1.0),
        'mod_w': nrm(5, (DEPTH, D, 6 * D), 0.5 * D ** -0.5),
        'mod_b': nrm(6, (DEPTH, 6 * D), 0.02),
        'norm_mix': 1.0 + nrm(7, (DEPTH, D), 0.05),
        'norm_ffn': 1.0 + nrm(8, (DEPTH, D), 0.05),
        'final_norm': 1.0 + nrm(9, (D,), 0.05),
        'ev_w_in': nrm(10, (N_EVEN, D, 3 * D_A + D_B), D ** -0.5),
        'ev_w_out': nrm(11, (N_EVEN, D_A + D_B, D), (D_A + D_B) ** -0.5),
        'ev_mu_rkv': uni(12, (N_EVEN, 3, D_A), 0.0, 1.0),
        'ev_mu_wag': uni(13, (N_EVEN, 3, D), 0.0, 1.0),
        'ev_w0': uni(14, (N_EVEN, N_DIR, D_A), -5.0, 1.0),
        'ev_w1': nrm(15, (N_EVEN, N_DIR, D, DECAY_LORA), D ** -0.5),
        'ev_w2': nrm(16, (N_EVEN, N_DIR, DECAY_LORA, D_A), 0.5 * DECAY_LORA ** -0.5),
        'ev_a0': nrm(17, (N_EVEN, N_DIR, D_A), 0.3),
        'ev_a1': nrm(18, (N_EVEN, N_DIR, D, AAA_LORA), D ** -0.5),
        'ev_a2': nrm(19, (N_EVEN, N_DIR, AAA_LORA, D_A), 0.5 * AAA_LORA ** -0.5),
        'ev_g1': nrm(20, (N_EVEN, D, GATE_LORA), D ** -0.5),
        'ev_g2': nrm(21, (N_EVEN, GATE_LORA, D_A), GATE_LORA ** -0.5),
        'ev_k_k': 0.85 + nrm(22, (N_EVEN, D_A), 0.05),
        'ev_k_a': 1.0 + nrm(23, (N_EVEN, D_A), 0.05),
        'ev_r_k': nrm(24, (N_EVEN, A_HEADS, A_HEAD_DIM), 0.1),
        'ev_gn_w': 1.0 + nrm(25, (N_EVEN, D_A), 0.05),
        'ev_gn_b': nrm(26, (N_EVEN, D_A), 0.02),
        'od_w_in': nrm(27, (N_ODD, D, 2 * D_C + 2 * D_D), D ** -0.5),
        'od_w_out': nrm(28, (N_ODD, D_C + D_D, D), (D_C + D_D) ** -0.5),
        'od_conv_w': nrm(29, (N_ODD, CONV_WIDTH, D_C), CONV_WIDTH ** -0.5),
        'od_conv_b': nrm(30, (N_ODD, D_C), 0.02),
        'od_cln_g': 1.0 + nrm(31, (N_ODD, D_C), 0.05),
        'od_cln_b': nrm(32, (N_ODD, D_C), 0.02),
        'od_vln_g': 1.0 + nrm(33, (N_ODD, D_D), 0.05),
        'od_vln_b': nrm(34, (N_ODD, D_D), 0.02),
        'od_w_s': nrm(35, (N_ODD, D_HEADS, CHUNK, CHUNK), CHUNK ** -0.5),
        'od_b_s': 1.0 + nrm(36, (N_ODD, D_HEADS, CHUNK), 0.1),
        'moe_router': nrm(37, (DEPTH, D, N_EXPERTS), D ** -0.5),
        'moe_router_b': nrm(38, (DEPTH, N_EXPERTS), 0.01),
        'moe_w_gate': nrm(39, (DEPTH, N_EXPERTS, D, D_EXPERT), D ** -0.5),
        'moe_w_up': nrm(40, (DEPTH, N_EXPERTS, D, D_EXPERT), D ** -0.5),
        'moe_w_down': nrm(41, (DEPTH, N_EXPERTS, D_EXPERT, D), D_EXPERT ** -0.5),
    }

def reference(x_prompt, x_sample, state_wkv, c, c_ctx, mod_w, mod_b, norm_mix, norm_ffn, final_norm,
              ev_w_in, ev_w_out, ev_mu_rkv, ev_mu_wag, ev_w0, ev_w1, ev_w2, ev_a0, ev_a1, ev_a2,
              ev_g1, ev_g2, ev_k_k, ev_k_a, ev_r_k, ev_gn_w, ev_gn_b,
              od_w_in, od_w_out, od_conv_w, od_conv_b, od_cln_g, od_cln_b, od_vln_g, od_vln_b,
              od_w_s, od_b_s, moe_router, moe_router_b, moe_w_gate, moe_w_up, moe_w_down):
    P = dict(mod_w=mod_w, mod_b=mod_b, norm_mix=norm_mix, norm_ffn=norm_ffn, final_norm=final_norm,
             ev_w_in=ev_w_in, ev_w_out=ev_w_out, ev_mu_rkv=ev_mu_rkv, ev_mu_wag=ev_mu_wag,
             ev_w0=ev_w0, ev_w1=ev_w1, ev_w2=ev_w2, ev_a0=ev_a0, ev_a1=ev_a1, ev_a2=ev_a2,
             ev_g1=ev_g1, ev_g2=ev_g2, ev_k_k=ev_k_k, ev_k_a=ev_k_a, ev_r_k=ev_r_k,
             ev_gn_w=ev_gn_w, ev_gn_b=ev_gn_b,
             od_w_in=od_w_in, od_w_out=od_w_out, od_conv_w=od_conv_w, od_conv_b=od_conv_b,
             od_cln_g=od_cln_g, od_cln_b=od_cln_b, od_vln_g=od_vln_g, od_vln_b=od_vln_b,
             od_w_s=od_w_s, od_b_s=od_b_s, moe_router=moe_router, moe_router_b=moe_router_b,
             moe_w_gate=moe_w_gate, moe_w_up=moe_w_up, moe_w_down=moe_w_down)
    s_zero = jnp.zeros((x_prompt.shape[0], N_EVEN, N_DIR, A_HEADS, A_HEAD_DIM, A_HEAD_DIM), jnp.float32)
    y_prompt, new_state_wkv = run_trunk(x_prompt, c_ctx[None, :], s_zero, P)
    x_lat = x_sample + grid_posemb(x_sample.shape[1], x_sample.dtype)[None]
    y_sample, _ = run_trunk(x_lat, c, state_wkv, P)
    return (y_prompt, y_sample, new_state_wkv)


_drawn_inputs = setup_inputs


def setup_inputs(seed=0):
    import zlib

    import numpy as np

    out = dict(_drawn_inputs(seed))
    spreads = {}
    factors = {'state_wkv': 3.486,
     'norm_ffn': 3.974,
     'ev_gn_w': 5.918,
     'ev_gn_b': 8.0,
     'od_conv_b': 8.0,
     'od_cln_g': 6.566,
     'od_cln_b': 8.0,
     'od_vln_g': 7.472,
     'od_vln_b': 8.0,
     'od_b_s': 3.791,
     'moe_router_b': 8.0}
    for name, (base, spread) in spreads.items():
        noise = np.random.default_rng([zlib.crc32(name.encode()), seed]).standard_normal(out[name].shape)
        drawn = base * np.exp(spread * noise) if base else spread * noise
        out[name] = __import__('jax').numpy.asarray(drawn.astype(out[name].dtype))
    for name, factor in factors.items():
        out[name] = (out[name] * factor).astype(out[name].dtype)
    return out
```

```python
from contextlib import ExitStack, contextmanager

import numpy as np
import concourse.bass as bass
from concourse import mybir

ALU = mybir.AluOpType
ACT = mybir.ActivationFunctionType
AX = mybir.AxisListType
F32 = mybir.dt.float32
U8 = mybir.dt.uint8
U32 = mybir.dt.uint32

P = 128
D = 1024
KC = D // P
NS, NP = 512, 128
T = NS + NP
NT = T // P
ST = NS // P
SEGS = ((0, 0, NS), (1, NS, T))
HP = 6
HD = 64
E = 16
CAPS, CAPP = 2 * NS // E, 2 * NP // E
CAP = CAPS + CAPP
LEVELS = 6
TAPS = 31
EXPH = float(np.exp(-0.5))
RMS_EPS, LN_EPS, GN_EPS = 1e-6, 1e-5, 64e-5

VEC = {}
_n = 0
for _name, _w in (("mod_b", 96), ("norm_mix", 16), ("norm_ffn", 16), ("final", 8), ("mu_wag", 24), ("cond", 16),
                  ("conv_w", 4 * TAPS), ("conv_b", 4), ("cln_g", 4), ("cln_b", 4), ("vln_g", 4), ("vln_b", 4)):
    VEC[_name] = (_n, _n + _w)
    _n += _w
NVEC = _n
CST = {}
_n = 0
for _name, _w in (("ident", 128), ("headones", 128), ("iota", 64), ("dft64", 256), ("posrow", 32), ("poscol", 256),
                  ("tri", 1024)):
    CST[_name] = (_n, _n + _w)
    _n += _w
NCST = _n
HPV = dict(mu=0, w0=3, a0=5, k_k=7, k_a=8, r_k=9, gn_w=10, gn_b=11)
NHPV = 12


def bcast(ap, axis, n):
    ap = ap.unsqueeze(axis)
    shape = list(ap.shape)
    shape[axis] = n
    return ap.broadcast_to(shape)


def build(nc, t, stop=99):
    ctx = ExitStack()
    with ctx:
        def sb(name, shape, dt=F32):
            return ctx.enter_context(nc.sbuf_tensor(name, shape, dt))

        lasting, passing = {}, {}
        scope = []

        def sem(name):
            if name.startswith(("slab", "act_done", "dve_done", "pool_done", "sp_done", "pe_done")):
                if name not in lasting:
                    lasting[name] = ctx.enter_context(nc.semaphore(name))
                return lasting[name]
            if name not in passing:
                passing[name] = scope[-1].enter_context(nc.semaphore(name))
            return passing[name]

        @contextmanager
        def stage():
            with ExitStack() as names:
                scope.append(names)
                with nc.Block() as block:
                    yield block
                scope.pop()
                passing.clear()

        x = sb("x", [P, KC, T])
        h = sb("h", [P, KC, T])
        mix = sb("mix", [P, KC, T])
        vec = sb("vec", [P, NVEC])
        cst = sb("cst", [P, NCST])
        m8 = sb("m8", [P, LEVELS + 1, 2, P], U8)
        mod = sb("mod", [P, 2, 6, KC, 2])
        gain = sb("gain", [P, 4, KC, 2])
        mean1024 = sb("mean1024", [P, P])
        mean512 = sb("mean512", [P, P])
        ones = sb("ones", [P, P])
        lora = sb("lora", [P, 3, T])
        slot = sb("slot", [P, NT, E])
        aff = sb("aff", [P, NT, E])
        eps = sb("eps", [P, 3])
        WKN = 32200
        wk = sb("wk", [P, WKN])
        ps = ctx.enter_context(nc.psum_tensor("ps", [P, 8, 512], F32))
        psf = ps[:, :, :].rearrange("p b n -> p (b n)")

        def pair(q):
            return psf[:, q * 1024:q * 1024 + T]

        def V(name, a=0, b=None):
            lo, hi = VEC[name]
            return vec[:, lo + a:(lo + b) if b is not None else hi]

        def C(name):
            lo, hi = CST[name]
            return cst[:, lo:hi]

        class Carve:

            def __init__(self, at=0):
                self.at = at

            def __call__(self, *shape, parts=P):
                n = int(np.prod(shape))
                ap = wk[0:parts, self.at:self.at + n]
                self.at += n
                assert self.at <= WKN, self.at
                if len(shape) == 1:
                    return ap
                names = "abcde"[:len(shape)]
                kw = {names[i]: shape[i] for i in range(1, len(shape))}
                return ap.rearrange(f"p ({' '.join(names)}) -> p {' '.join(names)}", **kw)

        ident = C("ident")
        for name in [f"slab{n}" for n in range(6)] + ["slab_free"] + ["act_done", "dve_done", "pool_done", "sp_done", "pe_done"]:
            sem(name)
        act_done, dve_done, pool_done, sp_done = (sem(e + "_done") for e in ("act", "dve", "pool", "sp"))

        ring = Carve()(6, 4, 1024)

        def half_rows(w, k):
            return w[k * 512:(k + 1) * 512, :].rearrange("(c p) n -> p c n", p=P)

        def setup():
            cv = Carve(24576)
            th = cv(KC, 2)
            scond = cv(KC, 2)
            m32 = cv((LEVELS + 1) * 2 * P)
            modw = t["mod_w"]

            with stage() as block:
                @block.sync
                def _(sp):
                    sp.dma_start(vec[:, :], t["vec"]).then_inc(sem("vec_in"), 16)
                    sp.dma_start(cst[:, :], t["cst"]).then_inc(sem("const_in"), 16)
                    sp.dma_start(m32, t["m8"]).then_inc(sem("const_in"), 16)
                    sp.sem_inc(sem("slab_free"), 6)
                    for l in range(2):
                        with sp.Fori(0, 2) as i:
                            for s in range(3):
                                for k in range(2):
                                    sp.wait_ge(sem("slab_free"), 1).then_inc(sem("slab_free"), -1)
                                    src = modw[l, k * 512:(k + 1) * 512, :].rearrange("(c p) (i s n) -> i s p c n", p=P, i=2, s=3)
                                    sp.dma_start(ring[:, 2 * s + k], src[bass.ds(i, 1), s].rearrange("a p c n -> p (a c) n")).then_inc(sem(f"slab{2 * s + k}"), 16)
                        if l == 0:
                            sp.dma_start(x[:, :, :], t["xT"].rearrange("(c p) n -> p c n", p=P)).then_inc(sem("x_in"), 16)
                    sp.wait_ge(sem("slab_free"), 6).then_inc(sem("slab_free"), -6)
                    sp.wait_ge(sem("x_in"), 16).then_inc(sem("x_in"), -16)
                    sp.sem_inc(sem("x_here"), 1)
                    sp.sem_inc(sem("x_here2"), 1)

                @block.scalar
                def _(act):
                    act.wait_ge(sem("vec_in"), 16).then_inc(sem("vec_in"), -16)
                    act.activation(th, V("cond").rearrange("p (c r) -> p c r", r=2), ACT.Tanh, scale=0.5).then_inc(act_done, 1)
                    act.wait_ge(act_done, 1).then_inc(act_done, -1)
                    act.sem_inc(sem("th"), 1)

                @block.tensor
                def _(pe):
                    pe.wait_ge(sem("scond"), 1).then_inc(sem("scond"), -1)
                    for l in range(2):
                        with pe.Fori(0, 2) as i:
                            for s in range(3):
                                for k in range(2):
                                    pe.wait_ge(sem(f"slab{2 * s + k}"), 16).then_inc(sem(f"slab{2 * s + k}"), -16)
                                for j in range(KC):
                                    for c in range(KC):
                                        last = pe.matmul(ps[:, s, 2 * j:2 * j + 2], ring[:, 2 * s + c // 4, c % 4, j * P:(j + 1) * P],
                                                        scond[:, c, :], start=c == 0, stop=c == KC - 1)
                                last.then_inc(sem("mod_done"), 1)
                                pe.wait_ge(sem("mod_read"), 1).then_inc(sem("mod_read"), -1)
                                pe.sem_inc(sem("slab_free"), 2)

                @block.vector
                def _(dve):
                    dve.wait_ge(sem("th"), 1).then_inc(sem("th"), -1)
                    cond = V("cond").rearrange("p (c r) -> p c r", r=2)
                    dve.scalar_tensor_tensor(scond, th, 1.0, cond, ALU.add, ALU.mult).then_inc(dve_done, 1)
                    dve.wait_ge(dve_done, 1).then_inc(dve_done, -1)
                    dve.tensor_scalar(scond, scond, 0.5, None, ALU.mult).then_inc(dve_done, 1)
                    dve.wait_ge(dve_done, 1).then_inc(dve_done, -1)
                    dve.sem_inc(sem("scond"), 1)
                    modv = mod[:, :, :, :, :].rearrange("p l (i s) j r -> p l i s j r", i=2)
                    modb = V("mod_b").rearrange("p (l i s j) -> p l i s j", l=2, i=2, s=3)
                    for l in range(2):
                        with dve.Fori(0, 2) as i:
                            for s in range(3):
                                dve.wait_ge(sem("mod_done"), 1).then_inc(sem("mod_done"), -1)
                                out = modv[:, l, bass.ds(i, 1), s].rearrange("p a j r -> p (a j) r")
                                b = modb[:, l, bass.ds(i, 1), s].rearrange("p a j -> p (a j)")
                                dve.tensor_tensor(out, ps[:, s, 0:16].rearrange("p (j r) -> p j r", r=2), bcast(b, 2, 2), ALU.add).then_inc(dve_done, 1)
                                dve.wait_ge(dve_done, 1).then_inc(dve_done, -1)
                                dve.sem_inc(sem("mod_read"), 1)
                    for l in range(2):
                        for n, (part, g) in enumerate(((1, "norm_mix"), (4, "norm_ffn"))):
                            dve.scalar_tensor_tensor(gain[:, 2 * l + n], mod[:, l, part], 1.0,
                                                        bcast(V(g, 8 * l, 8 * l + 8), 2, 2), ALU.add, ALU.mult).then_inc(dve_done, 1)
                    dve.wait_ge(dve_done, 4).then_inc(dve_done, -4)

                @block.gpsimd
                def _(pool):
                    pool.memset(mean1024[:, :], 1.0 / D).then_inc(pool_done, 1)
                    pool.memset(mean512[:, :], 1.0 / 512).then_inc(pool_done, 1)
                    pool.memset(ones[:, :], 1.0).then_inc(pool_done, 1)
                    for n, v in enumerate((RMS_EPS, LN_EPS, GN_EPS)):
                        pool.memset(eps[:, n:n + 1], v).then_inc(pool_done, 1)
                    pool.wait_ge(pool_done, 6).then_inc(pool_done, -6)
                    pool.wait_ge(sem("const_in"), 32).then_inc(sem("const_in"), -32)
                    pool.tensor_copy(m8[:, :, :, :].rearrange("p l z n -> p (l z n)"), m32).then_inc(pool_done, 1)
                    pool.wait_ge(sem("x_here"), 1).then_inc(sem("x_here"), -1)
                    pool.wait_ge(sem("x_here2"), 1).then_inc(sem("x_here2"), -1)
                    row = C("posrow").rearrange("p (c r) -> p c r", c=4)
                    col = C("poscol").rearrange("p (c w) -> p c w", c=4)
                    for c in range(4):
                        g = x[:, c, 0:NS].rearrange("p (r w) -> p r w", w=64)
                        pool.tensor_tensor(g, g, bcast(row[:, c], 2, 64), ALU.add).then_inc(pool_done, 1)
                        g = x[:, c + 4, 0:NS].rearrange("p (r w) -> p r w", w=64)
                        pool.tensor_tensor(g, g, bcast(col[:, c], 1, 8), ALU.add).then_inc(pool_done, 1)
                    pool.wait_ge(pool_done, 9).then_inc(pool_done, -9)

        def norm(l, n, prefetch=None):
            cv = Carve(24576 if prefetch else 0)
            sq = cv(2, T)
            root = cv(T)
            rstd = cv(T)

            with stage() as block:
                @block.scalar
                def _(act):
                    for c in range(KC):
                        if c >= 2:
                            act.wait_ge(sem("sq_used"), 1).then_inc(sem("sq_used"), -1)
                        act.activation(sq[:, c % 2], x[:, c], ACT.Square).then_inc(act_done, 1)
                        act.wait_ge(act_done, 1).then_inc(act_done, -1)
                        act.sem_inc(sem("sq_ready"), 1)
                    act.wait_ge(sem("sq_used"), 2).then_inc(sem("sq_used"), -2)
                    act.wait_ge(sem("mean_ready"), 1).then_inc(sem("mean_ready"), -1)
                    act.activation(root, pair(0), ACT.Sqrt, bias=eps[:, 0:1]).then_inc(act_done, 1)
                    act.wait_ge(act_done, 1).then_inc(act_done, -1)
                    act.sem_inc(sem("root_ready"), 1)
                    for c in range(KC):
                        act.wait_ge(sem("scaled"), 1).then_inc(sem("scaled"), -1)
                        if n is None:
                            act.mul(h[:, c], h[:, c], V("final", c, c + 1)).then_inc(act_done, 1)
                            continue
                        for r, a, b in SEGS:
                            act.activation(h[:, c, a:b], h[:, c, a:b], ACT.Identity, scale=gain[:, 2 * l + n, c, r:r + 1],
                                              bias=mod[:, l, 3 * n, c, r:r + 1]).then_inc(act_done, 1)
                    act.wait_ge(act_done, KC if n is None else 2 * KC).then_inc(act_done, -(KC if n is None else 2 * KC))
                    if n is None:
                        act.sem_inc(sem("final_ready"), 1)

                @block.tensor
                def _(pe):
                    for c in range(KC):
                        pe.wait_ge(sem("sq_ready"), 1).then_inc(sem("sq_ready"), -1)
                        for a, b in ((0, NS), (NS, T)):
                            last = pe.matmul(pair(0)[:, a:b], mean1024[:, :], sq[:, c % 2, a:b], start=c == 0, stop=c == KC - 1)
                        last.then_inc(sem("sq_used"), 1)
                    pe.drain().then_inc(sem("mean_ready"), 1)

                @block.vector
                def _(dve):
                    dve.wait_ge(sem("root_ready"), 1).then_inc(sem("root_ready"), -1)
                    dve.reciprocal(rstd, root).then_inc(dve_done, 1)
                    dve.wait_ge(dve_done, 1).then_inc(dve_done, -1)
                    for c in range(KC):
                        dve.tensor_tensor(h[:, c], x[:, c], rstd, ALU.mult).then_inc(dve_done, 1)
                        dve.wait_ge(dve_done, 1).then_inc(dve_done, -1)
                        dve.sem_inc(sem("scaled"), 1)

                @block.sync
                def _(sp):
                    if n is None:
                        sp.wait_ge(sem("final_ready"), 1).then_inc(sem("final_ready"), -1)
                        sp.dma_start(t["yT"].rearrange("(c p) n -> p c n", p=P), h[:, :, :]).then_inc(sem("y_out"), 16)
                        sp.wait_ge(sem("y_out"), 16).then_inc(sem("y_out"), -16)
                        return
                    if prefetch:
                        prefetch(sp)

        def out_x():
            with stage() as block:
                @block.sync
                def _(sp):
                    sp.dma_start(t["yT"].rearrange("(c p) n -> p c n", p=P), x[:, :, :]).then_inc(sem("y_out"), 16)
                    sp.wait_ge(sem("y_out"), 16).then_inc(sem("y_out"), -16)

        def even_front():
            cv = Carve()
            dh = cv(KC, T)
            xm = cv(2, KC, T)
            w1 = cv(KC, 3, P)
            wu = cv(KC, 256)
            ufeat = cv(2, T)
            utok = cv(NT, 2, 2, P)
            dfs = cv(4, 2, NS)
            dfp = cv(2, NP)
            dft64 = C("dft64")

            with stage() as block:
                @block.sync
                def _(sp):
                    sp.dma_start(w1, t["lora1"].rearrange("(c p) (s n) -> p c s n", p=P, s=3)).then_inc(sem("w1_in"), 16)
                    sp.dma_start(wu, t["ev_w_in"][:, 3 * 768:].rearrange("(c p) n -> p c n", p=P)).then_inc(sem("wu_in"), 16)
                    sp.dma_start(dfs, t["dft_s"].rearrange("p (c k n) -> p c k n", c=4, k=2)).then_inc(sem("dft_in"), 16)
                    sp.dma_start(dfp, t["dft_p"].rearrange("p (k n) -> p k n", k=2)).then_inc(sem("dft_in"), 16)

                @block.vector
                def _(dve):
                    for c in range(KC):
                        dve.tensor_tensor(dh[:, c, 1:T - 1], h[:, c, 0:T - 2], h[:, c, 2:T], ALU.add).then_inc(dve_done, 1)
                    dve.wait_ge(dve_done, 8).then_inc(dve_done, -8)
                    dve.tensor_copy(dh[:, :, 0:NS + 1:NS], h[:, :, 1:NS + 2:NS]).then_inc(dve_done, 1)
                    dve.tensor_copy(dh[:, :, NS - 1:T:NP], h[:, :, NS - 2:T - 1:NP]).then_inc(dve_done, 1)
                    dve.wait_ge(dve_done, 2).then_inc(dve_done, -2)
                    for c in range(KC):
                        dve.scalar_tensor_tensor(dh[:, c], dh[:, c], 0.5, h[:, c], ALU.mult, ALU.subtract).then_inc(dve_done, 1)
                    dve.wait_ge(dve_done, 8).then_inc(dve_done, -8)
                    mu = V("mu_wag").rearrange("p (s c) -> p s c", s=3)
                    for s in range(3):
                        if s >= 2:
                            dve.wait_ge(sem("xm_used"), 1).then_inc(sem("xm_used"), -1)
                        for c in range(KC):
                            dve.scalar_tensor_tensor(xm[:, s % 2, c], dh[:, c], mu[:, s, c:c + 1], h[:, c], ALU.mult, ALU.add).then_inc(dve_done, 1)
                        dve.wait_ge(dve_done, 8).then_inc(dve_done, -8)
                        dve.sem_inc(sem("xm_ready"), 1)
                    dve.wait_ge(sem("xm_used"), 2).then_inc(sem("xm_used"), -2)
                    dve.wait_ge(sem("half_sigmoid"), 1).then_inc(sem("half_sigmoid"), -1)
                    dve.tensor_scalar(lora[:, 2], lora[:, 2], 0.5, 0.5, ALU.mult, ALU.add).then_inc(dve_done, 1)
                    dve.wait_ge(dve_done, 1).then_inc(dve_done, -1)

                @block.tensor
                def _(pe):
                    pe.wait_ge(sem("w1_in"), 16).then_inc(sem("w1_in"), -16)
                    for s in range(3):
                        pe.wait_ge(sem("xm_ready"), 1).then_inc(sem("xm_ready"), -1)
                        for a, b in ((0, NS), (NS, T)):
                            for c in range(KC):
                                last = pe.matmul(pair(s)[:, a:b], w1[:, c, s], xm[:, s % 2, c, a:b], start=c == 0, stop=c == KC - 1)
                        last.then_inc(sem("xm_used"), 1)
                        pe.drain().then_inc(sem("lora_ready"), 1)
                    pe.wait_ge(sem("wu_in"), 16).then_inc(sem("wu_in"), -16)
                    for m in range(2):
                        pe.wait_ge(sem("lora_read"), 1).then_inc(sem("lora_read"), -1)
                        for a, b in ((0, NS), (NS, T)):
                            for c in range(KC):
                                last = pe.matmul(pair(m)[:, a:b], wu[:, c, m * P:(m + 1) * P], h[:, c, a:b], start=c == 0, stop=c == KC - 1)
                        last.then_inc(sem("u_ready"), 1)
                    pe.wait_ge(sem("u_sbuf"), 1).then_inc(sem("u_sbuf"), -1)
                    pe.wait_ge(sem("lora_read"), 1).then_inc(sem("lora_read"), -1)
                    for tt in range(NT):
                        b = 4 + tt % 2
                        if tt >= 2:
                            pe.wait_ge(sem("utok_copied"), 1).then_inc(sem("utok_copied"), -1)
                        for m in range(2):
                            last = pe.matmul(ps[:, b, m * 256:(m + 1) * 256], ufeat[:, m, tt * P:(tt + 1) * P], dft64, start=True, stop=True)
                        last.then_inc(sem("utok_ready"), 1)
                    pe.wait_ge(sem("utok_copied"), 2).then_inc(sem("utok_copied"), -2)
                    pe.wait_ge(sem("dft_in"), 32).then_inc(sem("dft_in"), -32)
                    for m in range(2):
                        for tt in range(ST):
                            for k in range(2):
                                pe.matmul(pair(m)[:, 0:NS], utok[:, tt, m, k], dfs[:, tt, k], start=tt + k == 0, stop=(tt, k) == (ST - 1, 1))
                        for k in range(2):
                            last = pe.matmul(pair(m)[:, NS:T], utok[:, ST, m, k], dfp[:, k], start=k == 0, stop=k == 1)
                        last.then_inc(sem("fourier_ready"), 1)

                @block.scalar
                def _(act):
                    for s in range(3):
                        act.wait_ge(sem("lora_ready"), 1).then_inc(sem("lora_ready"), -1)
                        act.activation(lora[:, s], pair(s), ACT.Copy if s == 1 else ACT.Tanh, scale=(1.0, 1.0, 0.5)[s]).then_inc(act_done, 1)
                        act.wait_ge(act_done, 1).then_inc(act_done, -1)
                        act.sem_inc(sem("lora_read"), 1)
                    act.sem_inc(sem("half_sigmoid"), 1)
                    for m in range(2):
                        act.wait_ge(sem("u_ready"), 1).then_inc(sem("u_ready"), -1)
                        act.activation(ufeat[:, m], pair(m), ACT.Copy).then_inc(act_done, 1)
                    act.wait_ge(act_done, 2).then_inc(act_done, -2)
                    act.sem_inc(sem("u_sbuf"), 1)
                    for tt in range(NT):
                        act.wait_ge(sem("utok_ready"), 1).then_inc(sem("utok_ready"), -1)
                        act.activation(utok[:, tt].rearrange("p m k n -> p (m k n)"), ps[:, 4 + tt % 2], ACT.Copy).then_inc(act_done, 1)
                        act.wait_ge(act_done, 1).then_inc(act_done, -1)
                        act.sem_inc(sem("utok_copied"), 1)
                    for m in range(2):
                        act.wait_ge(sem("fourier_ready"), 1).then_inc(sem("fourier_ready"), -1)
                        act.activation(mix[:, HP + m], pair(m), ACT.Copy).then_inc(act_done, 1)
                    act.wait_ge(act_done, 2).then_inc(act_done, -2)

        def even_heads():
            ca = Carve()
            mat = ca(NT, 2, 2, 4, P)
            inv = ca(NT, 4, P)
            invT = ca(NT, 4, P)
            end = ca.at
            ct = Carve()
            raw = ct(3, T)
            shf = ct(3, T)
            rkv = ct(3, T)
            icl = ct(2, T)
            lw = ct(2, T)
            cum = ct(NT, P)
            rel = ct(2, NT, P + 1)
            kq = ct(T)
            sq = ct(T)
            kk = ct(T)
            eP = ct(2, NT, P + 1)
            eN = ct(2, NT, P + 1)
            assert ct.at <= end, (ct.at, end)
            cg = Carve(end - 2 * NT * 4 * P)
            ysb = cg(T)
            yc = cg(T)
            root = cg(T)
            ysq = cg(T)
            cb = Carve(end)
            win = cb(KC, 3, P)
            w2 = cb(3, P)
            hpv = cb(NHPV)
            hv = cb(NHPV + 5)
            ar = cb(2, NT, 2, P)
            nb = cb(2, NT, P)
            kp = cb(2, NT, P)
            yw = wk[:, cb.at - 2 * T * 2:cb.at].rearrange("p (g u n) -> p g u n", g=NT, u=4)
            tokm = cb(NT, 4, P)
            vtok = cb(NT, P)
            s0 = cb(2, NT, HD)
            us = cb(2, NT, P)
            rs = cb(4, P)
            bon = cb(T)
            gate = cb(T)
            ec = cb(2, NT)
            ctr = cb(NT)
            stin = cb(2, HD)
            sout = cb(2, HD)
            stmp = cb(4, HD)
            headones = C("headones")
            tri = C("tri").rearrange("p (z n) -> p z n", z=2)
            lv = m8

            steps = [[(0, j), (1, ST - 1 - j)] + ([(0, ST), (1, ST)] if j == 0 else []) for j in range(ST)]

            with stage() as block:
                @block.sync
                def _(sp):
                    with sp.Fori(0, HP) as i:
                        wv = t["ev_w_in"][:, 0:2304].rearrange("(c p) (s q n) -> q s p c n", p=P, s=3, q=HP)
                        for s in range(3):
                            sp.dma_start(win[:, :, s], wv[bass.ds(i, 1), s].rearrange("a p c n -> p (a c) n")).then_inc(sem("win_in"), 16)
                        sp.dma_start(w2, t["lora2"].rearrange("s p (q n) -> q p s n", q=HP)[bass.ds(i, 1)].rearrange("a p s n -> p (a s) n")).then_inc(sem("win_in"), 16)
                        sp.dma_start(hpv, t["hpv"][bass.ds(i, 1)].rearrange("a p n -> p (a n)")).then_inc(sem("hpv_in"), 16)
                        sp.dma_start(stin, t["state"].rearrange("z q p v -> q p z v")[bass.ds(i, 1)].rearrange("a p z v -> p (a z) v")).then_inc(sem("state_in"), 16)
                        sp.wait_ge(sem("sout_ready"), 1).then_inc(sem("sout_ready"), -1)
                        sp.dma_start(t["st_out"].rearrange("z q p v -> q p z v")[bass.ds(i, 1)].rearrange("a p z v -> p (a z) v"), sout).then_inc(sem("state_out"), 16)
                        sp.wait_ge(sem("state_out"), 16).then_inc(sem("state_out"), -16)
                        sp.wait_ge(sem("heads_done_sp"), 1).then_inc(sem("heads_done_sp"), -1)

                @block.tensor
                def _(pe):
                    with pe.Fori(0, HP) as i:
                        pe.wait_ge(sem("win_in"), 64).then_inc(sem("win_in"), -64)
                        for s in range(3):
                            for a, b in ((0, NS), (NS, T)):
                                for c in range(KC):
                                    last = pe.matmul(pair(s)[:, a:b], win[:, c, s], h[:, c, a:b], start=c == 0, stop=c == KC - 1)
                            last.then_inc(sem("proj_ready"), 1)
                        for n, (q, s, z) in enumerate(((3, 0, 0), (0, 0, 1), (1, 1, 0), (2, 1, 1), (3, 2, None))):
                            if n:
                                pe.wait_ge(sem("proj_read"), 1).then_inc(sem("proj_read"), -1)
                            lo, hi = (0, P) if z is None else (z * HD, z * HD + HD)
                            for a, b in ((0, NS), (NS, T)):
                                last = pe.matmul(pair(q)[:, a:b], w2[lo:hi, s], lora[lo:hi, s, a:b], start=True, stop=True)
                            last.then_inc(sem("proj_ready"), 1)
                        pe.wait_ge(sem("proj_read"), 4).then_inc(sem("proj_read"), -4)
                        pe.wait_ge(sem("sq_ready"), 1).then_inc(sem("sq_ready"), -1)
                        for a, b in ((0, NS), (NS, T)):
                            last = pe.matmul(pair(0)[:, a:b], headones, sq[:, a:b], start=True, stop=True)
                        last.then_inc(sem("knorm_ready"), 1)
                        pe.wait_ge(sem("bonus_in"), 1).then_inc(sem("bonus_in"), -1)
                        for a, b in ((0, NS), (NS, T)):
                            last = pe.matmul(pair(1)[:, a:b], headones, shf[:, 0, a:b], start=True, stop=True)
                        last.then_inc(sem("bonus_sum"), 1)
                        pe.wait_ge(sem("knorm_read"), 1).then_inc(sem("knorm_read"), -1)
                        pe.wait_ge(sem("bonus_read"), 1).then_inc(sem("bonus_read"), -1)
                        pe.wait_ge(sem("feat_ready"), 2).then_inc(sem("feat_ready"), -2)
                        for tt in range(NT):
                            if tt >= 2:
                                pe.wait_ge(sem("tok_copied"), 1).then_inc(sem("tok_copied"), -1)
                            for z in range(2):
                                pe.transpose(ps[:, tt % 2, z * P:(z + 1) * P], nb[:, z, tt], ident)
                                last = pe.transpose(ps[:, tt % 2, (2 + z) * P:(3 + z) * P], kp[:, z, tt], ident)
                            last.then_inc(sem("tok_ready"), 1)
                        for tt in range(NT):
                            last = pe.transpose(pair(1)[:, tt * P:(tt + 1) * P], rkv[:, 2, tt * P:(tt + 1) * P], ident)
                        last.then_inc(sem("vtok_ready"), 1)
                        n = 0
                        for tt in range(NT):
                            for z in range(2):
                                for hh in range(2):
                                    lo, hi = hh * HD, hh * HD + HD
                                    if n >= 4:
                                        pe.wait_ge(sem("mat_read"), 1).then_inc(sem("mat_read"), -1)
                                    pe.matmul(ps[:, 4 + n % 4, 0:256], nb[lo:hi, z, tt], ar[lo:hi, z, tt], start=True, stop=True)
                                    pe.matmul(ps[:, 4 + n % 4, 256:512], kp[lo:hi, z, tt], ar[lo:hi, z, tt], start=True, stop=True)\
                                        .then_inc(sem("mat_ready"), 1)
                                    n += 1
                        pe.wait_ge(sem("mat_read"), 4).then_inc(sem("mat_read"), -4)
                        pe.wait_ge(sem("tok_copied"), 2).then_inc(sem("tok_copied"), -2)
                        pe.wait_ge(sem("vtok_copied"), 1).then_inc(sem("vtok_copied"), -1)
                        pe.wait_ge(sem("inv_start"), 1).then_inc(sem("inv_start"), -1)
                        for lev in range(LEVELS):
                            for g in range(NT):
                                pe.wait_ge(sem("invT_ready"), 1).then_inc(sem("invT_ready"), -1)
                                if g >= 2:
                                    pe.wait_ge(sem("inv_copied"), 1).then_inc(sem("inv_copied"), -1)
                                for u in range(4):
                                    last = pe.transpose(ps[:, g % 2, u * P:(u + 1) * P], invT[:, g, u], ident)
                                last.then_inc(sem("inv_ready"), 1)
                            for g in range(NT):
                                if g >= 2:
                                    pe.wait_ge(sem("yw_copied"), 1).then_inc(sem("yw_copied"), -1)
                                pe.wait_ge(sem("inv_copied_n"), 1).then_inc(sem("inv_copied_n"), -1)
                                for u in range(4):
                                    last = pe.matmul(ps[:, 2 + g % 2, u * P:(u + 1) * P], mat[:, g, u // 2, u % 2, 0], inv[:, g, u], start=True, stop=True)
                                last.then_inc(sem("yw_ready"), 1)
                            pe.wait_ge(sem("inv_copied"), 2).then_inc(sem("inv_copied"), -2)
                            for g in range(NT):
                                pe.wait_ge(sem("yw_copied_n"), 1).then_inc(sem("yw_copied_n"), -1)
                                if g >= 2:
                                    pe.wait_ge(sem("invT_read"), 1).then_inc(sem("invT_read"), -1)
                                for u in range(4):
                                    last = pe.matmul(ps[:, 4 + g % 2, u * P:(u + 1) * P], yw[:, g, u], invT[:, g, u], start=True, stop=True)
                                last.then_inc(sem("z_ready"), 1)
                            pe.wait_ge(sem("yw_copied"), 2).then_inc(sem("yw_copied"), -2)
                            pe.wait_ge(sem("invT_read"), 2).then_inc(sem("invT_read"), -2)
                        pe.wait_ge(sem("invT_ready"), NT).then_inc(sem("invT_ready"), -NT)
                        for j, cells in enumerate(steps):
                            pe.wait_ge(sem("s0_ready"), 1).then_inc(sem("s0_ready"), -1)
                            for q, (z, tt) in enumerate(cells):
                                for hh in range(2):
                                    lo, hi = hh * HD, hh * HD + HD
                                    o = ps[:, 6 - hh, q * HD:(q + 1) * HD]
                                    pe.matmul(o, ar[lo:hi, z, tt, 0], s0[lo:hi, z, tt], start=True, stop=False)
                                    last = pe.matmul(o, mat[:, tt, z, hh, 2], vtok[:, tt, lo:hi], start=False, stop=True)
                            last.then_inc(sem("r_ready"), 1)
                            pe.wait_ge(sem("r_copied"), 1).then_inc(sem("r_copied"), -1)
                            for q, (z, tt) in enumerate(cells):
                                for hh in range(2):
                                    lo, hi = hh * HD, hh * HD + HD
                                    last = pe.matmul(ps[:, 7, q * P + lo:q * P + hi], invT[:, tt, z * 2 + hh], rs[:, q, lo:hi], start=True, stop=True)
                            last.then_inc(sem("u_ready"), 1)
                            pe.wait_ge(sem("u_copied"), 1).then_inc(sem("u_copied"), -1)
                            for q, (z, tt) in enumerate(cells):
                                for hh in range(2):
                                    lo, hi = hh * HD, hh * HD + HD
                                    o = ps[lo:hi, 4, q * HD:(q + 1) * HD]
                                    pe.matmul(o, tokm[:, tt, 2 + z, lo:hi], vtok[:, tt, lo:hi], start=True, stop=False)
                                    last = pe.matmul(o, tokm[:, tt, z, lo:hi], us[:, z, tt, lo:hi], start=False, stop=True)
                            last.then_inc(sem("s_ready"), 1)
                        for tt in range(NT):
                            for hh in range(2):
                                lo, hi = hh * HD, hh * HD + HD
                                o = pair(0)[lo:hi, tt * P:(tt + 1) * P]
                                for z in range(2):
                                    pe.matmul(o, s0[lo:hi, z, tt], ar[lo:hi, z, tt, 1], start=z == 0, stop=False)
                                for z in range(2):
                                    pe.matmul(o, us[:, z, tt, lo:hi], mat[:, tt, z, hh, 1], start=False, stop=False)
                                    last = pe.matmul(o, vtok[:, tt, lo:hi], mat[:, tt, z, hh, 3], start=False, stop=z == 1)
                        last.then_inc(sem("y_ready"), 1)
                        for src, q, s in ((ysb, 1, "y_sbuf"), (ysq, 2, "ysq_ready")):
                            pe.wait_ge(sem(s), 1).then_inc(sem(s), -1)
                            for a, b in ((0, NS), (NS, T)):
                                last = pe.matmul(pair(q)[:, a:b], headones, src[:, a:b], start=True, stop=True)
                            last.then_inc(sem("ymean_ready" if q == 1 else "yvar_ready"), 1)
                        pe.wait_ge(sem("heads_done_pe"), 1).then_inc(sem("heads_done_pe"), -1)

                @block.scalar
                def _(act):
                    with act.Fori(0, HP) as i:
                        act.wait_ge(sem("hv_act"), 1).then_inc(sem("hv_act"), -1)
                        for s in range(3):
                            act.wait_ge(sem("proj_ready"), 1).then_inc(sem("proj_ready"), -1)
                            act.activation(raw[:, s], pair(s), ACT.Copy).then_inc(act_done, 1)
                            act.wait_ge(act_done, 1).then_inc(act_done, -1)
                            act.sem_inc(sem("raw_ready"), 1)
                            act.sem_inc(sem("proj_read"), 1)
                        for n, (q, out, b) in enumerate(((3, lw[:, 0], 12), (0, lw[:, 1], 13), (1, icl[:, 0], 14), (2, icl[:, 1], 15))):
                            act.wait_ge(sem("proj_ready"), 1).then_inc(sem("proj_ready"), -1)
                            act.activation(out, pair(q), ACT.Tanh, scale=0.5, bias=hv[:, b:b + 1]).then_inc(act_done, 1)
                            act.wait_ge(act_done, 1).then_inc(act_done, -1)
                            act.sem_inc(sem("proj_read"), 1)
                            act.sem_inc(sem("lw_ready" if n < 2 else "icl_ready"), 1)
                        act.wait_ge(sem("proj_ready"), 1).then_inc(sem("proj_ready"), -1)
                        act.activation(gate, pair(3), ACT.Copy).then_inc(act_done, 1)
                        act.wait_ge(act_done, 1).then_inc(act_done, -1)
                        act.sem_inc(sem("proj_read"), 1)
                        act.wait_ge(sem("k_ready"), 1).then_inc(sem("k_ready"), -1)
                        act.mul(kq, rkv[:, 1], hv[:, HPV["k_k"]:HPV["k_k"] + 1]).then_inc(act_done, 1)
                        act.activation(sq, rkv[:, 1], ACT.Square, scale=hv[:, HPV["k_k"]:HPV["k_k"] + 1]).then_inc(act_done, 1)
                        act.wait_ge(act_done, 2).then_inc(act_done, -2)
                        act.sem_inc(sem("sq_ready"), 1)
                        act.wait_ge(sem("knorm_ready"), 1).then_inc(sem("knorm_ready"), -1)
                        act.activation(kk, pair(0), ACT.Sqrt).then_inc(act_done, 1)
                        act.wait_ge(act_done, 1).then_inc(act_done, -1)
                        act.sem_inc(sem("knorm_read"), 1)
                        act.sem_inc(sem("knorm_root"), 1)
                        for z in range(2):
                            act.wait_ge(sem("rel_ready"), 1).then_inc(sem("rel_ready"), -1)
                            act.activation(eP[:, z], rel[:, z], ACT.Exp).then_inc(act_done, 1)
                            act.activation(eN[:, z], rel[:, z], ACT.Exp, scale=-1.0).then_inc(act_done, 1)
                            act.wait_ge(act_done, 2).then_inc(act_done, -2)
                            act.sem_inc(sem("exp_ready"), 1)
                        for tt in range(NT):
                            act.wait_ge(sem("tok_ready"), 1).then_inc(sem("tok_ready"), -1)
                            act.activation(tokm[:, tt].rearrange("p u n -> p (u n)"), ps[:, tt % 2], ACT.Copy).then_inc(act_done, 1)
                            act.wait_ge(act_done, 1).then_inc(act_done, -1)
                            act.sem_inc(sem("tok_copied"), 1)
                        act.wait_ge(sem("vtok_ready"), 1).then_inc(sem("vtok_ready"), -1)
                        act.activation(vtok.rearrange("p t n -> p (t n)"), pair(1), ACT.Copy).then_inc(act_done, 1)
                        act.wait_ge(act_done, 1).then_inc(act_done, -1)
                        act.sem_inc(sem("vtok_copied"), 1)
                        for lev in range(LEVELS):
                            for g in range(NT):
                                act.wait_ge(sem("inv_ready"), 1).then_inc(sem("inv_ready"), -1)
                                act.activation(inv[:, g].rearrange("p u n -> p (u n)"), ps[:, g % 2], ACT.Copy).then_inc(act_done, 1)
                                act.wait_ge(act_done, 1).then_inc(act_done, -1)
                                act.sem_inc(sem("inv_copied"), 1)
                                act.sem_inc(sem("inv_copied_n"), 1)
                            for g in range(NT):
                                act.wait_ge(sem("yw_ready"), 1).then_inc(sem("yw_ready"), -1)
                                act.activation(yw[:, g].rearrange("p u n -> p (u n)"), ps[:, 2 + g % 2], ACT.Copy).then_inc(act_done, 1)
                                act.wait_ge(act_done, 1).then_inc(act_done, -1)
                                act.sem_inc(sem("yw_copied"), 1)
                                act.sem_inc(sem("yw_copied_n"), 1)
                        for j, cells in enumerate(steps):
                            act.wait_ge(sem("r_ready"), 1).then_inc(sem("r_ready"), -1)
                            n = len(cells)
                            for hh in range(2):
                                act.activation(rs[:, 0:n, hh * HD:(hh + 1) * HD], ps[:, 6 - hh, 0:n * HD].rearrange("p (u n) -> p u n", u=n), ACT.Copy).then_inc(act_done, 1)
                            act.wait_ge(act_done, 2).then_inc(act_done, -2)
                            act.sem_inc(sem("r_copied"), 1)
                            act.wait_ge(sem("u_ready"), 1).then_inc(sem("u_ready"), -1)
                            for q, (z, tt) in enumerate(cells):
                                act.activation(us[:, z, tt], ps[:, 7, q * P:(q + 1) * P], ACT.Copy).then_inc(act_done, 1)
                            act.wait_ge(act_done, len(cells)).then_inc(act_done, -(len(cells)))
                            act.sem_inc(sem("u_copied"), 1)
                        act.wait_ge(sem("y_ready"), 1).then_inc(sem("y_ready"), -1)
                        act.activation(ysb, pair(0), ACT.Copy).then_inc(act_done, 1)
                        act.wait_ge(act_done, 1).then_inc(act_done, -1)
                        act.sem_inc(sem("y_sbuf"), 1)
                        act.sem_inc(sem("y_sbuf_v"), 1)
                        act.wait_ge(sem("yc_ready"), 1).then_inc(sem("yc_ready"), -1)
                        act.activation(ysq, yc, ACT.Square).then_inc(act_done, 1)
                        act.wait_ge(act_done, 1).then_inc(act_done, -1)
                        act.sem_inc(sem("ysq_ready"), 1)
                        act.wait_ge(sem("yvar_ready"), 1).then_inc(sem("yvar_ready"), -1)
                        act.activation(root, pair(2), ACT.Sqrt, scale=1.0 / HD, bias=eps[:, 2:3]).then_inc(act_done, 1)
                        act.wait_ge(act_done, 1).then_inc(act_done, -1)
                        act.sem_inc(sem("yroot_ready"), 1)
                        act.wait_ge(sem("heads_done_act"), 1).then_inc(sem("heads_done_act"), -1)

                @block.gpsimd
                def _(pool):
                    with pool.Fori(0, HP) as i:
                        for s in range(3):
                            pool.wait_ge(sem("raw_ready"), 1).then_inc(sem("raw_ready"), -1)
                            pool.tensor_tensor(shf[:, s, 1:T - 1], raw[:, s, 0:T - 2], raw[:, s, 2:T], ALU.add).then_inc(pool_done, 1)
                            pool.wait_ge(pool_done, 1).then_inc(pool_done, -1)
                            pool.tensor_copy(shf[:, s, 0:NS + 1:NS], raw[:, s, 1:NS + 2:NS]).then_inc(pool_done, 1)
                            pool.tensor_copy(shf[:, s, NS - 1:T:NP], raw[:, s, NS - 2:T - 1:NP]).then_inc(pool_done, 1)
                            pool.wait_ge(pool_done, 2).then_inc(pool_done, -2)
                            pool.sem_inc(sem("shf_ready"), 1)
                        pool.wait_ge(sem("heads_done_pool"), 1).then_inc(sem("heads_done_pool"), -1)

                @block.vector
                def _(dve):
                    with dve.Fori(0, HP) as i:
                        dve.wait_ge(sem("hpv_in"), 16).then_inc(sem("hpv_in"), -16)
                        dve.tensor_copy(hv[:, 0:NHPV], hpv).then_inc(dve_done, 1)
                        dve.tensor_scalar(hv[:, 12:16], hpv[:, 3:7], 0.5, None, ALU.mult).then_inc(dve_done, 1)
                        dve.tensor_scalar(hv[:, 16:17], hpv[:, 8:9], -1.0, 1.0, ALU.mult, ALU.add).then_inc(dve_done, 1)
                        dve.wait_ge(dve_done, 3).then_inc(dve_done, -3)
                        dve.sem_inc(sem("hv_act"), 1)

                        def col(name, k=0):
                            n = HPV[name] + k
                            return hv[:, n:n + 1]

                        for s in range(3):
                            dve.wait_ge(sem("shf_ready"), 1).then_inc(sem("shf_ready"), -1)
                            dve.scalar_tensor_tensor(shf[:, s], shf[:, s], 0.5, raw[:, s], ALU.mult, ALU.subtract).then_inc(dve_done, 1)
                            dve.wait_ge(dve_done, 1).then_inc(dve_done, -1)
                            dve.scalar_tensor_tensor(rkv[:, s], shf[:, s], col("mu", s), raw[:, s], ALU.mult, ALU.add).then_inc(dve_done, 1)
                            dve.wait_ge(dve_done, 1).then_inc(dve_done, -1)
                            if s == 1:
                                dve.sem_inc(sem("k_ready"), 1)
                                dve.scalar_tensor_tensor(shf[:, 0], rkv[:, 0], col("r_k"), rkv[:, 1], ALU.mult, ALU.mult).then_inc(dve_done, 1)
                                dve.wait_ge(dve_done, 1).then_inc(dve_done, -1)
                                dve.sem_inc(sem("bonus_in"), 1)
                        for z in range(2):
                            dve.wait_ge(sem("lw_ready"), 1).then_inc(sem("lw_ready"), -1)
                            dve.tensor_scalar(lw[:, z], lw[:, z], -EXPH / 2, -EXPH / 2, ALU.mult, ALU.add).then_inc(dve_done, 1)
                            dve.wait_ge(dve_done, 1).then_inc(dve_done, -1)
                            for tt in range(NT):
                                dve.tensor_tensor_scan(cum[:, tt], ones[:, :], lw[:, z, tt * P:(tt + 1) * P], 0.0, ALU.mult, ALU.add).then_inc(dve_done, 1)
                            dve.wait_ge(dve_done, 5).then_inc(dve_done, -5)
                            dve.tensor_scalar(ctr, cum[:, :, P - 1], 0.5, None, ALU.mult).then_inc(dve_done, 1)
                            dve.wait_ge(dve_done, 1).then_inc(dve_done, -1)
                            dve.tensor_tensor(rel[:, z, :, 1:P + 1], cum, bcast(ctr, 2, P), ALU.subtract).then_inc(dve_done, 1)
                            dve.tensor_scalar(rel[:, z, :, 0], ctr, -1.0, None, ALU.mult).then_inc(dve_done, 1)
                            dve.wait_ge(dve_done, 2).then_inc(dve_done, -2)
                            dve.sem_inc(sem("rel_ready"), 1)
                        dve.wait_ge(sem("knorm_root"), 1).then_inc(sem("knorm_root"), -1)
                        dve.tensor_scalar(kk, kk, 1e-12, None, ALU.max).then_inc(dve_done, 1)
                        dve.wait_ge(dve_done, 1).then_inc(dve_done, -1)
                        dve.reciprocal(kk, kk).then_inc(dve_done, 1)
                        dve.wait_ge(dve_done, 1).then_inc(dve_done, -1)
                        dve.tensor_tensor(kk, kk, kq, ALU.mult).then_inc(dve_done, 1)
                        dve.wait_ge(dve_done, 1).then_inc(dve_done, -1)
                        dve.wait_ge(sem("bonus_sum"), 1).then_inc(sem("bonus_sum"), -1)
                        dve.tensor_tensor(bon, pair(1), rkv[:, 2], ALU.mult).then_inc(dve_done, 1)
                        dve.wait_ge(dve_done, 1).then_inc(dve_done, -1)
                        dve.sem_inc(sem("bonus_read"), 1)
                        kk3 = kk.rearrange("p (t n) -> p t n", t=NT)
                        r3 = rkv[:, 0].rearrange("p (t n) -> p t n", t=NT)
                        for z in range(2):
                            dve.wait_ge(sem("icl_ready"), 1).then_inc(sem("icl_ready"), -1)
                            dve.tensor_scalar(icl[:, z], icl[:, z], 0.5, 0.5, ALU.mult, ALU.add).then_inc(dve_done, 1)
                            dve.wait_ge(dve_done, 1).then_inc(dve_done, -1)
                            dve.tensor_scalar(lw[:, z], icl[:, z], col("k_a"), hv[:, 16:17], ALU.mult, ALU.add).then_inc(dve_done, 1)
                            dve.wait_ge(dve_done, 1).then_inc(dve_done, -1)
                            dve.tensor_tensor(lw[:, z], lw[:, z], rkv[:, 1], ALU.mult).then_inc(dve_done, 1)
                            dve.scalar_tensor_tensor(icl[:, z], icl[:, z], -1.0, kk, ALU.mult, ALU.mult).then_inc(dve_done, 1)
                            dve.wait_ge(dve_done, 2).then_inc(dve_done, -2)
                            k3 = lw[:, z].rearrange("p (t n) -> p t n", t=NT)
                            b3 = icl[:, z].rearrange("p (t n) -> p t n", t=NT)
                            dve.wait_ge(sem("exp_ready"), 1).then_inc(sem("exp_ready"), -1)
                            inc, exc = slice(1, P + 1), slice(0, P)
                            if z == 0:
                                fr, fa, fb = eP[:, z, :, inc], eP[:, z, :, exc], eN[:, z, :, inc]
                            else:
                                fr, fa, fb = eN[:, z, :, exc], eN[:, z, :, inc], eP[:, z, :, exc]
                            dve.tensor_tensor(ar[:, z, :, 0], kk3, fa, ALU.mult).then_inc(dve_done, 1)
                            dve.tensor_tensor(ar[:, z, :, 1], r3, fr, ALU.mult).then_inc(dve_done, 1)
                            dve.tensor_tensor(nb[:, z], b3, fb, ALU.mult).then_inc(dve_done, 1)
                            dve.tensor_tensor(kp[:, z], k3, fb, ALU.mult).then_inc(dve_done, 1)
                            dve.tensor_copy(ec[:, z], eN[:, z, :, 0]).then_inc(dve_done, 1)
                            dve.wait_ge(dve_done, 5).then_inc(dve_done, -5)
                            dve.sem_inc(sem("feat_ready"), 1)
                        n = 0
                        for tt in range(NT):
                            for z in range(2):
                                for hh in range(2):
                                    dve.wait_ge(sem("mat_ready"), 1).then_inc(sem("mat_ready"), -1)
                                    dve.tensor_tensor(mat[:, tt, z, hh].rearrange("p k n -> p (k n)"), ps[:, 4 + n % 4], tri[:, z], ALU.mult).then_inc(dve_done, 1)
                                    dve.wait_ge(dve_done, 1).then_inc(dve_done, -1)
                                    dve.sem_inc(sem("mat_read"), 1)
                                    n += 1
                        dve.tensor_copy(invT, bcast(bcast(ident, 1, 4), 1, NT)).then_inc(dve_done, 1)
                        dve.wait_ge(dve_done, 1).then_inc(dve_done, -1)
                        for g in range(NT):
                            for z in range(2):
                                dve.copy_predicated(invT[:, g, 2 * z:2 * z + 2], bcast(lv[:, 0, z], 1, 2), mat[:, g, z, :, 0]).then_inc(dve_done, 1)
                        dve.wait_ge(dve_done, 10).then_inc(dve_done, -10)
                        dve.sem_inc(sem("inv_start"), 1)
                        dve.sem_inc(sem("invT_ready"), NT)
                        dve.wait_ge(sem("state_in"), 16).then_inc(sem("state_in"), -16)
                        dve.tensor_scalar(s0[:, 0, 0], stin[:, 0], ec[:, 0, 0:1], None, ALU.mult).then_inc(dve_done, 1)
                        dve.tensor_scalar(s0[:, 1, ST - 1], stin[:, 1], ec[:, 1, ST - 1:ST], None, ALU.mult).then_inc(dve_done, 1)
                        dve.memset(s0[:, :, ST], 0.0).then_inc(dve_done, 1)
                        dve.wait_ge(dve_done, 3).then_inc(dve_done, -3)
                        dve.sem_inc(sem("s0_ready"), 1)
                        for lev in range(LEVELS):
                            for g in range(NT):
                                dve.wait_ge(sem("z_ready"), 1).then_inc(sem("z_ready"), -1)
                                for z in range(2):
                                    dve.copy_predicated(invT[:, g, 2 * z:2 * z + 2], bcast(lv[:, 1 + lev, z], 1, 2),
                                                           ps[:, 4 + g % 2, 2 * z * P:(2 * z + 2) * P].rearrange("p (u n) -> p u n", u=2)).then_inc(dve_done, 1)
                                dve.wait_ge(dve_done, 2).then_inc(dve_done, -2)
                                dve.sem_inc(sem("invT_read"), 1)
                                dve.sem_inc(sem("invT_ready"), 1)
                        for j, cells in enumerate(steps):
                            dve.wait_ge(sem("s_ready"), 1).then_inc(sem("s_ready"), -1)
                            for q, (z, tt) in enumerate(cells):
                                dve.tensor_tensor(stmp[:, q], ps[:, 4, q * HD:(q + 1) * HD], s0[:, z, tt], ALU.add).then_inc(dve_done, 1)
                            dve.wait_ge(dve_done, len(cells)).then_inc(dve_done, -(len(cells)))
                            for q, (z, tt) in enumerate(cells):
                                if tt == ST:
                                    dve.tensor_scalar(sout[:, z], stmp[:, q], ec[:, z, tt:tt + 1], None, ALU.mult).then_inc(dve_done, 1)
                                elif j < ST - 1:
                                    nx = tt + 1 - 2 * z
                                    dve.tensor_scalar(s0[:, z, nx], stmp[:, q], ec[:, z, tt:tt + 1], ec[:, z, nx:nx + 1], ALU.mult, ALU.mult).then_inc(dve_done, 1)
                            if j < ST - 1:
                                dve.wait_ge(dve_done, len(cells)).then_inc(dve_done, -(len(cells)))
                                dve.sem_inc(sem("s0_ready"), 1)
                            if j == 0:
                                dve.sem_inc(sem("sout_ready"), 1)
                        dve.wait_ge(sem("y_sbuf_v"), 1).then_inc(sem("y_sbuf_v"), -1)
                        dve.wait_ge(sem("ymean_ready"), 1).then_inc(sem("ymean_ready"), -1)
                        dve.scalar_tensor_tensor(yc, pair(1), -1.0 / HD, ysb, ALU.mult, ALU.add).then_inc(dve_done, 1)
                        dve.wait_ge(dve_done, 1).then_inc(dve_done, -1)
                        dve.sem_inc(sem("yc_ready"), 1)
                        dve.wait_ge(sem("yroot_ready"), 1).then_inc(sem("yroot_ready"), -1)
                        dve.reciprocal(root, root).then_inc(dve_done, 1)
                        dve.wait_ge(dve_done, 1).then_inc(dve_done, -1)
                        dve.tensor_tensor(yc, yc, root, ALU.mult).then_inc(dve_done, 1)
                        dve.wait_ge(dve_done, 1).then_inc(dve_done, -1)
                        dve.tensor_scalar(yc, yc, col("gn_w"), col("gn_b"), ALU.mult, ALU.add).then_inc(dve_done, 1)
                        dve.wait_ge(dve_done, 1).then_inc(dve_done, -1)
                        dve.tensor_tensor(yc, yc, bon, ALU.add).then_inc(dve_done, 1)
                        dve.wait_ge(dve_done, 1).then_inc(dve_done, -1)
                        dve.tensor_tensor(mix[:, bass.ds(i, 1)].rearrange("p a n -> p (a n)"), yc, gate, ALU.mult).then_inc(dve_done, 1)
                        dve.wait_ge(dve_done, 1).then_inc(dve_done, -1)
                        for name in ("heads_done_sp", "heads_done_pe", "heads_done_act", "heads_done_pool"):
                            dve.sem_inc(sem(name), 1)

        def out_proj(l, w):
            w_sb = Carve()(2, 4, 1024)

            with stage() as block:
                @block.sync
                def _(sp):
                    for k in range(2):
                        sp.dma_start(w_sb[:, k], half_rows(w, k)).then_inc(sem(f"wout{k}"), 16)

                @block.tensor
                def _(pe):
                    for k in range(2):
                        pe.wait_ge(sem(f"wout{k}"), 16).then_inc(sem(f"wout{k}"), -16)
                    for m in range(KC):
                        if m >= 4:
                            pe.wait_ge(sem("out_read"), 1).then_inc(sem("out_read"), -1)
                        for a, b in ((0, NS), (NS, T)):
                            for c in range(KC):
                                last = pe.matmul(pair(m % 4)[:, a:b], w_sb[:, c // 4, c % 4, m * P:(m + 1) * P], mix[:, c, a:b],
                                                start=c == 0, stop=c == KC - 1)
                        last.then_inc(sem("out_ready"), 1)
                    pe.wait_ge(sem("out_read"), 4).then_inc(sem("out_read"), -4)

                @block.vector
                def _(dve):
                    for m in range(KC):
                        dve.wait_ge(sem("out_ready"), 1).then_inc(sem("out_ready"), -1)
                        for r, a, b in SEGS:
                            dve.scalar_tensor_tensor(x[:, m, a:b], pair(m % 4)[:, a:b], mod[:, l, 2, m, r:r + 1], x[:, m, a:b], ALU.mult, ALU.add).then_inc(dve_done, 1)
                        dve.wait_ge(dve_done, 2).then_inc(dve_done, -2)
                        dve.sem_inc(sem("out_read"), 1)

        def route(l, prefetch):
            htok = mix[:, :, :].rearrange("p c n -> p (c n)").rearrange("p (t d) -> p t d", t=NT)
            cv = Carve(24576)
            wr = cv(KC, E)
            br = cv(E, parts=1)
            lg = cv(NT, E)
            mx = cv(NT)
            work = cv(T, parts=E)
            pos = cv(T, parts=E)
            m8v = cv(8, parts=E)
            one16 = cv(T, parts=E)
            sl = cv(T, parts=E)

            with stage() as block:
                @block.sync
                def _(sp):
                    sp.dma_start(wr, t["router"][l].rearrange("(c p) n -> p c n", p=P)).then_inc(sem("wr_in"), 16)
                    sp.dma_start(br, t["router_b"][l:l + 1, :]).then_inc(sem("wr_in"), 16)
                    prefetch(sp)

                @block.tensor
                def _(pe):
                    pe.wait_ge(sem("wr_in"), 32).then_inc(sem("wr_in"), -32)
                    for tt in range(NT):
                        o = ps[:, 0, tt * E:(tt + 1) * E]
                        for c in range(KC):
                            pe.matmul(o, h[:, c, tt * P:(tt + 1) * P], wr[:, c], start=c == 0, stop=False)
                        last = pe.matmul(o, ones[0:1, :], br, start=False, stop=True)
                    last.then_inc(sem("logits_ready"), 1)
                    for n in range(10):
                        b = 2 + n % 4
                        if n >= 4:
                            pe.wait_ge(sem("htok_read"), 1).then_inc(sem("htok_read"), -1)
                        for k in range(4):
                            tt, c = n // 2, 4 * (n % 2) + k
                            last = pe.transpose(ps[:, b, k * P:(k + 1) * P], h[:, c, tt * P:(tt + 1) * P], ident)
                        last.then_inc(sem("htok_ready"), 1)
                    pe.wait_ge(sem("htok_read"), 4).then_inc(sem("htok_read"), -4)
                    pe.wait_ge(sem("aff_ready"), 1).then_inc(sem("aff_ready"), -1)
                    for tt in range(NT):
                        last = pe.transpose(pair(0)[0:E, tt * P:(tt + 1) * P], aff[:, tt], ident)
                    last.then_inc(sem("affT_ready"), 1)
                    pe.wait_ge(sem("slots_ready"), 1).then_inc(sem("slots_ready"), -1)
                    for tt in range(NT):
                        last = pe.transpose(ps[:, 2, tt * E:(tt + 1) * E], sl[:, tt * P:(tt + 1) * P], ident[0:E, 0:E])
                    last.then_inc(sem("slotsT_ready"), 1)

                @block.scalar
                def _(act):
                    for n in range(10):
                        act.wait_ge(sem("htok_ready"), 1).then_inc(sem("htok_ready"), -1)
                        act.activation(htok[:, n // 2, 512 * (n % 2):512 * (n % 2) + 512], ps[:, 2 + n % 4], ACT.Copy).then_inc(act_done, 1)
                        act.wait_ge(act_done, 1).then_inc(act_done, -1)
                        act.sem_inc(sem("htok_read"), 1)
                        if n == 1:
                            act.wait_ge(sem("lg_ready"), 1).then_inc(sem("lg_ready"), -1)
                            act.activation(aff[:, :, :], lg, ACT.Exp).then_inc(act_done, 1)
                            act.wait_ge(act_done, 1).then_inc(act_done, -1)
                            act.sem_inc(sem("exp_done"), 1)

                @block.vector
                def _(dve):
                    dve.wait_ge(sem("logits_ready"), 1).then_inc(sem("logits_ready"), -1)
                    lp = ps[:, 0, 0:NT * E].rearrange("p (t e) -> p t e", t=NT)
                    dve.tensor_reduce(mx, lp, AX.X, ALU.max).then_inc(dve_done, 1)
                    dve.wait_ge(dve_done, 1).then_inc(dve_done, -1)
                    dve.tensor_tensor(lg, lp, bcast(mx, 2, E), ALU.subtract).then_inc(dve_done, 1)
                    dve.wait_ge(dve_done, 1).then_inc(dve_done, -1)
                    dve.sem_inc(sem("lg_ready"), 1)
                    dve.wait_ge(sem("exp_done"), 1).then_inc(sem("exp_done"), -1)
                    dve.tensor_reduce(mx, aff[:, :, :], AX.X, ALU.add).then_inc(dve_done, 1)
                    dve.wait_ge(dve_done, 1).then_inc(dve_done, -1)
                    dve.reciprocal(mx, mx).then_inc(dve_done, 1)
                    dve.wait_ge(dve_done, 1).then_inc(dve_done, -1)
                    dve.tensor_tensor(aff[:, :, :], aff[:, :, :], bcast(mx, 2, E), ALU.mult).then_inc(dve_done, 1)
                    dve.wait_ge(dve_done, 1).then_inc(dve_done, -1)
                    dve.sem_inc(sem("aff_ready"), 1)
                    dve.memset(one16, 1.0).then_inc(dve_done, 1)
                    dve.wait_ge(dve_done, 1).then_inc(dve_done, -1)
                    dve.wait_ge(sem("affT_ready"), 1).then_inc(sem("affT_ready"), -1)
                    dve.tensor_copy(work, pair(0)[0:E, :]).then_inc(dve_done, 1)
                    dve.wait_ge(dve_done, 1).then_inc(dve_done, -1)
                    for a, b, cap in ((0, NS, CAPS), (NS, T, CAPP)):
                        for n in range(cap // 8):
                            dve.max(m8v, work[:, a:b]).then_inc(dve_done, 1)
                            dve.wait_ge(dve_done, 1).then_inc(dve_done, -1)
                            dve.match_replace(work[:, a:b], m8v, work[:, a:b], -1.0).then_inc(dve_done, 1)
                            dve.wait_ge(dve_done, 1).then_inc(dve_done, -1)
                    dve.tensor_scalar(work, work, 0.0, None, ALU.is_lt).then_inc(dve_done, 1)
                    dve.wait_ge(dve_done, 1).then_inc(dve_done, -1)
                    for a, b in ((0, NS), (NS, T)):
                        dve.tensor_tensor_scan(pos[:, a:b], one16[:, a:b], work[:, a:b], 0.0, ALU.mult, ALU.add).then_inc(dve_done, 1)
                    dve.wait_ge(dve_done, 2).then_inc(dve_done, -2)
                    dve.tensor_tensor(pos, pos, work, ALU.mult).then_inc(dve_done, 1)
                    dve.wait_ge(dve_done, 1).then_inc(dve_done, -1)
                    dve.tensor_scalar(sl, pos, -1.0, None, ALU.add).then_inc(dve_done, 1)
                    dve.wait_ge(dve_done, 1).then_inc(dve_done, -1)
                    dve.sem_inc(sem("slots_ready"), 1)
                    dve.wait_ge(sem("slotsT_ready"), 1).then_inc(sem("slotsT_ready"), -1)
                    dve.tensor_copy(slot[:, :, :], ps[:, 2, 0:NT * E].rearrange("p (t e) -> p t e", t=NT)).then_inc(dve_done, 1)
                    dve.wait_ge(dve_done, 1).then_inc(dve_done, -1)

        def expert_slabs(l):
            out = []
            for name in ("moe_w_gate", "moe_w_up", "moe_w_down"):
                w = t[name][l].rearrange("(q e) (k c p) n -> q e k p c n", e=2, k=2, p=P)
                out.append(w)
            order = [(0, 0), (1, 0), (0, 1), (1, 1), (2, 0), (2, 1)]
            return [(out[m], ee, k) for m, ee in order for k in range(2)]

        def load_slab(sp, l, i, n):
            w, ee, k = expert_slabs(l)[n]
            src = w[i, ee, k] if isinstance(i, int) else w[bass.ds(i, 1), ee, k].rearrange("a p c n -> p (a c) n")
            sp.dma_start(ring[:, n % 6], src).then_inc(sem(f"slab{n % 6}"), 16)

        def experts(l):
            htok = mix[:, :, :].rearrange("p c n -> p (c n)").rearrange("p (t d) -> p t d", t=NT)
            cv = Carve(24576)
            oh = cv(ST, 2, CAPS)
            ohw = cv(ST, 2, CAPS)
            ohp = cv(2, CAPP)
            ohpw = cv(2, CAPP)
            slp = cv(NT, 2)
            afp = cv(NT, 2)
            gs = cv(NS)
            gp = cv(NP, parts=2 * CAPP)
            xs = cv(KC, 2, CAP)
            hid = cv(2, KC, CAP)
            th = cv(4, CAP)
            yT = xs.rearrange("p c e s -> p c (e s)")
            ysn = hid.rearrange("p e c s -> p (e c s)")[:, 0:D]
            ypn = cv(D, parts=2 * CAPP)
            iota = C("iota")

            with stage() as block:
                @block.sync
                def _(sp):
                    with sp.Fori(0, E // 2 - 1) as i:
                        for n in range(6, 12):
                            sp.wait_ge(sem("slab_free"), 1).then_inc(sem("slab_free"), -1)
                            load_slab(sp, l, i, n)
                        for n in range(6):
                            sp.wait_ge(sem("slab_free"), 1).then_inc(sem("slab_free"), -1)
                            load_slab(sp, l, i + 1, n)
                    for n in range(6, 12):
                        sp.wait_ge(sem("slab_free"), 1).then_inc(sem("slab_free"), -1)
                        load_slab(sp, l, E // 2 - 1, n)
                    sp.wait_ge(sem("slab_free"), 6).then_inc(sem("slab_free"), -6)

                @block.vector
                def _(dve):
                    with dve.Fori(0, E // 2) as i:
                        dve.tensor_scalar(slp, slot[:, :, :].rearrange("p t (q e) -> p q t e", e=2)[:, bass.ds(i, 1)].rearrange("p a t e -> p (a t) e"), 0.0, None, ALU.add).then_inc(dve_done, 1)
                        dve.tensor_scalar(afp, aff[:, :, :].rearrange("p t (q e) -> p q t e", e=2)[:, bass.ds(i, 1)].rearrange("p a t e -> p (a t) e"), 0.0, None, ALU.add).then_inc(dve_done, 1)
                        dve.wait_ge(dve_done, 2).then_inc(dve_done, -2)
                        io = bcast(bcast(iota, 1, 2), 1, ST)
                        dve.tensor_tensor(oh, io, bcast(slp[:, 0:ST], 3, CAPS), ALU.is_equal).then_inc(dve_done, 1)
                        dve.tensor_tensor(ohp, bcast(iota[:, 0:CAPP], 1, 2), bcast(slp[:, ST], 2, CAPP), ALU.is_equal).then_inc(dve_done, 1)
                        dve.wait_ge(dve_done, 2).then_inc(dve_done, -2)
                        dve.sem_inc(sem("onehot_ready"), 1)
                        dve.tensor_tensor(ohw, oh, bcast(afp[:, 0:ST], 3, CAPS), ALU.mult).then_inc(dve_done, 1)
                        dve.tensor_tensor(ohpw, ohp, bcast(afp[:, ST], 2, CAPP), ALU.mult).then_inc(dve_done, 1)
                        dve.wait_ge(dve_done, 2).then_inc(dve_done, -2)
                        dve.sem_inc(sem("onehotw_ready"), 1)
                        for n in range(3):
                            dve.wait_ge(sem("xs_ready"), 1).then_inc(sem("xs_ready"), -1)
                            w = 3 if n < 2 else 2
                            dve.tensor_copy(xs[:, 3 * n:3 * n + w].rearrange("p c e s -> p (c e s)"), ps[:, n, 0:w * 2 * CAP]).then_inc(dve_done, 1)
                            dve.wait_ge(dve_done, 1).then_inc(dve_done, -1)
                            dve.sem_inc(sem("xs_copied"), 1)
                        for ee in range(2):
                            for f in range(2):
                                dve.wait_ge(sem("silu_ready"), 1).then_inc(sem("silu_ready"), -1)
                                g4 = ps[:, 2 * f, 0:4 * CAP].rearrange("p (c s) -> p c s", c=4)
                                u4 = ps[:, 2 * f + 1, 0:4 * CAP].rearrange("p (c s) -> p c s", c=4)
                                dve.scalar_tensor_tensor(th, th, 1.0, g4, ALU.add, ALU.mult).then_inc(dve_done, 1)
                                dve.wait_ge(dve_done, 1).then_inc(dve_done, -1)
                                dve.wait_ge(sem("up_ready"), 1).then_inc(sem("up_ready"), -1)
                                dve.scalar_tensor_tensor(hid[:, ee, 4 * f:4 * f + 4], th, 0.5, u4, ALU.mult, ALU.mult).then_inc(dve_done, 1)
                                dve.wait_ge(dve_done, 1).then_inc(dve_done, -1)
                                dve.sem_inc(sem("hid_ready"), 1)
                                dve.sem_inc(sem("gu_read"), 1)
                                dve.sem_inc(sem("th_free"), 1)
                        dve.wait_ge(sem("yp_ready"), 1).then_inc(sem("yp_ready"), -1)
                        for m in range(KC):
                            dve.scalar_tensor_tensor(x[:, m, NS:T], ps[:, 4 + m // 4, (m % 4) * NP:(m % 4 + 1) * NP], mod[:, l, 5, m, 1:2],
                                                        x[:, m, NS:T], ALU.mult, ALU.add).then_inc(dve_done, 1)
                        dve.wait_ge(dve_done, 8).then_inc(dve_done, -8)
                        dve.sem_inc(sem("yp_read"), 1)
                        for m in range(KC):
                            dve.wait_ge(sem("y_ready"), 1).then_inc(sem("y_ready"), -1)
                            o = ps[:, 6 + m % 2]
                            dve.scalar_tensor_tensor(x[:, m, 0:NS], o, mod[:, l, 5, m, 0:1], x[:, m, 0:NS], ALU.mult, ALU.add).then_inc(dve_done, 1)
                            dve.wait_ge(dve_done, 1).then_inc(dve_done, -1)
                            dve.sem_inc(sem("y_read"), 1)

                @block.scalar
                def _(act):
                    with act.Fori(0, E // 2) as i:
                        act.wait_ge(sem("gT_ready"), 1).then_inc(sem("gT_ready"), -1)
                        act.activation(gs, ps[:, 6], ACT.Copy).then_inc(act_done, 1)
                        act.activation(gp, ps[0:2 * CAPP, 7, 0:NP], ACT.Copy).then_inc(act_done, 1)
                        act.wait_ge(act_done, 2).then_inc(act_done, -2)
                        act.sem_inc(sem("gT_copied"), 1)
                        for ee in range(2):
                            for f in range(2):
                                act.wait_ge(sem("gate_ready"), 1).then_inc(sem("gate_ready"), -1)
                                act.activation(th, ps[:, 2 * f, 0:4 * CAP].rearrange("p (c s) -> p c s", c=4), ACT.Tanh, scale=0.5).then_inc(act_done, 1)
                                act.wait_ge(act_done, 1).then_inc(act_done, -1)
                                act.sem_inc(sem("silu_ready"), 1)
                                act.wait_ge(sem("th_free"), 1).then_inc(sem("th_free"), -1)
                        for ee in range(2):
                            for f in range(2):
                                act.wait_ge(sem("down_ready"), 1).then_inc(sem("down_ready"), -1)
                                d4 = ps[:, 4 + f, 0:4 * CAP].rearrange("p (c s) -> p c s", c=4)
                                act.activation(yT[:, 4 * f:4 * f + 4, ee * CAPS:(ee + 1) * CAPS], d4[:, :, 0:CAPS], ACT.Copy).then_inc(act_done, 1)
                                act.activation(yT[:, 4 * f:4 * f + 4, 2 * CAPS + ee * CAPP:2 * CAPS + (ee + 1) * CAPP], d4[:, :, CAPS:CAP], ACT.Copy).then_inc(act_done, 1)
                                act.wait_ge(act_done, 2).then_inc(act_done, -2)
                                act.sem_inc(sem("down_copied"), 1)
                        act.wait_ge(sem("yslots_ready"), 1).then_inc(sem("yslots_ready"), -1)
                        for k in range(2):
                            act.activation(ysn[:, k * 512:(k + 1) * 512], ps[:, k], ACT.Copy).then_inc(act_done, 1)
                            act.activation(ypn[:, k * 512:(k + 1) * 512], ps[0:2 * CAPP, 2 + k], ACT.Copy).then_inc(act_done, 1)
                        act.wait_ge(act_done, 4).then_inc(act_done, -4)
                        act.sem_inc(sem("yslots_copied"), 1)

                @block.tensor
                def _(pe):
                    with pe.Fori(0, E // 2) as i:
                        pe.wait_ge(sem("onehot_ready"), 1).then_inc(sem("onehot_ready"), -1)
                        for c in range(KC):
                            o = ps[:, c // 3, (c % 3) * 2 * CAP:(c % 3 + 1) * 2 * CAP].rearrange("p (e s) -> p e s", e=2)
                            for tt in range(ST):
                                pe.matmul(o[:, :, 0:CAPS], htok[:, tt, c * P:(c + 1) * P], oh[:, tt], start=tt == 0, stop=tt == ST - 1)
                            last = pe.matmul(o[:, :, CAPS:CAP], htok[:, ST, c * P:(c + 1) * P], ohp, start=True, stop=True)
                            if c % 3 == 2 or c == KC - 1:
                                last.then_inc(sem("xs_ready"), 1)
                        pe.wait_ge(sem("onehotw_ready"), 1).then_inc(sem("onehotw_ready"), -1)
                        for tt in range(ST):
                            pe.transpose(ps[:, 6, tt * P:(tt + 1) * P], ohw[:, tt].rearrange("p e s -> p (e s)"), ident)
                        pe.transpose(ps[0:2 * CAPP, 7, 0:NP], ohpw.rearrange("p e s -> p (e s)"), ident).then_inc(sem("gT_ready"), 1)
                        pe.wait_ge(sem("xs_copied"), 3).then_inc(sem("xs_copied"), -3)
                        for ee in range(2):
                            base = 4 * ee
                            for f in range(2):
                                if ee:
                                    pe.wait_ge(sem("gu_read"), 1).then_inc(sem("gu_read"), -1)
                                for m in range(2):
                                    sl0 = (base + 2 * m) % 6
                                    if f == 0:
                                        pe.wait_ge(sem(f"slab{sl0}"), 16).then_inc(sem(f"slab{sl0}"), -16)
                                        pe.wait_ge(sem(f"slab{sl0 + 1}"), 16).then_inc(sem(f"slab{sl0 + 1}"), -16)
                                    for k in range(4):
                                        ff = 4 * f + k
                                        for c in range(KC):
                                            last = pe.matmul(ps[:, 2 * f + m, k * CAP:(k + 1) * CAP], ring[:, sl0 + c // 4, c % 4, ff * P:(ff + 1) * P],
                                                            xs[:, c, ee], start=c == 0, stop=c == KC - 1)
                                    last.then_inc(sem("up_ready" if m else "gate_ready"), 1)
                            pe.drain().then_inc(sem("slab_free"), 4)
                        pe.wait_ge(sem("gu_read"), 2).then_inc(sem("gu_read"), -2)
                        for ee in range(2):
                            sl0 = (8 + 2 * ee) % 6
                            pe.wait_ge(sem(f"slab{sl0}"), 16).then_inc(sem(f"slab{sl0}"), -16)
                            pe.wait_ge(sem(f"slab{sl0 + 1}"), 16).then_inc(sem(f"slab{sl0 + 1}"), -16)
                            pe.wait_ge(sem("hid_ready"), 2).then_inc(sem("hid_ready"), -2)
                            for f in range(2):
                                if ee:
                                    pe.wait_ge(sem("down_copied"), 1).then_inc(sem("down_copied"), -1)
                                for k in range(4):
                                    m = 4 * f + k
                                    for c in range(KC):
                                        last = pe.matmul(ps[:, 4 + f, k * CAP:(k + 1) * CAP], ring[:, sl0 + c // 4, c % 4, m * P:(m + 1) * P],
                                                        hid[:, ee, c], start=c == 0, stop=c == KC - 1)
                                last.then_inc(sem("down_ready"), 1)
                            pe.drain().then_inc(sem("slab_free"), 2)
                        pe.wait_ge(sem("down_copied"), 2).then_inc(sem("down_copied"), -2)
                        for m in range(KC):
                            pe.transpose(ps[:, m // 4, (m % 4) * P:(m % 4 + 1) * P], yT[:, m, 0:2 * CAPS], ident)
                            last = pe.transpose(ps[0:2 * CAPP, 2 + m // 4, (m % 4) * P:(m % 4 + 1) * P], yT[:, m, 2 * CAPS:2 * CAP], ident)
                        last.then_inc(sem("yslots_ready"), 1)
                        pe.wait_ge(sem("yslots_copied"), 1).then_inc(sem("yslots_copied"), -1)
                        pe.wait_ge(sem("gT_copied"), 1).then_inc(sem("gT_copied"), -1)
                        for m in range(KC):
                            last = pe.matmul(ps[:, 4 + m // 4, (m % 4) * NP:(m % 4 + 1) * NP], ypn[:, m * P:(m + 1) * P], gp, start=True, stop=True)
                        last.then_inc(sem("yp_ready"), 1)
                        for m in range(KC):
                            if m >= 2:
                                pe.wait_ge(sem("y_read"), 1).then_inc(sem("y_read"), -1)
                            pe.matmul(ps[:, 6 + m % 2], ysn[:, m * P:(m + 1) * P], gs, start=True, stop=True).then_inc(sem("y_ready"), 1)
                        pe.wait_ge(sem("y_read"), 2).then_inc(sem("y_read"), -2)
                        pe.wait_ge(sem("yp_read"), 1).then_inc(sem("yp_read"), -1)

        def odd_mixer():
            PADW = 15
            W = T + 4 * PADW
            WO = W - 2 * PADW
            OFF = NS + 2 * PADW
            cv = Carve()
            win = cv(KC, 2048)
            xp = cv(4, W)
            acc = cv(4, WO)
            vn = cv(4, T)
            vtok = cv(NT, 512)
            ws = cv(4, P)
            bs = cv(4, P, parts=1)
            th = cv(2, T)
            sq = cv(2, T)
            root = cv(T)
            rp = root
            tho = th[:, 0]
            cw = V("conv_w").rearrange("p (c k) -> p c k", c=4)
            tiles = [m for c in range(4) for m in (4 + c, c)] + [12, 13, 14, 15, 8, 9, 10, 11]

            def seg(ap, off):
                return ap[:, 0:NS], ap[:, off:off + NP]

            with stage() as block:
                @block.sync
                def _(sp):
                    for k in range(4):
                        src = t["od_w_in"].rearrange("(c p) (k n) -> k p c n", p=P, k=4)
                        for q in ((1, 0, 3, 2)[k],):
                            sp.dma_start(win[:, :, q * 512:(q + 1) * 512], src[q]).then_inc(sem(f"win{q}"), 16)
                    sp.dma_start(ws, t["ws"].rearrange("p (h n) -> p h n", h=4)).then_inc(sem("ws_in"), 16)
                    sp.dma_start(bs, t["bs"].rearrange("a (h n) -> a h n", h=4)).then_inc(sem("ws_in"), 16)

                @block.tensor
                def _(pe):
                    for n, m in enumerate(tiles):
                        if n == 0:
                            pe.wait_ge(sem("win1"), 16).then_inc(sem("win1"), -16)
                            pe.wait_ge(sem("win0"), 16).then_inc(sem("win0"), -16)
                        if n == 8:
                            pe.wait_ge(sem("win3"), 16).then_inc(sem("win3"), -16)
                        if n == 12:
                            pe.wait_ge(sem("win2"), 16).then_inc(sem("win2"), -16)
                        if n >= 3:
                            pe.wait_ge(sem("tile_read_a" if n - 3 < 8 and (n - 3) % 2 else "tile_read"), 1).then_inc(sem("tile_read_a" if n - 3 < 8 and (n - 3) % 2 else "tile_read"), -1)
                        for a, b in ((0, NS), (NS, T)):
                            for c in range(KC):
                                last = pe.matmul(pair(n % 3)[:, a:b], win[:, c, m * P:(m + 1) * P], h[:, c, a:b], start=c == 0, stop=c == KC - 1)
                        last.then_inc(sem("tile_b" if n < 8 and n % 2 == 0 else "tile_a" if n < 8 else "tile_vu"), 1)
                    pe.wait_ge(sem("tile_read"), 3).then_inc(sem("tile_read"), -3)

                    def layer_mean(src, tag):
                        for c in range(4):
                            pe.wait_ge(sem(tag + "_in"), 1).then_inc(sem(tag + "_in"), -1)
                            for (a, b), s in zip(((0, NS), (NS, T)), src(c)):
                                last = pe.matmul(pair(3)[:, a:b], mean512[:, :], s, start=c == 0, stop=c == 3)
                            if tag.endswith("sq"):
                                last.then_inc(sem(tag + "_used"), 1)
                        pe.drain().then_inc(sem(tag + "_mean"), 1)

                    pe.wait_ge(sem("ws_in"), 32).then_inc(sem("ws_in"), -32)
                    layer_mean(lambda c: (vn[:, c, 0:NS], vn[:, c, NS:T]), "v")
                    pe.wait_ge(sem("v_mean_read"), 1).then_inc(sem("v_mean_read"), -1)
                    layer_mean(lambda c: (sq[:, c % 2, 0:NS], sq[:, c % 2, NS:T]), "vsq")
                    pe.wait_ge(sem("vsq_mean_read"), 1).then_inc(sem("vsq_mean_read"), -1)
                    pe.wait_ge(sem("vn_done"), 1).then_inc(sem("vn_done"), -1)
                    for tt in range(NT):
                        if tt >= 2:
                            pe.wait_ge(sem("vtok_copied"), 1).then_inc(sem("vtok_copied"), -1)
                        for c in range(4):
                            last = pe.transpose(ps[:, tt % 2, c * P:(c + 1) * P], vn[:, c, tt * P:(tt + 1) * P], ident)
                        last.then_inc(sem("vtok_ready"), 1)
                    pe.wait_ge(sem("vtok_copied"), 2).then_inc(sem("vtok_copied"), -2)
                    pe.wait_ge(sem("vtok_all"), 1).then_inc(sem("vtok_all"), -1)
                    for hd in range(4):
                        if hd >= 2:
                            pe.wait_ge(sem("mixed_read"), 1).then_inc(sem("mixed_read"), -1)
                        q = 1 + hd % 2
                        for tt in range(NT):
                            o = pair(q)[:, tt * P:(tt + 1) * P]
                            pe.matmul(o, vtok[:, tt, hd * P:(hd + 1) * P], ws[:, hd], start=True, stop=False)
                            last = pe.matmul(o, ones[0:1, :], bs[:, hd], start=False, stop=True)
                        last.then_inc(sem("mixed_ready"), 1)
                    pe.wait_ge(sem("mixed_read"), 2).then_inc(sem("mixed_read"), -2)
                    layer_mean(lambda c: seg(acc[:, c], OFF), "c")
                    pe.wait_ge(sem("c_mean_read"), 1).then_inc(sem("c_mean_read"), -1)
                    layer_mean(lambda c: (sq[:, c % 2, 0:NS], sq[:, c % 2, NS:T]), "csq")
                    pe.wait_ge(sem("csq_mean_read"), 1).then_inc(sem("csq_mean_read"), -1)

                @block.scalar
                def _(act):
                    for c in range(4):
                        act.wait_ge(sem("tile_b"), 1).then_inc(sem("tile_b"), -1)
                        if c >= 2:
                            act.wait_ge(sem("th_used"), 1).then_inc(sem("th_used"), -1)
                        act.activation(th[:, c % 2], pair(2 * c % 3), ACT.Tanh, scale=0.5).then_inc(act_done, 1)
                        act.wait_ge(act_done, 1).then_inc(act_done, -1)
                        act.sem_inc(sem("tile_read"), 1)
                        act.sem_inc(sem("th_ready"), 1)
                    act.wait_ge(sem("th_used"), 2).then_inc(sem("th_used"), -2)
                    for n in range(8, 16):
                        act.wait_ge(sem("tile_vu"), 1).then_inc(sem("tile_vu"), -1)
                        out = vn[:, n - 8] if n < 12 else mix[:, n - 8]
                        act.activation(out, pair(n % 3), ACT.Gelu_apprx_tanh).then_inc(act_done, 1)
                        act.wait_ge(act_done, 1).then_inc(act_done, -1)
                        act.sem_inc(sem("tile_read"), 1)
                        if n < 12:
                            act.sem_inc(sem("v_in"), 1)
                    act.sem_inc(sem("gelu_done"), 1)

                    def var(src, tag):
                        for c in range(4):
                            act.wait_ge(sem(tag + "_centred"), 1).then_inc(sem(tag + "_centred"), -1)
                            if c >= 2:
                                act.wait_ge(sem(tag + "sq_used"), 1).then_inc(sem(tag + "sq_used"), -1)
                            for (a, b), s in zip(((0, NS), (NS, T)), src(c)):
                                act.activation(sq[:, c % 2, a:b], s, ACT.Square).then_inc(act_done, 1)
                            act.wait_ge(act_done, 2).then_inc(act_done, -2)
                            act.sem_inc(sem(tag + "sq_in"), 1)
                        act.wait_ge(sem(tag + "sq_used"), 2).then_inc(sem(tag + "sq_used"), -2)
                        act.wait_ge(sem(tag + "sq_mean"), 1).then_inc(sem(tag + "sq_mean"), -1)
                        act.activation(root, pair(3), ACT.Sqrt, bias=eps[:, 1:2]).then_inc(act_done, 1)
                        act.wait_ge(act_done, 1).then_inc(act_done, -1)
                        act.sem_inc(sem(tag + "_root"), 1)
                        act.sem_inc(sem(tag + "sq_mean_read"), 1)

                    var(lambda c: (vn[:, c, 0:NS], vn[:, c, NS:T]), "v")
                    for c in range(4):
                        act.wait_ge(sem("v_scaled"), 1).then_inc(sem("v_scaled"), -1)
                        act.activation(vn[:, c], vn[:, c], ACT.Identity, scale=V("vln_g", c, c + 1), bias=V("vln_b", c, c + 1)).then_inc(act_done, 1)
                    act.wait_ge(act_done, 4).then_inc(act_done, -4)
                    act.sem_inc(sem("vn_done"), 1)
                    for tt in range(NT):
                        act.wait_ge(sem("vtok_ready"), 1).then_inc(sem("vtok_ready"), -1)
                        act.activation(vtok[:, tt], ps[:, tt % 2], ACT.Copy).then_inc(act_done, 1)
                        act.wait_ge(act_done, 1).then_inc(act_done, -1)
                        act.sem_inc(sem("vtok_copied"), 1)
                    act.sem_inc(sem("vtok_all"), 1)
                    var(lambda c: seg(acc[:, c], OFF), "c")
                    for c in range(4):
                        act.wait_ge(sem("c_scaled"), 1).then_inc(sem("c_scaled"), -1)
                        act.activation(acc[:, c], acc[:, c], ACT.Identity, scale=V("cln_g", c, c + 1), bias=V("cln_b", c, c + 1)).then_inc(act_done, 1)
                        act.wait_ge(act_done, 1).then_inc(act_done, -1)
                        if c:
                            act.wait_ge(sem("tho_used"), 1).then_inc(sem("tho_used"), -1)
                        for (a, b), s in zip(((0, NS), (NS, T)), seg(acc[:, c], OFF)):
                            act.activation(tho[:, a:b], s, ACT.Tanh, scale=0.5).then_inc(act_done, 1)
                        act.wait_ge(act_done, 2).then_inc(act_done, -2)
                        act.sem_inc(sem("tho_ready"), 1)
                    act.wait_ge(sem("tho_used"), 1).then_inc(sem("tho_used"), -1)

                @block.gpsimd
                def _(pool):
                    pool.memset(xp, 0.0).then_inc(pool_done, 1)
                    pool.wait_ge(pool_done, 1).then_inc(pool_done, -1)
                    pool.sem_inc(sem("xp_zero"), 1)

                @block.vector
                def _(dve):
                    dve.wait_ge(sem("xp_zero"), 1).then_inc(sem("xp_zero"), -1)
                    for c in range(4):
                        dve.wait_ge(sem("tile_a"), 1).then_inc(sem("tile_a"), -1)
                        dve.wait_ge(sem("th_ready"), 1).then_inc(sem("th_ready"), -1)
                        for (a, b), s in zip(((0, NS), (NS, T)), seg(xp[:, c, PADW:W - PADW], OFF)):
                            dve.scalar_tensor_tensor(s, th[:, c % 2, a:b], 1.0, pair((2 * c + 1) % 3)[:, a:b], ALU.add, ALU.mult).then_inc(dve_done, 1)
                        dve.wait_ge(dve_done, 2).then_inc(dve_done, -2)
                        dve.sem_inc(sem("tile_read_a"), 1)
                        dve.sem_inc(sem("th_used"), 1)
                    dve.tensor_scalar(xp, xp, 0.5, None, ALU.mult).then_inc(dve_done, 1)
                    dve.wait_ge(dve_done, 1).then_inc(dve_done, -1)
                    for k in range(TAPS):
                        for c in range(4):
                            src = xp[:, c, k:k + WO]
                            if k == 0:
                                dve.tensor_scalar(acc[:, c], src, cw[:, c, 0:1], V("conv_b", c, c + 1), ALU.mult, ALU.add).then_inc(dve_done, 1)
                            else:
                                dve.scalar_tensor_tensor(acc[:, c], src, cw[:, c, k:k + 1], acc[:, c], ALU.mult, ALU.add).then_inc(dve_done, 1)
                        dve.wait_ge(dve_done, 4).then_inc(dve_done, -4)

                    def centre(dst, tag):
                        dve.wait_ge(sem(tag + "_mean"), 1).then_inc(sem(tag + "_mean"), -1)
                        for c in range(4):
                            for (a, b), s in zip(((0, NS), (NS, T)), dst(c)):
                                dve.tensor_tensor(s, s, pair(3)[:, a:b], ALU.subtract).then_inc(dve_done, 1)
                            dve.wait_ge(dve_done, 2).then_inc(dve_done, -2)
                            dve.sem_inc(sem(tag + "_centred"), 1)
                        dve.sem_inc(sem(tag + "_mean_read"), 1)

                    def scale(dst, tag):
                        dve.wait_ge(sem(tag + "_root"), 1).then_inc(sem(tag + "_root"), -1)
                        dve.reciprocal(rp, root).then_inc(dve_done, 1)
                        dve.wait_ge(dve_done, 1).then_inc(dve_done, -1)
                        for c in range(4):
                            for (a, b), s in zip(((0, NS), (NS, T)), dst(c)):
                                dve.tensor_tensor(s, s, rp[:, a:b], ALU.mult).then_inc(dve_done, 1)
                            dve.wait_ge(dve_done, 2).then_inc(dve_done, -2)
                            dve.sem_inc(sem(tag + "_scaled"), 1)

                    vd = lambda c: (vn[:, c, 0:NS], vn[:, c, NS:T])
                    cd = lambda c: seg(acc[:, c], OFF)
                    centre(vd, "v")
                    scale(vd, "v")
                    dve.wait_ge(sem("gelu_done"), 1).then_inc(sem("gelu_done"), -1)
                    for hd in range(4):
                        dve.wait_ge(sem("mixed_ready"), 1).then_inc(sem("mixed_ready"), -1)
                        dve.tensor_tensor(mix[:, 4 + hd], mix[:, 4 + hd], pair(1 + hd % 2), ALU.mult).then_inc(dve_done, 1)
                        dve.wait_ge(dve_done, 1).then_inc(dve_done, -1)
                        dve.sem_inc(sem("mixed_read"), 1)
                    dve.sem_inc(sem("c_in"), 4)
                    centre(cd, "c")
                    scale(cd, "c")
                    for c in range(4):
                        dve.wait_ge(sem("tho_ready"), 1).then_inc(sem("tho_ready"), -1)
                        for (a, b), s in zip(((0, NS), (NS, T)), cd(c)):
                            dve.scalar_tensor_tensor(mix[:, c, a:b], tho[:, a:b], 1.0, s, ALU.add, ALU.mult).then_inc(dve_done, 1)
                        dve.wait_ge(dve_done, 2).then_inc(dve_done, -2)
                        dve.sem_inc(sem("tho_used"), 1)
                        dve.tensor_scalar(mix[:, c], mix[:, c], 0.5, None, ALU.mult).then_inc(dve_done, 1)
                        dve.wait_ge(dve_done, 1).then_inc(dve_done, -1)

        def fill(l):
            def go(sp):
                for n in range(6):
                    load_slab(sp, l, 0, n)
            return go

        def layer_tail(l, w):
            out_proj(l, w)
            norm(l, 1, fill(l))
            route(l, lambda sp: None)
            experts(l)

        setup()
        if stop >= 1:
            norm(0, 0)
            even_front()
            even_heads()
            if stop >= 2:
                out_proj(0, t["ev_w_out"])
            if stop >= 3:
                norm(0, 1, fill(0))
                route(0, lambda sp: None)
                experts(0)
        if stop >= 4:
            norm(1, 0)
            odd_mixer()
            layer_tail(1, t["od_w_out"])
            norm(None, None)
        else:
            out_x()


def _constants():
    p = np.arange(P)
    cst = np.zeros((P, NCST), np.float32)

    def put(name, a):
        lo, hi = CST[name]
        cst[:, lo:hi] = np.asarray(a, np.float32).reshape(P, hi - lo)

    put("ident", np.eye(P))
    put("headones", (p[:, None] // HD == p[None, :] // HD))
    put("iota", np.broadcast_to(np.arange(64), (P, 64)))
    m = np.arange(64)
    ang = 2 * np.pi * ((m[:, None] * m[None, :]) % 64) / 64
    two = np.eye(2)
    put("dft64", np.concatenate([np.kron(two, np.cos(ang)), np.kron(two, -np.sin(ang))], axis=1))
    freq = (1.0 / (np.float32(10000.0) ** (np.arange(256, dtype=np.float32) / np.float32(256)))).astype(np.float32)
    ar = (freq[:, None] * np.arange(8, dtype=np.float32)[None]).astype(np.float32)
    ac = (freq[:, None] * np.arange(64, dtype=np.float32)[None]).astype(np.float32)
    row = np.concatenate([np.sin(ar), np.cos(ar)]).reshape(4, P, 8).transpose(1, 0, 2)
    col = np.concatenate([np.sin(ac), np.cos(ac)]).reshape(4, P, 64).transpose(1, 0, 2)
    put("posrow", row)
    put("poscol", col)
    s, t = p[:, None], p[None, :]
    tri = np.stack([np.concatenate([s < t, s <= t] * 2, axis=1), np.concatenate([s > t, s >= t] * 2, axis=1)], axis=1)
    put("tri", tri)
    m8 = np.zeros((P, LEVELS + 1, 2, P), np.float32)
    for lev in range(LEVELS + 1):
        b = 2 ** lev
        same = (s // (2 * b) == t // (2 * b)) & (s // b != t // b)
        m8[:, lev, 0] = same & (s < t)
        m8[:, lev, 1] = same & (s > t)

    def dft(n):
        k = np.arange(n)
        a = 2 * np.pi * ((k[:, None] * k[None, :]) % n) / n
        both = np.stack([np.cos(a), np.sin(a)], axis=1) / np.sqrt(n * 64.0)
        return both.reshape(n // P, P, 2, n).transpose(1, 0, 2, 3).reshape(P, -1).astype(np.float32)

    return {"cst": cst, "m8": m8.reshape(P, -1), "dft_s": dft(NS), "dft_p": dft(NP)}


STOP = 99


def kernel(**inputs):
    import concourse.bacc as _bacc
    from concourse.bass_utils import run_bass_kernel_spmd as _run

    a = {k: np.asarray(v) for k, v in inputs.items()}

    def cols(v):
        return v.reshape(-1, P).T

    vec = np.concatenate([
        cols(a["mod_b"]), cols(a["norm_mix"]), cols(a["norm_ffn"]), cols(a["final_norm"]), cols(a["ev_mu_wag"]),
        np.stack([cols(a["c"]), cols(a["c_ctx"])], axis=2).reshape(P, 16),
        a["od_conv_w"][0].T.reshape(4, P, TAPS).transpose(1, 0, 2).reshape(P, -1),
        cols(a["od_conv_b"]), cols(a["od_cln_g"]), cols(a["od_cln_b"]), cols(a["od_vln_g"]), cols(a["od_vln_b"]),
    ], axis=1)
    heads = [a["ev_mu_rkv"][0, 0], a["ev_mu_rkv"][0, 1], a["ev_mu_rkv"][0, 2], a["ev_w0"][0, 0], a["ev_w0"][0, 1],
             a["ev_a0"][0, 0], a["ev_a0"][0, 1], a["ev_k_k"][0], a["ev_k_a"][0], a["ev_r_k"][0].reshape(-1),
             a["ev_gn_w"][0], a["ev_gn_b"][0]]
    dirs = lambda w: w[0].transpose(1, 0, 2).reshape(D, P)
    arrays = {
        "xT": np.concatenate([a["x_sample"][0], a["x_prompt"][0]], axis=0).T,
        "vec": vec,
        "hpv": np.stack(heads, axis=1).reshape(HP, P, NHPV),
        "state": a["state_wkv"][0, 0].transpose(0, 1, 3, 2).reshape(2, HP, P, HD),
        "lora1": np.concatenate([dirs(a["ev_w1"]), dirs(a["ev_a1"]), a["ev_g1"][0]], axis=1),
        "lora2": np.stack([a["ev_w2"][0].reshape(P, -1), a["ev_a2"][0].reshape(P, -1), a["ev_g2"][0]]),
        "router": a["moe_router"], "router_b": a["moe_router_b"],
        "ws": a["od_w_s"][0].transpose(2, 0, 1).reshape(P, 512), "bs": a["od_b_s"].reshape(1, 512),
        "ev_w_in": a["ev_w_in"][0], "ev_w_out": a["ev_w_out"][0], "od_w_in": a["od_w_in"][0], "od_w_out": a["od_w_out"][0],
        "mod_w": a["mod_w"], "moe_w_gate": a["moe_w_gate"], "moe_w_up": a["moe_w_up"], "moe_w_down": a["moe_w_down"],
        **_constants(),
    }
    arrays = {k: np.ascontiguousarray(v) for k, v in arrays.items()}
    nc = _bacc.Bacc("TRN2", target_bir_lowering=False, num_devices=1)
    t = {k: nc.dram_tensor("in_" + k, v.shape, mybir.dt.from_np(v.dtype), kind="ExternalInput").ap() for k, v in arrays.items()}
    t["yT"] = nc.dram_tensor("out_y", (D, T), F32, kind="ExternalOutput").ap()
    t["st_out"] = nc.dram_tensor("out_state", (2, HP, P, HD), F32, kind="ExternalOutput").ap()
    build(nc, t, STOP)
    r = _run(nc, [{"in_" + k: v for k, v in arrays.items()}], core_ids=[0]).results[0]
    y = np.asarray(r["out_y"]).T
    state = np.asarray(r["out_state"]).reshape(2, 2 * HP, HD, HD).transpose(0, 1, 3, 2)
    return np.ascontiguousarray(y[NS:])[None], np.ascontiguousarray(y[:NS])[None], np.ascontiguousarray(state)[None, None]
```

```python
from contextlib import ExitStack, contextmanager

import numpy as np
import concourse.bass as bass
from concourse import mybir

ALU = mybir.AluOpType
ACT = mybir.ActivationFunctionType
AX = mybir.AxisListType
F32 = mybir.dt.float32
F32R = mybir.dt.float32r
U8 = mybir.dt.uint8
U32 = mybir.dt.uint32

P = 128
D = 1024
KC = D // P
NS, NP = 512, 128
T = NS + NP
NT = T // P
ST = NS // P
SEGS = ((0, 0, NS), (1, NS, T))
HP = 6
HD = 64
E = 16
CAPS, CAPP = 2 * NS // E, 2 * NP // E
CAP = CAPS + CAPP
LEVELS = 6
TAPS = 31
EXPH = float(np.exp(-0.5))
RMS_EPS, LN_EPS, GN_EPS = 1e-6, 1e-5, 64e-5

VEC = {}
_n = 0
for _name, _w in (("mod_b", 96), ("norm_mix", 16), ("norm_ffn", 16), ("final", 8), ("mu_wag", 24), ("cond", 16),
                  ("conv_w", 4 * TAPS), ("conv_b", 4), ("cln_g", 4), ("cln_b", 4), ("vln_g", 4), ("vln_b", 4)):
    VEC[_name] = (_n, _n + _w)
    _n += _w
NVEC = _n
CST = {}
_n = 0
for _name, _w in (("ident", 128), ("headones", 128), ("iota", 64), ("dft64", 256), ("posrow", 32), ("poscol", 256), ("tri", 1024)):
    CST[_name] = (_n, _n + _w)
    _n += _w
NCST = _n
NKEEP = CST["iota"][1]
HPV = dict(mu=0, w0=3, a0=5, k_k=7, k_a=8, r_k=9, gn_w=10, gn_b=11)
NHPV = 12


def bcast(ap, axis, n):
    ap = ap.unsqueeze(axis)
    shape = list(ap.shape)
    shape[axis] = n
    return ap.broadcast_to(shape)


def build(nc, t):
    ctx = ExitStack()
    with ctx:
        def sb(name, shape, dt=F32):
            return ctx.enter_context(nc.sbuf_tensor(name, shape, dt))

        lasting, passing = {}, {}
        scope = []

        def sem(name):
            if name.startswith(("slab", "act_done", "dve_done", "pool_done", "sp_done", "pe_done")):
                if name not in lasting:
                    lasting[name] = ctx.enter_context(nc.semaphore(name))
                return lasting[name]
            if name not in passing:
                passing[name] = scope[-1].enter_context(nc.semaphore(name))
            return passing[name]

        @contextmanager
        def stage():
            with ExitStack() as names:
                scope.append(names)
                with nc.Block() as block:
                    yield block
                scope.pop()
                passing.clear()

        x = sb("x", [P, KC, T])
        h = sb("h", [P, KC, T])
        vec = sb("vec", [P, NVEC])
        cst = sb("cst", [P, NKEEP])
        mod = sb("mod", [P, 2, 6, KC, 2])
        gain = sb("gain", [P, 4, KC, 2])
        mean1024 = sb("mean1024", [P, P])
        mean512 = sb("mean512", [P, P])
        ones = sb("ones", [P, P])
        slot = sb("slot", [P, NT, E + 2])
        aff = sb("aff", [P, NT, E + 2])
        eps = sb("eps", [P, 3])
        work = {}
        ps = ctx.enter_context(nc.psum_tensor("ps", [P, 8, 512], F32))
        psf = ps[:, :, :].rearrange("p b n -> p (b n)")

        def pair(q):
            return psf[:, q * 1024:q * 1024 + T]

        def V(name, a=0, b=None):
            lo, hi = VEC[name]
            return vec[:, lo + a:(lo + b) if b is not None else hi]

        def C(name):
            lo, hi = CST[name]
            return cst[:, lo:hi] if hi <= NKEEP else work["tables"][:, lo - NKEEP:hi - NKEEP]

        class Carve:

            def __init__(self, at=0):
                self.at = at
                self.area, self.size = work["area"], work["size"]

            def __call__(self, *shape, parts=P):
                n = int(np.prod(shape))
                ap = self.area[0:parts, self.at:self.at + n]
                self.at += n
                assert self.at <= self.size, self.at
                if len(shape) == 1:
                    return ap
                names = "abcde"[:len(shape)]
                kw = {names[i]: shape[i] for i in range(1, len(shape))}
                return ap.rearrange(f"p ({' '.join(names)}) -> p {' '.join(names)}", **kw)

        ident = C("ident")
        for name in [f"slab{n}" for n in range(6)] + ["slab_free"] + ["act_done", "dve_done", "pool_done", "sp_done", "pe_done"]:
            sem(name)
        act_done, dve_done, pool_done, sp_done = (sem(e + "_done") for e in ("act", "dve", "pool", "sp"))

        @contextmanager
        def mixer_memory(layer):
            with ExitStack() as mem:
                mix = mem.enter_context(nc.sbuf_tensor(f"mix_{layer}", [P, KC, T], F32))
                lora = mem.enter_context(nc.sbuf_tensor(f"lora_{layer}", [P, 3, T], F32))
                tables = mem.enter_context(nc.sbuf_tensor(f"tables_{layer}", [P, NCST - NKEEP], F32))
                m8 = mem.enter_context(nc.sbuf_tensor(f"m8_{layer}", [P, LEVELS + 1, 2, P], U8))
                size = 32300
                area = mem.enter_context(nc.sbuf_tensor(f"wk_{layer}", [P, size], F32))
                work.update(area=area, size=size, mix=mix, lora=lora, tables=tables, m8=m8)
                yield
                work.clear()

        PIECES = 48
        RAW, SPLIT = 4, 6

        @contextmanager
        def expert_memory(layer):
            with ExitStack() as mem:
                def tile(name, shape, dt=F32):
                    work[name] = mem.enter_context(nc.sbuf_tensor(f"{name}_{layer}", shape, dt))
                tile("raw", [P, RAW, 2, D])
                tile("wh", [P, SPLIT, D], F32R)
                tile("wl", [P, SPLIT, D], F32R)
                tile("htok", [P, 2, NT, D], F32R)
                tile("oh", [P, ST, 2, CAPS], F32R)
                tile("ohp", [P, 2, CAPP], F32R)
                tile("ohg", [P, 80], F32R)
                tile("gs", [P, NS], F32R)
                tile("gp", [80, NP], F32R)
                tile("xs0", [P, 2, KC, 80], F32R)
                tile("xs1", [P, 2, KC, P], F32R)
                tile("ys", [P, 2, D], F32R)
                tile("yp", [80, 2, D], F32R)
                work.update(area=work["raw"][:, RAW - 2:].rearrange("p a c n -> p (a c n)"), size=4 * D)
                yield
                work.clear()

        def setup():
            cv = Carve()
            ring = cv(6, 4, 1024)
            th = cv(KC, 2)
            scond = cv(KC, 2)
            rows = cv(3, D, parts=2)
            m32 = cv((LEVELS + 1) * 2 * P)
            modw = t["mod_w"]

            with stage() as block:
                @block.sync
                def _(sp):
                    sp.dma_start(vec[:, :], t["vec"]).then_inc(sem("vec_in"), 16)
                    sp.dma_start(cst[:, :], t["cst"][:, 0:NKEEP]).then_inc(sem("const_in"), 16)
                    sp.dma_start(work["tables"][:, :], t["cst"][:, NKEEP:]).then_inc(sem("const_in"), 16)
                    sp.dma_start(m32, t["m8"]).then_inc(sem("const_in"), 16)
                    sp.sem_inc(sem("slab_free"), 6)
                    for l in range(2):
                        with sp.Fori(0, 2) as i:
                            for s in range(3):
                                for k in range(2):
                                    sp.wait_ge(sem("slab_free"), 1).then_inc(sem("slab_free"), -1)
                                    src = modw[l, k * 512:(k + 1) * 512, :].rearrange("(c p) (i s n) -> i s p c n", p=P, i=2, s=3)
                                    sp.dma_start(ring[:, 2 * s + k], src[bass.ds(i, 1), s].rearrange("a p c n -> p (a c) n")).then_inc(sem(f"slab{2 * s + k}"), 16)
                        if l == 0:
                            sp.dma_start(x[:, :, :], t["xT"].rearrange("(c p) n -> p c n", p=P)).then_inc(sem("x_in"), 16)
                    sp.wait_ge(sem("slab_free"), 6).then_inc(sem("slab_free"), -6)
                    sp.wait_ge(sem("x_in"), 16).then_inc(sem("x_in"), -16)
                    sp.sem_inc(sem("x_here"), 1)
                    sp.sem_inc(sem("x_here2"), 1)

                @block.scalar
                def _(act):
                    act.wait_ge(sem("vec_in"), 16).then_inc(sem("vec_in"), -16)
                    act.activation(th, V("cond").rearrange("p (c r) -> p c r", r=2), ACT.Tanh, scale=0.5).then_inc(act_done, 1)
                    act.wait_ge(act_done, 1).then_inc(act_done, -1)
                    act.sem_inc(sem("th"), 1)
                    for l in range(2):
                        with act.Fori(0, 2) as i:
                            for s in range(3):
                                act.wait_ge(sem("rows_ready"), 1).then_inc(sem("rows_ready"), -1)
                                act.activation(rows[:, s], psf[0:2, s * D:(s + 1) * D], ACT.Copy).then_inc(sem("rows_copied"), 1)

                @block.tensor
                def _(pe):

                    def turn(s):
                        pe.wait_ge(sem("rows_copied"), 1).then_inc(sem("rows_copied"), -1)
                        for j in range(KC):
                            last = pe.transpose(ps[:, 6 + s % 2, 2 * j:2 * j + 2], rows[:, s, j * P:(j + 1) * P], ident[0:2, 0:2])
                        last.then_inc(sem("mod_done"), 1)

                    pe.wait_ge(sem("scond"), 1).then_inc(sem("scond"), -1)
                    pe.wait_ge(sem("ident_in"), 1).then_inc(sem("ident_in"), -1)
                    for l in range(2):
                        with pe.Fori(0, 2) as i:
                            for s in range(3):
                                for k in range(2):
                                    pe.wait_ge(sem(f"slab{2 * s + k}"), 16).then_inc(sem(f"slab{2 * s + k}"), -16)
                                    for c in range(4 * k, 4 * k + 4):
                                        for b in range(2):
                                            last = pe.matmul(ps[0:2, 2 * s + b], scond[:, c, :], ring[:, 2 * s + k, c % 4, b * 512:(b + 1) * 512],
                                                            start=c == 0, stop=c == KC - 1)
                                    last.then_inc(sem("slab_free"), 1)
                                pe.drain().then_inc(sem("rows_ready"), 1)
                                if s:
                                    turn(s - 1)
                            pe.wait_ge(sem("mod_read"), 1).then_inc(sem("mod_read"), -1)
                            turn(2)
                            pe.wait_ge(sem("mod_read"), 2).then_inc(sem("mod_read"), -2)

                @block.vector
                def _(dve):
                    dve.wait_ge(sem("th"), 1).then_inc(sem("th"), -1)
                    cond = V("cond").rearrange("p (c r) -> p c r", r=2)
                    dve.scalar_tensor_tensor(scond, th, 1.0, cond, ALU.add, ALU.mult).then_inc(dve_done, 1)
                    dve.wait_ge(dve_done, 1).then_inc(dve_done, -1)
                    dve.tensor_scalar(scond, scond, 0.5, None, ALU.mult).then_inc(dve_done, 1)
                    dve.wait_ge(dve_done, 1).then_inc(dve_done, -1)
                    dve.sem_inc(sem("scond"), 1)
                    modv = mod[:, :, :, :, :].rearrange("p l (i s) j r -> p l i s j r", i=2)
                    modb = V("mod_b").rearrange("p (l i s j) -> p l i s j", l=2, i=2, s=3)
                    for l in range(2):
                        with dve.Fori(0, 2) as i:
                            for s in range(3):
                                dve.wait_ge(sem("mod_done"), 1).then_inc(sem("mod_done"), -1)
                                out = modv[:, l, bass.ds(i, 1), s].rearrange("p a j r -> p (a j) r")
                                b = modb[:, l, bass.ds(i, 1), s].rearrange("p a j -> p (a j)")
                                dve.tensor_tensor(out, ps[:, 6 + s % 2, 0:16].rearrange("p (j r) -> p j r", r=2), bcast(b, 2, 2), ALU.add).then_inc(dve_done, 1)
                                dve.wait_ge(dve_done, 1).then_inc(dve_done, -1)
                                dve.sem_inc(sem("mod_read"), 1)
                    for l in range(2):
                        for n, (part, g) in enumerate(((1, "norm_mix"), (4, "norm_ffn"))):
                            dve.scalar_tensor_tensor(gain[:, 2 * l + n], mod[:, l, part], 1.0,
                                                        bcast(V(g, 8 * l, 8 * l + 8), 2, 2), ALU.add, ALU.mult).then_inc(dve_done, 1)
                    dve.wait_ge(dve_done, 4).then_inc(dve_done, -4)

                @block.gpsimd
                def _(pool):
                    pool.memset(mean1024[:, :], 1.0 / D).then_inc(pool_done, 1)
                    pool.memset(mean512[:, :], 1.0 / 512).then_inc(pool_done, 1)
                    pool.memset(ones[:, :], 1.0).then_inc(pool_done, 1)
                    pool.memset(slot[:, :, E:], -1.0).then_inc(pool_done, 1)
                    pool.memset(aff[:, :, E:], 0.0).then_inc(pool_done, 1)
                    for n, v in enumerate((RMS_EPS, LN_EPS, GN_EPS)):
                        pool.memset(eps[:, n:n + 1], v).then_inc(pool_done, 1)
                    pool.wait_ge(pool_done, 8).then_inc(pool_done, -8)
                    pool.wait_ge(sem("const_in"), 48).then_inc(sem("const_in"), -48)
                    pool.sem_inc(sem("ident_in"), 1)
                    pool.tensor_copy(work["m8"][:, :, :, :].rearrange("p l z n -> p (l z n)"), m32).then_inc(pool_done, 1)
                    pool.wait_ge(sem("x_here"), 1).then_inc(sem("x_here"), -1)
                    pool.wait_ge(sem("x_here2"), 1).then_inc(sem("x_here2"), -1)
                    row = C("posrow").rearrange("p (c r) -> p c r", c=4)
                    col = C("poscol").rearrange("p (c w) -> p c w", c=4)
                    for c in range(4):
                        g = x[:, c, 0:NS].rearrange("p (r w) -> p r w", w=64)
                        pool.tensor_tensor(g, g, bcast(row[:, c], 2, 64), ALU.add).then_inc(pool_done, 1)
                        g = x[:, c + 4, 0:NS].rearrange("p (r w) -> p r w", w=64)
                        pool.tensor_tensor(g, g, bcast(col[:, c], 1, 8), ALU.add).then_inc(pool_done, 1)
                    pool.wait_ge(pool_done, 9).then_inc(pool_done, -9)

        def norm(l, n, prefetch=None):
            cv = Carve()
            sq = cv(2, T)
            root = cv(T)
            rstd = cv(T)

            with stage() as block:
                @block.scalar
                def _(act):
                    for c in range(KC):
                        if c >= 2:
                            act.wait_ge(sem("sq_used"), 1).then_inc(sem("sq_used"), -1)
                        act.activation(sq[:, c % 2], x[:, c], ACT.Square).then_inc(sem("sq_ready"), 1)
                    act.wait_ge(sem("sq_used"), 2).then_inc(sem("sq_used"), -2)
                    act.wait_ge(sem("mean_ready"), 1).then_inc(sem("mean_ready"), -1)
                    act.activation(root, pair(0), ACT.Sqrt, bias=eps[:, 0:1]).then_inc(act_done, 1)
                    act.wait_ge(act_done, 1).then_inc(act_done, -1)
                    act.sem_inc(sem("root_ready"), 1)
                    for c in range(KC):
                        act.wait_ge(sem("scaled"), 1).then_inc(sem("scaled"), -1)
                        if n is None:
                            act.mul(h[:, c], h[:, c], V("final", c, c + 1)).then_inc(act_done, 1)
                            continue
                        for r, a, b in SEGS:
                            act.activation(h[:, c, a:b], h[:, c, a:b], ACT.Identity, scale=gain[:, 2 * l + n, c, r:r + 1],
                                              bias=mod[:, l, 3 * n, c, r:r + 1]).then_inc(act_done, 1)
                    act.wait_ge(act_done, KC if n is None else 2 * KC).then_inc(act_done, -(KC if n is None else 2 * KC))
                    if n is None:
                        act.sem_inc(sem("final_ready"), 1)

                @block.tensor
                def _(pe):
                    for c in range(KC):
                        pe.wait_ge(sem("sq_ready"), 1).then_inc(sem("sq_ready"), -1)
                        for a, b in ((0, NS), (NS, T)):
                            last = pe.matmul(pair(0)[:, a:b], mean1024[:, :], sq[:, c % 2, a:b], start=c == 0, stop=c == KC - 1)
                        last.then_inc(sem("sq_used"), 1)
                    pe.drain().then_inc(sem("mean_ready"), 1)

                @block.vector
                def _(dve):
                    dve.wait_ge(sem("root_ready"), 1).then_inc(sem("root_ready"), -1)
                    dve.reciprocal(rstd, root).then_inc(dve_done, 1)
                    dve.wait_ge(dve_done, 1).then_inc(dve_done, -1)
                    for c in range(KC):
                        dve.tensor_tensor(h[:, c], x[:, c], rstd, ALU.mult).then_inc(sem("scaled"), 1)

                @block.sync
                def _(sp):
                    if n is None:
                        sp.wait_ge(sem("final_ready"), 1).then_inc(sem("final_ready"), -1)
                        sp.dma_start(t["yT"].rearrange("(c p) n -> p c n", p=P), h[:, :, :]).then_inc(sem("y_out"), 16)
                        sp.wait_ge(sem("y_out"), 16).then_inc(sem("y_out"), -16)
                        return
                    if prefetch:
                        prefetch(sp)

        def even_front():
            mix, lora = work["mix"], work["lora"]
            cv = Carve()
            dh = cv(KC, T)
            xm = cv(2, KC, T)
            w1 = cv(KC, 3, P)
            wu = cv(KC, 256)
            ufeat = cv(2, T)
            utok = cv(NT, 2, 2, P)
            dfs = cv(4, 2, NS)
            dfp = cv(2, NP)
            dft64 = C("dft64")

            with stage() as block:
                @block.sync
                def _(sp):
                    sp.dma_start(w1, t["lora1"].rearrange("(c p) (s n) -> p c s n", p=P, s=3)).then_inc(sem("w1_in"), 16)
                    sp.dma_start(wu, t["ev_w_in"][:, 3 * 768:].rearrange("(c p) n -> p c n", p=P)).then_inc(sem("wu_in"), 16)
                    sp.dma_start(dfs, t["dft_s"].rearrange("p (c k n) -> p c k n", c=4, k=2)).then_inc(sem("dft_in"), 16)
                    sp.dma_start(dfp, t["dft_p"].rearrange("p (k n) -> p k n", k=2)).then_inc(sem("dft_in"), 16)

                @block.vector
                def _(dve):
                    for c in range(KC):
                        dve.tensor_tensor(dh[:, c, 1:T - 1], h[:, c, 0:T - 2], h[:, c, 2:T], ALU.add).then_inc(dve_done, 1)
                    dve.wait_ge(dve_done, 8).then_inc(dve_done, -8)
                    dve.tensor_copy(dh[:, :, 0:NS + 1:NS], h[:, :, 1:NS + 2:NS]).then_inc(dve_done, 1)
                    dve.tensor_copy(dh[:, :, NS - 1:T:NP], h[:, :, NS - 2:T - 1:NP]).then_inc(dve_done, 1)
                    dve.wait_ge(dve_done, 2).then_inc(dve_done, -2)
                    for c in range(KC):
                        dve.scalar_tensor_tensor(dh[:, c], dh[:, c], 0.5, h[:, c], ALU.mult, ALU.subtract).then_inc(dve_done, 1)
                    dve.wait_ge(dve_done, 8).then_inc(dve_done, -8)
                    mu = V("mu_wag").rearrange("p (s c) -> p s c", s=3)
                    for s in range(3):
                        if s >= 2:
                            dve.wait_ge(sem("xm_used"), 1).then_inc(sem("xm_used"), -1)
                        for c in range(KC):
                            dve.scalar_tensor_tensor(xm[:, s % 2, c], dh[:, c], mu[:, s, c:c + 1], h[:, c], ALU.mult, ALU.add).then_inc(dve_done, 1)
                        dve.wait_ge(dve_done, 8).then_inc(dve_done, -8)
                        dve.sem_inc(sem("xm_ready"), 1)
                    dve.wait_ge(sem("xm_used"), 2).then_inc(sem("xm_used"), -2)
                    dve.wait_ge(sem("half_sigmoid"), 1).then_inc(sem("half_sigmoid"), -1)
                    dve.tensor_scalar(lora[:, 2], lora[:, 2], 0.5, 0.5, ALU.mult, ALU.add).then_inc(dve_done, 1)
                    dve.wait_ge(dve_done, 1).then_inc(dve_done, -1)

                @block.tensor
                def _(pe):
                    pe.wait_ge(sem("w1_in"), 16).then_inc(sem("w1_in"), -16)
                    for s in range(3):
                        pe.wait_ge(sem("xm_ready"), 1).then_inc(sem("xm_ready"), -1)
                        for a, b in ((0, NS), (NS, T)):
                            for c in range(KC):
                                last = pe.matmul(pair(s)[:, a:b], w1[:, c, s], xm[:, s % 2, c, a:b], start=c == 0, stop=c == KC - 1)
                        last.then_inc(sem("xm_used"), 1)
                        pe.drain().then_inc(sem("lora_ready"), 1)
                    pe.wait_ge(sem("wu_in"), 16).then_inc(sem("wu_in"), -16)
                    for m in range(2):
                        pe.wait_ge(sem("lora_read"), 1).then_inc(sem("lora_read"), -1)
                        for a, b in ((0, NS), (NS, T)):
                            for c in range(KC):
                                last = pe.matmul(pair(m)[:, a:b], wu[:, c, m * P:(m + 1) * P], h[:, c, a:b], start=c == 0, stop=c == KC - 1)
                        last.then_inc(sem("u_ready"), 1)
                    pe.wait_ge(sem("u_sbuf"), 1).then_inc(sem("u_sbuf"), -1)
                    pe.wait_ge(sem("lora_read"), 1).then_inc(sem("lora_read"), -1)
                    for tt in range(NT):
                        b = 4 + tt % 2
                        if tt >= 2:
                            pe.wait_ge(sem("utok_copied"), 1).then_inc(sem("utok_copied"), -1)
                        for m in range(2):
                            last = pe.matmul(ps[:, b, m * 256:(m + 1) * 256], ufeat[:, m, tt * P:(tt + 1) * P], dft64, start=True, stop=True)
                        last.then_inc(sem("utok_ready"), 1)
                    pe.wait_ge(sem("utok_copied"), 2).then_inc(sem("utok_copied"), -2)
                    pe.wait_ge(sem("dft_in"), 32).then_inc(sem("dft_in"), -32)
                    for m in range(2):
                        for tt in range(ST):
                            for k in range(2):
                                pe.matmul(pair(m)[:, 0:NS], utok[:, tt, m, k], dfs[:, tt, k], start=tt + k == 0, stop=(tt, k) == (ST - 1, 1))
                        for k in range(2):
                            last = pe.matmul(pair(m)[:, NS:T], utok[:, ST, m, k], dfp[:, k], start=k == 0, stop=k == 1)
                        last.then_inc(sem("fourier_ready"), 1)

                @block.scalar
                def _(act):
                    for s in range(3):
                        act.wait_ge(sem("lora_ready"), 1).then_inc(sem("lora_ready"), -1)
                        act.activation(lora[:, s], pair(s), ACT.Copy if s == 1 else ACT.Tanh, scale=(1.0, 1.0, 0.5)[s]).then_inc(act_done, 1)
                        act.wait_ge(act_done, 1).then_inc(act_done, -1)
                        act.sem_inc(sem("lora_read"), 1)
                    act.sem_inc(sem("half_sigmoid"), 1)
                    for m in range(2):
                        act.wait_ge(sem("u_ready"), 1).then_inc(sem("u_ready"), -1)
                        act.activation(ufeat[:, m], pair(m), ACT.Copy).then_inc(act_done, 1)
                    act.wait_ge(act_done, 2).then_inc(act_done, -2)
                    act.sem_inc(sem("u_sbuf"), 1)
                    for tt in range(NT):
                        act.wait_ge(sem("utok_ready"), 1).then_inc(sem("utok_ready"), -1)
                        act.activation(utok[:, tt].rearrange("p m k n -> p (m k n)"), ps[:, 4 + tt % 2], ACT.Copy).then_inc(act_done, 1)
                        act.wait_ge(act_done, 1).then_inc(act_done, -1)
                        act.sem_inc(sem("utok_copied"), 1)
                    for m in range(2):
                        act.wait_ge(sem("fourier_ready"), 1).then_inc(sem("fourier_ready"), -1)
                        act.activation(mix[:, HP + m], pair(m), ACT.Copy).then_inc(act_done, 1)
                    act.wait_ge(act_done, 2).then_inc(act_done, -2)

        def even_heads():
            mix, lora, wk = work["mix"], work["lora"], work["area"]
            ca = Carve()
            mat = ca(NT, 2, 2, 4, P)
            inv = ca(NT, 4, P)
            invT = ca(NT, 4, P)
            end = ca.at
            ct = Carve()
            raw = ct(3, T)
            shf = ct(3, T)
            rkv = ct(3, T)
            icl = ct(2, T)
            lw = ct(2, T)
            cum = ct(NT, P)
            rel = ct(2, NT, P + 1)
            kq = ct(T)
            sq = ct(T)
            kk = ct(T)
            eP = ct(2, NT, P + 1)
            eN = ct(2, NT, P + 1)
            assert ct.at <= end, (ct.at, end)
            cg = Carve(end - NT * 4 * P)
            ysb = cg(T)
            yc = cg(T)
            root = cg(T)
            ysq = cg(T)
            cb = Carve(end)
            win = cb(KC, 3, P)
            w2 = cb(3, P)
            hpv = cb(NHPV)
            hv = cb(NHPV + 5)
            muv = cb(4)
            ar = cb(2, NT, 2, P)
            nb = cb(2, NT, P)
            kp = cb(2, NT, P)
            yw = wk[:, cb.at - 2 * T * 2:cb.at].rearrange("p (g u n) -> p g u n", g=NT, u=4)
            tokm = cb(NT, 4, P)
            vtok = cb(NT, P)
            s0 = cb(2, NT, HD)
            us = cb(2, NT, P)
            rs = cb(4, P)
            bon = cb(T)
            gate = cb(T)
            ec = cb(2, NT)
            ctr = cb(NT)
            stin = cb(2, HD)
            sout = cb(2, HD)
            stmp = cb(4, HD)
            headones = C("headones")
            tri = C("tri").rearrange("p (z n) -> p z n", z=2)
            lv = work["m8"]

            steps = [[(0, j), (1, ST - 1 - j)] + ([(0, ST), (1, ST)] if j == 0 else []) for j in range(ST)]

            with stage() as block:
                @block.sync
                def _(sp):
                    wv = t["ev_w_in"][:, 0:2304].rearrange("(c p) (s q n) -> q s p c n", p=P, s=3, q=HP)
                    w2v = t["lora2"].rearrange("s p (q n) -> q p s n", q=HP)
                    stv = t["state"].rearrange("z q p v -> q p z v")
                    outv = t["st_out"].rearrange("z q p v -> q p z v")

                    def load_vectors(i):
                        sp.dma_start(hpv, t["hpv"][bass.ds(i, 1)].rearrange("a p n -> p (a n)")).then_inc(sem("hpv_in"), 16)

                    def load_weights(i):
                        for s in range(3):
                            sp.dma_start(win[:, :, s], wv[bass.ds(i, 1), s].rearrange("a p c n -> p (a c) n")).then_inc(sem("win_in"), 16)
                        sp.dma_start(w2, w2v[bass.ds(i, 1)].rearrange("a p s n -> p (a s) n")).then_inc(sem("win_in"), 16)

                    def load_state(i):
                        sp.dma_start(stin, stv[bass.ds(i, 1)].rearrange("a p z v -> p (a z) v")).then_inc(sem("state_in"), 16)

                    load_vectors(0)
                    load_weights(0)
                    load_state(0)
                    sp.sem_inc(sem("sout_free"), 1)
                    with sp.Fori(0, HP - 1) as i:
                        sp.wait_ge(sem("hpv_free"), 1).then_inc(sem("hpv_free"), -1)
                        load_vectors(i + 1)
                        sp.wait_ge(sem("win_free"), 1).then_inc(sem("win_free"), -1)
                        load_weights(i + 1)
                        sp.wait_ge(sem("state_free"), 1).then_inc(sem("state_free"), -1)
                        load_state(i + 1)
                        sp.wait_ge(sem("sout_ready"), 1).then_inc(sem("sout_ready"), -1)
                        sp.dma_start(outv[bass.ds(i, 1)].rearrange("a p z v -> p (a z) v"), sout).then_inc(sem("state_out"), 16)
                        sp.wait_ge(sem("state_out"), 16).then_inc(sem("state_out"), -16)
                        sp.sem_inc(sem("sout_free"), 1)
                    sp.wait_ge(sem("hpv_free"), 1).then_inc(sem("hpv_free"), -1)
                    sp.wait_ge(sem("win_free"), 1).then_inc(sem("win_free"), -1)
                    sp.wait_ge(sem("state_free"), 1).then_inc(sem("state_free"), -1)
                    sp.wait_ge(sem("sout_ready"), 1).then_inc(sem("sout_ready"), -1)
                    sp.dma_start(outv[HP - 1], sout).then_inc(sem("state_out"), 16)
                    sp.wait_ge(sem("state_out"), 16).then_inc(sem("state_out"), -16)

                @block.tensor
                def _(pe):
                    def project(s, c):
                        for a, b in ((0, NS), (NS, T)):
                            last = pe.matmul(pair(s % 2)[:, a:b], win[:, c, s], h[:, c, a:b], start=c == 0, stop=c == KC - 1)
                        if c == KC - 1:
                            pe.drain().then_inc(sem("proj_ready"), 1)

                    def heads(following):
                        ahead = [(s, c) for s in range(2) for c in range(KC)] if following else []

                        def fill_in(n):
                            for _ in range(min(n, len(ahead))):
                                project(*ahead.pop(0))

                        for n, (q, s, z) in enumerate(((1, 0, 0), (2, 0, 1), (3, 1, 0), (0, 1, 1), (1, 2, None))):
                            if n in (0, 2, 4):
                                pe.wait_ge(sem("proj_read"), 1).then_inc(sem("proj_read"), -1)
                            lo, hi = (0, P) if z is None else (z * HD, z * HD + HD)
                            for a, b in ((0, NS), (NS, T)):
                                last = pe.matmul(pair(q)[:, a:b], w2[lo:hi, s], lora[lo:hi, s, a:b], start=True, stop=True)
                            last.then_inc(sem("proj_ready"), 1)
                        pe.drain().then_inc(sem("win_free"), 1)
                        pe.wait_ge(sem("proj_read"), 2).then_inc(sem("proj_read"), -2)
                        pe.wait_ge(sem("sq_ready"), 1).then_inc(sem("sq_ready"), -1)
                        for a, b in ((0, NS), (NS, T)):
                            last = pe.matmul(pair(2)[:, a:b], headones, sq[:, a:b], start=True, stop=True)
                        last.then_inc(sem("knorm_ready"), 1)
                        pe.wait_ge(sem("bonus_in"), 1).then_inc(sem("bonus_in"), -1)
                        for a, b in ((0, NS), (NS, T)):
                            last = pe.matmul(pair(3)[:, a:b], headones, shf[:, 0, a:b], start=True, stop=True)
                        last.then_inc(sem("bonus_sum"), 1)
                        pe.wait_ge(sem("knorm_read"), 1).then_inc(sem("knorm_read"), -1)
                        pe.wait_ge(sem("bonus_read"), 1).then_inc(sem("bonus_read"), -1)
                        pe.wait_ge(sem("proj_read"), 2).then_inc(sem("proj_read"), -2)
                        pe.wait_ge(sem("feat_ready"), 2).then_inc(sem("feat_ready"), -2)
                        for tt in range(NT):
                            if tt >= 2:
                                pe.wait_ge(sem("tok_copied"), 1).then_inc(sem("tok_copied"), -1)
                            for z in range(2):
                                pe.transpose(ps[:, tt % 2, z * P:(z + 1) * P], nb[:, z, tt], ident)
                                last = pe.transpose(ps[:, tt % 2, (2 + z) * P:(3 + z) * P], kp[:, z, tt], ident)
                            last.then_inc(sem("tok_ready"), 1)
                        for tt in range(NT):
                            last = pe.transpose(pair(1)[:, tt * P:(tt + 1) * P], rkv[:, 2, tt * P:(tt + 1) * P], ident)
                        last.then_inc(sem("vtok_ready"), 1)
                        n = 0
                        for tt in range(NT):
                            for z in range(2):
                                for hh in range(2):
                                    lo, hi = hh * HD, hh * HD + HD
                                    if n >= 4:
                                        pe.wait_ge(sem("mat_read"), 1).then_inc(sem("mat_read"), -1)
                                    pe.matmul(ps[:, 4 + n % 4, 0:256], nb[lo:hi, z, tt], ar[lo:hi, z, tt], start=True, stop=True)
                                    pe.matmul(ps[:, 4 + n % 4, 256:512], kp[lo:hi, z, tt], ar[lo:hi, z, tt], start=True, stop=True)\
                                        .then_inc(sem("mat_ready"), 1)
                                    n += 1
                        pe.wait_ge(sem("mat_read"), 4).then_inc(sem("mat_read"), -4)
                        pe.wait_ge(sem("tok_copied"), 2).then_inc(sem("tok_copied"), -2)
                        pe.wait_ge(sem("vtok_copied"), 1).then_inc(sem("vtok_copied"), -1)
                        pe.wait_ge(sem("inv_start"), 1).then_inc(sem("inv_start"), -1)
                        for lev in range(LEVELS):
                            for g in range(NT):
                                pe.wait_ge(sem("invT_ready"), 1).then_inc(sem("invT_ready"), -1)
                                if g >= 2:
                                    pe.wait_ge(sem("inv_copied"), 1).then_inc(sem("inv_copied"), -1)
                                for u in range(4):
                                    last = pe.transpose(ps[:, g % 2, u * P:(u + 1) * P], invT[:, g, u], ident)
                                last.then_inc(sem("inv_ready"), 1)
                            for g in range(NT):
                                if g >= 2:
                                    pe.wait_ge(sem("yw_copied"), 1).then_inc(sem("yw_copied"), -1)
                                pe.wait_ge(sem("inv_copied_n"), 1).then_inc(sem("inv_copied_n"), -1)
                                for u in range(4):
                                    last = pe.matmul(ps[:, 2 + g % 2, u * P:(u + 1) * P], mat[:, g, u // 2, u % 2, 0], inv[:, g, u], start=True, stop=True)
                                last.then_inc(sem("yw_ready"), 1)
                            pe.wait_ge(sem("inv_copied"), 2).then_inc(sem("inv_copied"), -2)
                            for g in range(NT):
                                pe.wait_ge(sem("yw_copied_n"), 1).then_inc(sem("yw_copied_n"), -1)
                                if g >= 2:
                                    pe.wait_ge(sem("invT_read"), 1).then_inc(sem("invT_read"), -1)
                                for u in range(4):
                                    last = pe.matmul(ps[:, 4 + g % 2, u * P:(u + 1) * P], yw[:, g, u], invT[:, g, u], start=True, stop=True)
                                last.then_inc(sem("z_ready"), 1)
                            pe.wait_ge(sem("yw_copied"), 2).then_inc(sem("yw_copied"), -2)
                            pe.wait_ge(sem("invT_read"), 2).then_inc(sem("invT_read"), -2)
                        pe.wait_ge(sem("invT_ready"), NT).then_inc(sem("invT_ready"), -NT)
                        if following:
                            pe.wait_ge(sem("win_in"), 64).then_inc(sem("win_in"), -64)
                        for j, cells in enumerate(steps):
                            pe.wait_ge(sem("s0_ready"), 1).then_inc(sem("s0_ready"), -1)
                            for q, (z, tt) in enumerate(cells):
                                for hh in range(2):
                                    lo, hi = hh * HD, hh * HD + HD
                                    o = ps[:, 6 - hh, q * HD:(q + 1) * HD]
                                    pe.matmul(o, ar[lo:hi, z, tt, 0], s0[lo:hi, z, tt], start=True, stop=False)
                                    last = pe.matmul(o, mat[:, tt, z, hh, 2], vtok[:, tt, lo:hi], start=False, stop=True)
                            last.then_inc(sem("r_ready"), 1)
                            fill_in(1)
                            pe.wait_ge(sem("r_copied"), 1).then_inc(sem("r_copied"), -1)
                            for q, (z, tt) in enumerate(cells):
                                for hh in range(2):
                                    lo, hi = hh * HD, hh * HD + HD
                                    last = pe.matmul(ps[:, 7, q * P + lo:q * P + hi], invT[:, tt, z * 2 + hh], rs[:, q, lo:hi], start=True, stop=True)
                            last.then_inc(sem("u_ready"), 1)
                            fill_in(1 if j < ST - 1 else 2 * KC)
                            pe.wait_ge(sem("u_copied"), 1).then_inc(sem("u_copied"), -1)
                            if j == ST - 1:
                                break
                            for q, (z, tt) in enumerate(cells):
                                for hh in range(2):
                                    lo, hi = hh * HD, hh * HD + HD
                                    o = ps[lo:hi, 4, q * HD:(q + 1) * HD]
                                    pe.matmul(o, tokm[:, tt, 2 + z, lo:hi], vtok[:, tt, lo:hi], start=True, stop=False)
                                    last = pe.matmul(o, tokm[:, tt, z, lo:hi], us[:, z, tt, lo:hi], start=False, stop=True)
                            last.then_inc(sem("s_ready"), 1)
                            fill_in(2)
                        for tt in range(NT):
                            for hh in range(2):
                                lo, hi = hh * HD, hh * HD + HD
                                o = pair(3)[lo:hi, tt * P:(tt + 1) * P]
                                for z in range(2):
                                    pe.matmul(o, s0[lo:hi, z, tt], ar[lo:hi, z, tt, 1], start=z == 0, stop=False)
                                for z in range(2):
                                    pe.matmul(o, us[:, z, tt, lo:hi], mat[:, tt, z, hh, 1], start=False, stop=False)
                                    last = pe.matmul(o, vtok[:, tt, lo:hi], mat[:, tt, z, hh, 3], start=False, stop=z == 1)
                        last.then_inc(sem("y_ready"), 1)
                        for src, q, s in ((ysb, 2, "y_sbuf"), (ysq, 3, "ysq_ready")):
                            pe.wait_ge(sem(s), 1).then_inc(sem(s), -1)
                            for a, b in ((0, NS), (NS, T)):
                                last = pe.matmul(pair(q)[:, a:b], headones, src[:, a:b], start=True, stop=True)
                            last.then_inc(sem("ymean_ready" if q == 2 else "yvar_ready"), 1)
                            if following and q == 2:
                                pe.wait_ge(sem("proj_read"), 1).then_inc(sem("proj_read"), -1)
                                for c in range(KC):
                                    project(2, c)

                    pe.wait_ge(sem("win_in"), 64).then_inc(sem("win_in"), -64)
                    for s in range(3):
                        if s == 2:
                            pe.wait_ge(sem("proj_read"), 1).then_inc(sem("proj_read"), -1)
                        for c in range(KC):
                            project(s, c)
                    with pe.Fori(0, HP - 1) as i:
                        heads(True)
                    heads(False)

                @block.scalar
                def _(act):
                    def copy_raw(s):
                        act.wait_ge(sem("proj_ready"), 1).then_inc(sem("proj_ready"), -1)
                        act.activation(raw[:, s], pair(s % 2), ACT.Copy).then_inc(act_done, 1)
                        act.wait_ge(act_done, 1).then_inc(act_done, -1)
                        act.sem_inc(sem("raw_ready"), 1)
                        act.sem_inc(sem("proj_read"), 1)

                    def heads(following):
                        act.wait_ge(sem("hv_act"), 1).then_inc(sem("hv_act"), -1)
                        for n, (q, out, b) in enumerate(((1, lw[:, 0], 12), (2, lw[:, 1], 13), (3, icl[:, 0], 14), (0, icl[:, 1], 15))):
                            act.wait_ge(sem("proj_ready"), 1).then_inc(sem("proj_ready"), -1)
                            act.activation(out, pair(q), ACT.Tanh, scale=0.5, bias=hv[:, b:b + 1]).then_inc(act_done, 1)
                            act.wait_ge(act_done, 1).then_inc(act_done, -1)
                            act.sem_inc(sem("proj_read"), 1)
                            act.sem_inc(sem("lw_ready" if n < 2 else "icl_ready"), 1)
                        act.wait_ge(sem("proj_ready"), 1).then_inc(sem("proj_ready"), -1)
                        act.activation(gate, pair(1), ACT.Copy).then_inc(act_done, 1)
                        act.wait_ge(act_done, 1).then_inc(act_done, -1)
                        act.sem_inc(sem("proj_read"), 1)
                        act.wait_ge(sem("k_ready"), 1).then_inc(sem("k_ready"), -1)
                        act.mul(kq, rkv[:, 1], hv[:, HPV["k_k"]:HPV["k_k"] + 1]).then_inc(act_done, 1)
                        act.activation(sq, rkv[:, 1], ACT.Square, scale=hv[:, HPV["k_k"]:HPV["k_k"] + 1]).then_inc(act_done, 1)
                        act.wait_ge(act_done, 2).then_inc(act_done, -2)
                        act.sem_inc(sem("sq_ready"), 1)
                        act.wait_ge(sem("knorm_ready"), 1).then_inc(sem("knorm_ready"), -1)
                        act.activation(kk, pair(2), ACT.Sqrt).then_inc(act_done, 1)
                        act.wait_ge(act_done, 1).then_inc(act_done, -1)
                        act.sem_inc(sem("knorm_read"), 1)
                        act.sem_inc(sem("knorm_root"), 1)
                        for z in range(2):
                            act.wait_ge(sem("rel_ready"), 1).then_inc(sem("rel_ready"), -1)
                            act.activation(eP[:, z], rel[:, z], ACT.Exp).then_inc(act_done, 1)
                            act.activation(eN[:, z], rel[:, z], ACT.Exp, scale=-1.0).then_inc(act_done, 1)
                            act.wait_ge(act_done, 2).then_inc(act_done, -2)
                            act.sem_inc(sem("exp_ready"), 1)
                        for tt in range(NT):
                            act.wait_ge(sem("tok_ready"), 1).then_inc(sem("tok_ready"), -1)
                            act.activation(tokm[:, tt].rearrange("p u n -> p (u n)"), ps[:, tt % 2], ACT.Copy).then_inc(act_done, 1)
                            act.wait_ge(act_done, 1).then_inc(act_done, -1)
                            act.sem_inc(sem("tok_copied"), 1)
                        act.wait_ge(sem("vtok_ready"), 1).then_inc(sem("vtok_ready"), -1)
                        act.activation(vtok.rearrange("p t n -> p (t n)"), pair(1), ACT.Copy).then_inc(act_done, 1)
                        act.wait_ge(act_done, 1).then_inc(act_done, -1)
                        act.sem_inc(sem("vtok_copied"), 1)
                        for lev in range(LEVELS):
                            for g in range(NT):
                                act.wait_ge(sem("inv_ready"), 1).then_inc(sem("inv_ready"), -1)
                                act.activation(inv[:, g].rearrange("p u n -> p (u n)"), ps[:, g % 2], ACT.Copy).then_inc(act_done, 1)
                                act.wait_ge(act_done, 1).then_inc(act_done, -1)
                                act.sem_inc(sem("inv_copied"), 1)
                                act.sem_inc(sem("inv_copied_n"), 1)
                            for g in range(NT):
                                act.wait_ge(sem("yw_ready"), 1).then_inc(sem("yw_ready"), -1)
                                act.activation(yw[:, g].rearrange("p u n -> p (u n)"), ps[:, 2 + g % 2], ACT.Copy).then_inc(act_done, 1)
                                act.wait_ge(act_done, 1).then_inc(act_done, -1)
                                act.sem_inc(sem("yw_copied"), 1)
                                act.sem_inc(sem("yw_copied_n"), 1)
                        for j, cells in enumerate(steps):
                            act.wait_ge(sem("r_ready"), 1).then_inc(sem("r_ready"), -1)
                            n = len(cells)
                            for hh in range(2):
                                act.activation(rs[:, 0:n, hh * HD:(hh + 1) * HD], ps[:, 6 - hh, 0:n * HD].rearrange("p (u n) -> p u n", u=n), ACT.Copy).then_inc(act_done, 1)
                            act.wait_ge(act_done, 2).then_inc(act_done, -2)
                            act.sem_inc(sem("r_copied"), 1)
                            act.wait_ge(sem("u_ready"), 1).then_inc(sem("u_ready"), -1)
                            for q, (z, tt) in enumerate(cells):
                                act.activation(us[:, z, tt], ps[:, 7, q * P:(q + 1) * P], ACT.Copy).then_inc(act_done, 1)
                            act.wait_ge(act_done, len(cells)).then_inc(act_done, -(len(cells)))
                            act.sem_inc(sem("u_copied"), 1)
                        act.wait_ge(sem("y_ready"), 1).then_inc(sem("y_ready"), -1)
                        act.activation(ysb, pair(3), ACT.Copy).then_inc(act_done, 1)
                        act.wait_ge(act_done, 1).then_inc(act_done, -1)
                        act.sem_inc(sem("y_sbuf"), 1)
                        act.sem_inc(sem("y_sbuf_v"), 1)
                        if following:
                            copy_raw(0)
                            copy_raw(1)
                        act.wait_ge(sem("yc_ready"), 1).then_inc(sem("yc_ready"), -1)
                        act.activation(ysq, yc, ACT.Square).then_inc(act_done, 1)
                        act.wait_ge(act_done, 1).then_inc(act_done, -1)
                        act.sem_inc(sem("ysq_ready"), 1)
                        act.wait_ge(sem("yvar_ready"), 1).then_inc(sem("yvar_ready"), -1)
                        act.activation(root, pair(3), ACT.Sqrt, scale=1.0 / HD, bias=eps[:, 2:3]).then_inc(act_done, 1)
                        act.wait_ge(act_done, 1).then_inc(act_done, -1)
                        act.sem_inc(sem("yroot_ready"), 1)
                        if following:
                            copy_raw(2)

                    for s in range(3):
                        copy_raw(s)
                    with act.Fori(0, HP - 1) as i:
                        heads(True)
                    heads(False)

                @block.gpsimd
                def _(pool):
                    with pool.Fori(0, HP) as i:
                        for s in range(3):
                            pool.wait_ge(sem("raw_ready"), 1).then_inc(sem("raw_ready"), -1)
                            pool.tensor_tensor(shf[:, s, 1:T - 1], raw[:, s, 0:T - 2], raw[:, s, 2:T], ALU.add).then_inc(pool_done, 1)
                            pool.wait_ge(pool_done, 1).then_inc(pool_done, -1)
                            pool.tensor_copy(shf[:, s, 0:NS + 1:NS], raw[:, s, 1:NS + 2:NS]).then_inc(pool_done, 1)
                            pool.tensor_copy(shf[:, s, NS - 1:T:NP], raw[:, s, NS - 2:T - 1:NP]).then_inc(pool_done, 1)
                            pool.wait_ge(pool_done, 2).then_inc(pool_done, -2)
                            pool.sem_inc(sem("shf_ready"), 1)

                @block.vector
                def _(dve):
                    def col(name, k=0):
                        n = HPV[name] + k
                        return hv[:, n:n + 1]

                    def shift(s):
                        dve.wait_ge(sem("shf_ready"), 1).then_inc(sem("shf_ready"), -1)
                        dve.scalar_tensor_tensor(shf[:, s], shf[:, s], 0.5, raw[:, s], ALU.mult, ALU.subtract).then_inc(dve_done, 1)
                        dve.wait_ge(dve_done, 1).then_inc(dve_done, -1)
                        dve.scalar_tensor_tensor(rkv[:, s], shf[:, s], muv[:, s:s + 1], raw[:, s], ALU.mult, ALU.add).then_inc(dve_done, 1)
                        dve.wait_ge(dve_done, 1).then_inc(dve_done, -1)

                    def shift_rk():
                        dve.wait_ge(sem("hpv_in"), 16).then_inc(sem("hpv_in"), -16)
                        dve.tensor_copy(muv[:, 0:3], hpv[:, HPV["mu"]:HPV["mu"] + 3]).then_inc(dve_done, 1)
                        dve.tensor_copy(muv[:, 3:4], hpv[:, HPV["r_k"]:HPV["r_k"] + 1]).then_inc(dve_done, 1)
                        dve.wait_ge(dve_done, 2).then_inc(dve_done, -2)
                        shift(0)
                        shift(1)
                        dve.sem_inc(sem("k_ready"), 1)
                        dve.scalar_tensor_tensor(shf[:, 0], rkv[:, 0], muv[:, 3:4], rkv[:, 1], ALU.mult, ALU.mult).then_inc(dve_done, 1)
                        dve.wait_ge(dve_done, 1).then_inc(dve_done, -1)
                        dve.sem_inc(sem("bonus_in"), 1)

                    def heads(i, following):
                        dve.tensor_copy(hv[:, 0:NHPV], hpv).then_inc(dve_done, 1)
                        dve.tensor_scalar(hv[:, 12:16], hpv[:, 3:7], 0.5, None, ALU.mult).then_inc(dve_done, 1)
                        dve.tensor_scalar(hv[:, 16:17], hpv[:, 8:9], -1.0, 1.0, ALU.mult, ALU.add).then_inc(dve_done, 1)
                        dve.wait_ge(dve_done, 3).then_inc(dve_done, -3)
                        dve.sem_inc(sem("hv_act"), 1)
                        dve.sem_inc(sem("hpv_free"), 1)
                        shift(2)
                        for z in range(2):
                            dve.wait_ge(sem("lw_ready"), 1).then_inc(sem("lw_ready"), -1)
                            dve.tensor_scalar(lw[:, z], lw[:, z], -EXPH / 2, -EXPH / 2, ALU.mult, ALU.add).then_inc(dve_done, 1)
                            dve.wait_ge(dve_done, 1).then_inc(dve_done, -1)
                            for tt in range(NT):
                                dve.tensor_tensor_scan(cum[:, tt], ones[:, :], lw[:, z, tt * P:(tt + 1) * P], 0.0, ALU.mult, ALU.add).then_inc(dve_done, 1)
                            dve.wait_ge(dve_done, 5).then_inc(dve_done, -5)
                            dve.tensor_scalar(ctr, cum[:, :, P - 1], 0.5, None, ALU.mult).then_inc(dve_done, 1)
                            dve.wait_ge(dve_done, 1).then_inc(dve_done, -1)
                            dve.tensor_tensor(rel[:, z, :, 1:P + 1], cum, bcast(ctr, 2, P), ALU.subtract).then_inc(dve_done, 1)
                            dve.tensor_scalar(rel[:, z, :, 0], ctr, -1.0, None, ALU.mult).then_inc(dve_done, 1)
                            dve.wait_ge(dve_done, 2).then_inc(dve_done, -2)
                            dve.sem_inc(sem("rel_ready"), 1)
                        dve.wait_ge(sem("knorm_root"), 1).then_inc(sem("knorm_root"), -1)
                        dve.tensor_scalar(kk, kk, 1e-12, None, ALU.max).then_inc(dve_done, 1)
                        dve.wait_ge(dve_done, 1).then_inc(dve_done, -1)
                        dve.reciprocal(kk, kk).then_inc(dve_done, 1)
                        dve.wait_ge(dve_done, 1).then_inc(dve_done, -1)
                        dve.tensor_tensor(kk, kk, kq, ALU.mult).then_inc(dve_done, 1)
                        dve.wait_ge(dve_done, 1).then_inc(dve_done, -1)
                        dve.wait_ge(sem("bonus_sum"), 1).then_inc(sem("bonus_sum"), -1)
                        dve.tensor_tensor(bon, pair(3), rkv[:, 2], ALU.mult).then_inc(dve_done, 1)
                        dve.wait_ge(dve_done, 1).then_inc(dve_done, -1)
                        dve.sem_inc(sem("bonus_read"), 1)
                        kk3 = kk.rearrange("p (t n) -> p t n", t=NT)
                        r3 = rkv[:, 0].rearrange("p (t n) -> p t n", t=NT)
                        for z in range(2):
                            dve.wait_ge(sem("icl_ready"), 1).then_inc(sem("icl_ready"), -1)
                            dve.tensor_scalar(icl[:, z], icl[:, z], 0.5, 0.5, ALU.mult, ALU.add).then_inc(dve_done, 1)
                            dve.wait_ge(dve_done, 1).then_inc(dve_done, -1)
                            dve.tensor_scalar(lw[:, z], icl[:, z], col("k_a"), hv[:, 16:17], ALU.mult, ALU.add).then_inc(dve_done, 1)
                            dve.wait_ge(dve_done, 1).then_inc(dve_done, -1)
                            dve.tensor_tensor(lw[:, z], lw[:, z], rkv[:, 1], ALU.mult).then_inc(dve_done, 1)
                            dve.scalar_tensor_tensor(icl[:, z], icl[:, z], -1.0, kk, ALU.mult, ALU.mult).then_inc(dve_done, 1)
                            dve.wait_ge(dve_done, 2).then_inc(dve_done, -2)
                            k3 = lw[:, z].rearrange("p (t n) -> p t n", t=NT)
                            b3 = icl[:, z].rearrange("p (t n) -> p t n", t=NT)
                            dve.wait_ge(sem("exp_ready"), 1).then_inc(sem("exp_ready"), -1)
                            inc, exc = slice(1, P + 1), slice(0, P)
                            if z == 0:
                                fr, fa, fb = eP[:, z, :, inc], eP[:, z, :, exc], eN[:, z, :, inc]
                            else:
                                fr, fa, fb = eN[:, z, :, exc], eN[:, z, :, inc], eP[:, z, :, exc]
                            dve.tensor_tensor(ar[:, z, :, 0], kk3, fa, ALU.mult).then_inc(dve_done, 1)
                            dve.tensor_tensor(ar[:, z, :, 1], r3, fr, ALU.mult).then_inc(dve_done, 1)
                            dve.tensor_tensor(nb[:, z], b3, fb, ALU.mult).then_inc(dve_done, 1)
                            dve.tensor_tensor(kp[:, z], k3, fb, ALU.mult).then_inc(dve_done, 1)
                            dve.tensor_copy(ec[:, z], eN[:, z, :, 0]).then_inc(dve_done, 1)
                            dve.wait_ge(dve_done, 5).then_inc(dve_done, -5)
                            dve.sem_inc(sem("feat_ready"), 1)
                        n = 0
                        for tt in range(NT):
                            for z in range(2):
                                for hh in range(2):
                                    dve.wait_ge(sem("mat_ready"), 1).then_inc(sem("mat_ready"), -1)
                                    dve.tensor_tensor(mat[:, tt, z, hh].rearrange("p k n -> p (k n)"), ps[:, 4 + n % 4], tri[:, z], ALU.mult).then_inc(dve_done, 1)
                                    dve.wait_ge(dve_done, 1).then_inc(dve_done, -1)
                                    dve.sem_inc(sem("mat_read"), 1)
                                    n += 1
                        dve.tensor_copy(invT, bcast(bcast(ident, 1, 4), 1, NT)).then_inc(dve_done, 1)
                        dve.wait_ge(dve_done, 1).then_inc(dve_done, -1)
                        for g in range(NT):
                            for z in range(2):
                                dve.copy_predicated(invT[:, g, 2 * z:2 * z + 2], bcast(lv[:, 0, z], 1, 2), mat[:, g, z, :, 0]).then_inc(dve_done, 1)
                        dve.wait_ge(dve_done, 10).then_inc(dve_done, -10)
                        dve.sem_inc(sem("inv_start"), 1)
                        dve.sem_inc(sem("invT_ready"), NT)
                        dve.wait_ge(sem("state_in"), 16).then_inc(sem("state_in"), -16)
                        dve.tensor_scalar(s0[:, 0, 0], stin[:, 0], ec[:, 0, 0:1], None, ALU.mult).then_inc(dve_done, 1)
                        dve.tensor_scalar(s0[:, 1, ST - 1], stin[:, 1], ec[:, 1, ST - 1:ST], None, ALU.mult).then_inc(dve_done, 1)
                        dve.memset(s0[:, :, ST], 0.0).then_inc(dve_done, 1)
                        dve.wait_ge(dve_done, 3).then_inc(dve_done, -3)
                        dve.sem_inc(sem("s0_ready"), 1)
                        dve.sem_inc(sem("state_free"), 1)
                        for lev in range(LEVELS):
                            for g in range(NT):
                                dve.wait_ge(sem("z_ready"), 1).then_inc(sem("z_ready"), -1)
                                for z in range(2):
                                    dve.copy_predicated(invT[:, g, 2 * z:2 * z + 2], bcast(lv[:, 1 + lev, z], 1, 2),
                                                           ps[:, 4 + g % 2, 2 * z * P:(2 * z + 2) * P].rearrange("p (u n) -> p u n", u=2)).then_inc(dve_done, 1)
                                dve.wait_ge(dve_done, 2).then_inc(dve_done, -2)
                                dve.sem_inc(sem("invT_read"), 1)
                                dve.sem_inc(sem("invT_ready"), 1)
                        for j, cells in enumerate(steps[:ST - 1]):
                            dve.wait_ge(sem("s_ready"), 1).then_inc(sem("s_ready"), -1)
                            if j == 0:
                                dve.wait_ge(sem("sout_free"), 1).then_inc(sem("sout_free"), -1)
                            for q, (z, tt) in enumerate(cells):
                                dve.tensor_tensor(stmp[:, q], ps[:, 4, q * HD:(q + 1) * HD], s0[:, z, tt], ALU.add).then_inc(dve_done, 1)
                            dve.wait_ge(dve_done, len(cells)).then_inc(dve_done, -(len(cells)))
                            for q, (z, tt) in enumerate(cells):
                                if tt == ST:
                                    dve.tensor_scalar(sout[:, z], stmp[:, q], ec[:, z, tt:tt + 1], None, ALU.mult).then_inc(dve_done, 1)
                                else:
                                    nx = tt + 1 - 2 * z
                                    dve.tensor_scalar(s0[:, z, nx], stmp[:, q], ec[:, z, tt:tt + 1], ec[:, z, nx:nx + 1], ALU.mult, ALU.mult).then_inc(dve_done, 1)
                            dve.wait_ge(dve_done, len(cells)).then_inc(dve_done, -(len(cells)))
                            dve.sem_inc(sem("s0_ready"), 1)
                            if j == 0:
                                dve.sem_inc(sem("sout_ready"), 1)
                        dve.wait_ge(sem("y_sbuf_v"), 1).then_inc(sem("y_sbuf_v"), -1)
                        dve.wait_ge(sem("ymean_ready"), 1).then_inc(sem("ymean_ready"), -1)
                        dve.scalar_tensor_tensor(yc, pair(2), -1.0 / HD, ysb, ALU.mult, ALU.add).then_inc(dve_done, 1)
                        dve.wait_ge(dve_done, 1).then_inc(dve_done, -1)
                        dve.sem_inc(sem("yc_ready"), 1)
                        if following:
                            shift_rk()
                        dve.wait_ge(sem("yroot_ready"), 1).then_inc(sem("yroot_ready"), -1)
                        dve.reciprocal(root, root).then_inc(dve_done, 1)
                        dve.wait_ge(dve_done, 1).then_inc(dve_done, -1)
                        dve.tensor_tensor(yc, yc, root, ALU.mult).then_inc(dve_done, 1)
                        dve.wait_ge(dve_done, 1).then_inc(dve_done, -1)
                        dve.tensor_scalar(yc, yc, col("gn_w"), col("gn_b"), ALU.mult, ALU.add).then_inc(dve_done, 1)
                        dve.wait_ge(dve_done, 1).then_inc(dve_done, -1)
                        dve.tensor_tensor(yc, yc, bon, ALU.add).then_inc(dve_done, 1)
                        dve.wait_ge(dve_done, 1).then_inc(dve_done, -1)
                        dve.tensor_tensor(mix[:, bass.ds(i, 1)].rearrange("p a n -> p (a n)"), yc, gate, ALU.mult).then_inc(dve_done, 1)
                        dve.wait_ge(dve_done, 1).then_inc(dve_done, -1)

                    shift_rk()
                    with dve.Fori(0, HP - 1) as i:
                        heads(i, True)
                    heads(HP - 1, False)

        def out_proj(l, w):
            w_sb = Carve()(4, KC, 256)
            mix = work["mix"]

            with stage() as block:
                @block.sync
                def _(sp):
                    for q in range(4):
                        sp.dma_start(w_sb[:, q], w[:, q * 256:(q + 1) * 256].rearrange("(c p) n -> p c n", p=P)).then_inc(sem(f"wout{q}"), 16)

                @block.tensor
                def _(pe):
                    for m in range(KC):
                        if m % 2 == 0:
                            pe.wait_ge(sem(f"wout{m // 2}"), 16).then_inc(sem(f"wout{m // 2}"), -16)
                        if m >= 4:
                            pe.wait_ge(sem("out_read"), 1).then_inc(sem("out_read"), -1)
                        for a, b in ((0, NS), (NS, T)):
                            for c in range(KC):
                                last = pe.matmul(pair(m % 4)[:, a:b], w_sb[:, m // 2, c, m % 2 * P:(m % 2 + 1) * P], mix[:, c, a:b],
                                                start=c == 0, stop=c == KC - 1)
                        last.then_inc(sem("out_ready"), 1)
                    pe.wait_ge(sem("out_read"), 4).then_inc(sem("out_read"), -4)

                @block.vector
                def _(dve):
                    for m in range(KC):
                        dve.wait_ge(sem("out_ready"), 1).then_inc(sem("out_ready"), -1)
                        for r, a, b in SEGS:
                            dve.scalar_tensor_tensor(x[:, m, a:b], pair(m % 4)[:, a:b], mod[:, l, 2, m, r:r + 1], x[:, m, a:b], ALU.mult, ALU.add).then_inc(dve_done, 1)
                        dve.wait_ge(dve_done, 2).then_inc(dve_done, -2)
                        dve.sem_inc(sem("out_read"), 1)

        def route(l, prefetch):
            htok = work["htok"]
            cv = Carve()
            wr = cv(KC, E)
            br = cv(E, parts=1)
            lg = cv(NT, E)
            mx = cv(NT)
            left = cv(T, parts=E)
            pos = cv(T, parts=E)
            m8v = cv(8, parts=E)
            one16 = cv(T, parts=E)
            sl = cv(T, parts=E)

            with stage() as block:
                @block.sync
                def _(sp):
                    sp.dma_start(wr, t["router"][l].rearrange("(c p) n -> p c n", p=P)).then_inc(sem("wr_in"), 16)
                    sp.dma_start(br, t["router_b"][l:l + 1, :]).then_inc(sem("wr_in"), 16)
                    prefetch(sp)

                @block.tensor
                def _(pe):
                    pe.wait_ge(sem("wr_in"), 32).then_inc(sem("wr_in"), -32)
                    for tt in range(NT):
                        o = ps[:, 0, tt * E:(tt + 1) * E]
                        for c in range(KC):
                            pe.matmul(o, h[:, c, tt * P:(tt + 1) * P], wr[:, c], start=c == 0, stop=False)
                        last = pe.matmul(o, ones[0:1, :], br, start=False, stop=True)
                    last.then_inc(sem("logits_ready"), 1)
                    for n in range(10):
                        b = 2 + n % 4
                        if n >= 4:
                            pe.wait_ge(sem("htok_read"), 1).then_inc(sem("htok_read"), -1)
                        for k in range(4):
                            tt, c = n // 2, 4 * (n % 2) + k
                            last = pe.transpose(ps[:, b, k * P:(k + 1) * P], h[:, c, tt * P:(tt + 1) * P], ident)
                        last.then_inc(sem("htok_ready"), 1)
                    pe.wait_ge(sem("htok_read"), 4).then_inc(sem("htok_read"), -4)
                    pe.wait_ge(sem("aff_ready"), 1).then_inc(sem("aff_ready"), -1)
                    for tt in range(NT):
                        last = pe.transpose(pair(0)[0:E, tt * P:(tt + 1) * P], aff[:, tt, 0:E], ident)
                    last.then_inc(sem("affT_ready"), 1)
                    pe.wait_ge(sem("slots_ready"), 1).then_inc(sem("slots_ready"), -1)
                    for tt in range(NT):
                        last = pe.transpose(ps[:, 2, tt * E:(tt + 1) * E], sl[:, tt * P:(tt + 1) * P], ident[0:E, 0:E])
                    last.then_inc(sem("slotsT_ready"), 1)

                @block.scalar
                def _(act):
                    for n in range(10):
                        act.wait_ge(sem("htok_ready"), 1).then_inc(sem("htok_ready"), -1)
                        act.activation(htok[:, 0, n // 2, 512 * (n % 2):512 * (n % 2) + 512], ps[:, 2 + n % 4], ACT.Copy).then_inc(sem("htok_high"), 1)
                        if n == 1:
                            act.wait_ge(sem("lg_ready"), 1).then_inc(sem("lg_ready"), -1)
                            act.activation(aff[:, :, 0:E], lg, ACT.Exp).then_inc(sem("exp_done"), 1)

                @block.vector
                def _(dve):

                    def low(n):
                        dve.wait_ge(sem("htok_high"), 1).then_inc(sem("htok_high"), -1)
                        o = htok[:, :, n // 2, 512 * (n % 2):512 * (n % 2) + 512]
                        dve.tensor_tensor(o[:, 1], ps[:, 2 + n % 4], o[:, 0].bitcast(F32), ALU.subtract).then_inc(sem("htok_read"), 1)

                    dve.wait_ge(sem("logits_ready"), 1).then_inc(sem("logits_ready"), -1)
                    lp = ps[:, 0, 0:NT * E].rearrange("p (t e) -> p t e", t=NT)
                    dve.tensor_reduce(mx, lp, AX.X, ALU.max).then_inc(dve_done, 1)
                    dve.wait_ge(dve_done, 1).then_inc(dve_done, -1)
                    dve.tensor_tensor(lg, lp, bcast(mx, 2, E), ALU.subtract).then_inc(dve_done, 1)
                    dve.wait_ge(dve_done, 1).then_inc(dve_done, -1)
                    dve.sem_inc(sem("lg_ready"), 1)
                    low(0)
                    low(1)
                    dve.wait_ge(sem("exp_done"), 1).then_inc(sem("exp_done"), -1)
                    dve.tensor_reduce(mx, aff[:, :, 0:E], AX.X, ALU.add).then_inc(dve_done, 1)
                    dve.wait_ge(dve_done, 1).then_inc(dve_done, -1)
                    dve.reciprocal(mx, mx).then_inc(dve_done, 1)
                    dve.wait_ge(dve_done, 1).then_inc(dve_done, -1)
                    dve.tensor_tensor(aff[:, :, 0:E], aff[:, :, 0:E], bcast(mx, 2, E), ALU.mult).then_inc(dve_done, 1)
                    dve.wait_ge(dve_done, 1).then_inc(dve_done, -1)
                    dve.sem_inc(sem("aff_ready"), 1)
                    for n in range(2, 10):
                        low(n)
                    dve.memset(one16, 1.0).then_inc(dve_done, 1)
                    dve.wait_ge(dve_done, 1).then_inc(dve_done, -1)
                    dve.wait_ge(sem("affT_ready"), 1).then_inc(sem("affT_ready"), -1)
                    dve.tensor_copy(left, pair(0)[0:E, :]).then_inc(dve_done, 1)
                    dve.wait_ge(dve_done, 1).then_inc(dve_done, -1)
                    for a, b, cap in ((0, NS, CAPS), (NS, T, CAPP)):
                        for n in range(cap // 8):
                            dve.max(m8v, left[:, a:b]).then_inc(dve_done, 1)
                            dve.wait_ge(dve_done, 1).then_inc(dve_done, -1)
                            dve.match_replace(left[:, a:b], m8v, left[:, a:b], -1.0).then_inc(dve_done, 1)
                            dve.wait_ge(dve_done, 1).then_inc(dve_done, -1)
                    dve.tensor_scalar(left, left, 0.0, None, ALU.is_lt).then_inc(dve_done, 1)
                    dve.wait_ge(dve_done, 1).then_inc(dve_done, -1)
                    for a, b in ((0, NS), (NS, T)):
                        dve.tensor_tensor_scan(pos[:, a:b], one16[:, a:b], left[:, a:b], 0.0, ALU.mult, ALU.add).then_inc(dve_done, 1)
                    dve.wait_ge(dve_done, 2).then_inc(dve_done, -2)
                    dve.tensor_tensor(pos, pos, left, ALU.mult).then_inc(dve_done, 1)
                    dve.wait_ge(dve_done, 1).then_inc(dve_done, -1)
                    dve.tensor_scalar(sl, pos, -1.0, None, ALU.add).then_inc(dve_done, 1)
                    dve.wait_ge(dve_done, 1).then_inc(dve_done, -1)
                    dve.sem_inc(sem("slots_ready"), 1)
                    dve.wait_ge(sem("slotsT_ready"), 1).then_inc(sem("slotsT_ready"), -1)
                    dve.tensor_copy(slot[:, :, 0:E], ps[:, 2, 0:NT * E].rearrange("p (t e) -> p t e", t=NT)).then_inc(dve_done, 1)
                    dve.wait_ge(dve_done, 1).then_inc(dve_done, -1)

        def load_raw(sp, l, i, n):
            name, ee = (("moe_w_gate", 0), ("moe_w_up", 0), ("moe_w_gate", 1), ("moe_w_up", 1), ("moe_w_down", 0), ("moe_w_down", 1))[n // 4]
            w = t[name][l].rearrange("(q e) (k c p) n -> q e k p c n", e=2, k=4, p=P)
            src = w[i, ee, n % 4] if isinstance(i, int) else w[bass.ds(i, 1), ee, n % 4].rearrange("a p c n -> p (a c) n")
            sp.dma_start(work["raw"][:, n % RAW], src).then_inc(sem(f"slab{n % RAW}"), 16)

        def experts(l):
            raw, wh, wl, htok, oh, ohp, ohg, gs, gp, xs0, xs1, ys, yp = (work[k] for k in (
                "raw", "wh", "wl", "htok", "oh", "ohp", "ohg", "gs", "gp", "xs0", "xs1", "ys", "yp"))
            hf = h[:, :, :].rearrange("p c n -> p (c n)")
            hid = hf[:, 0:D]
            th = hf[:, D:2 * D]
            slp = hf[:, 2 * D:2 * D + 2 * NT].rearrange("p (t e) -> p t e", e=2)
            afp = hf[:, 2 * D + 16:2 * D + 16 + 2 * NT].rearrange("p (t e) -> p t e", e=2)
            half = hf[:, 2 * D + 32:2 * D + 34]
            iota = C("iota")
            XS = (xs0, xs1)
            M = (80, P)
            ROWS = (((0, CAPS), (CAPS, 80)), ((P - CAPS, P), (0, CAPP)))

            with stage() as block:
                @block.sync
                def _(sp):
                    for n in range(RAW - 2, RAW):
                        load_raw(sp, l, 0, n)
                    with sp.Fori(0, E // 2 - 1) as i:
                        for n in range(RAW, 24):
                            sp.wait_ge(sem("slab_free"), 1).then_inc(sem("slab_free"), -1)
                            load_raw(sp, l, i, n)
                        for n in range(RAW):
                            sp.wait_ge(sem("slab_free"), 1).then_inc(sem("slab_free"), -1)
                            load_raw(sp, l, i + 1, n)
                    for n in range(RAW, 24):
                        sp.wait_ge(sem("slab_free"), 1).then_inc(sem("slab_free"), -1)
                        load_raw(sp, l, E // 2 - 1, n)
                    sp.wait_ge(sem("slab_free"), RAW).then_inc(sem("slab_free"), -RAW)

                @block.gpsimd
                def _(pool):
                    for a in (xs1, ys, yp, gs, gp, ohg):
                        names = "abc"[:len(a.shape) - 1]
                        flat = a[:].rearrange(f"p {' '.join(names)} -> p ({' '.join(names)})") if len(names) > 1 else a[:]
                        pool.memset(flat.bitcast(F32), 0.0).then_inc(pool_done, 1)
                    pool.wait_ge(pool_done, 6).then_inc(pool_done, -6)
                    pool.sem_inc(sem("zeroed"), 1)
                    pool.sem_inc(sem("zeroed_act"), 1)
                    pool.sem_inc(sem("zeroed_dve"), 1)

                @block.tensor
                def _(pe):
                    NH = ((0, 512), (512, D))

                    def scatter_prompt():
                        for m in range(KC):
                            for k in range(2):
                                last = pe.matmul(ps[:, 6 + m // 4, (m % 4) * NP:(m % 4 + 1) * NP], yp[:, k, m * P:(m + 1) * P], gp[:, :], start=k == 0, stop=k == 1)
                        last.then_inc(sem("yp_ready"), 1)

                    def scatter(m):
                        if m >= 2:
                            pe.wait_ge(sem("y_read"), 1).then_inc(sem("y_read"), -1)
                        for k in range(2):
                            last = pe.matmul(ps[:, 4 + m % 2], ys[:, k, m * P:(m + 1) * P], gs[:, :], start=k == 0, stop=k == 1)
                        last.then_inc(sem("y_ready"), 1)

                    def two(b, c):
                        at = (c % 3) * 160
                        return ps[:, b, at:at + 192].rearrange("p (a s) -> p a s", a=2)[:, :, 0:CAPS]

                    def gather(chunks):
                        for c in chunks:
                            b = (0, 1, 6)[c // 3]
                            o = ps[:, b, (c % 3) * 160:(c % 3 + 1) * 160]
                            for tt in range(ST):
                                for k in range(2):
                                    lhs = htok[:, k, tt, c * P:(c + 1) * P]
                                    pe.matmul(two(b, c), lhs, oh[:, tt], start=tt + k == 0, stop=(tt, k) == (ST - 1, 1))
                            for k in range(2):
                                last = pe.matmul(o[:, CAPS:CAPS + 2 * CAPP], htok[:, k, ST, c * P:(c + 1) * P], ohp[:, :, :].rearrange("p e s -> p (e s)"), start=k == 0, stop=k == 1)
                            if c % 3 == 2 or c == KC - 1:
                                last.then_inc(sem("xs_ready"), 1)

                    def gather_weights():
                        for ee in range(2):
                            (a, b), (pa, pb) = ROWS[ee]
                            for tt in range(ST):
                                pe.matmul(ps[a:b, 7, ee:ee + 1], oh[:, tt, ee].bitcast(F32), afp[:, tt, ee:ee + 1], start=tt == 0, stop=tt == ST - 1)
                            last = pe.matmul(ps[pa:pb, 7, ee:ee + 1], ohp[:, ee].bitcast(F32), afp[:, ST, ee:ee + 1], start=True, stop=True)
                        last.then_inc(sem("weights_ready"), 1)

                    def piece(n, lhs, m, b0):
                        c, s = n % KC, n % SPLIT
                        pe.wait_ge(sem("low_ready"), 1).then_inc(sem("low_ready"), -1)
                        if n % 2:
                            pe.sem_inc(sem("slab_free"), 1)
                        for xk, w in ((0, wh), (0, wl), (1, wh)):
                            for k, (a, b) in enumerate(NH):
                                last = pe.matmul(ps[0:m, b0 + k], lhs[:, xk, c, 0:m], w[:, s, a:b],
                                                start=c == 0 and xk == 0 and w is wh, stop=c == KC - 1 and xk == 1)
                        last.then_inc(sem("split_free"), 1)
                        if c == KC - 1:
                            pe.drain().then_inc(sem("acc_ready"), 1)

                    pe.sem_inc(sem("split_free"), SPLIT)
                    pe.wait_ge(sem("zeroed"), 1).then_inc(sem("zeroed"), -1)
                    scatter(0)
                    scatter(1)
                    pe.wait_ge(sem("onehot_ready"), 1).then_inc(sem("onehot_ready"), -1)
                    gather(range(KC))
                    gather_weights()
                    with pe.Fori(0, E // 2) as i:
                        for n in range(PIECES):
                            mat, ee = n // KC, ((0, 0, 1, 1, 0, 1)[n // KC])
                            if n == 0:
                                pe.wait_ge(sem("xs_copied"), 1).then_inc(sem("xs_copied"), -1)
                            if n == 16:
                                pe.wait_ge(sem("y_read"), 2).then_inc(sem("y_read"), -2)
                            if n == 24:
                                pe.wait_ge(sem("yp_read"), 1).then_inc(sem("yp_read"), -1)
                            if n == 32:
                                pe.wait_ge(sem("hT_ready"), 1).then_inc(sem("hT_ready"), -1)
                            if n == 40:
                                pe.wait_ge(sem("hT_ready"), 1).then_inc(sem("hT_ready"), -1)
                            if mat < 4:
                                piece(n, XS[ee], M[ee], 2 * mat)
                            else:
                                piece(n, XS[ee], M[ee], 2 + 2 * ee)
                            if n == 0:
                                scatter_prompt()
                            if n < 12 and n % 2:
                                scatter(2 + n // 2)
                            if n in (25, 37):
                                pe.wait_ge(sem("hid_ready"), 1).then_inc(sem("hid_ready"), -1)
                                for c in range(KC):
                                    last = pe.transpose(ps[:, c // 4, (c % 4) * P:(c % 4) * P + (80 if n == 25 else P)],
                                                       hid[0:(80 if n == 25 else P), c * P:(c + 1) * P], ident[0:(80 if n == 25 else P), 0:(80 if n == 25 else P)])
                                last.then_inc(sem("hidT_ready"), 1)
                            if n == 37:
                                pe.wait_ge(sem("hid_read"), 1).then_inc(sem("hid_read"), -1)
                                for tt in range(ST):
                                    pe.transpose(ps[:, 6, tt * P:(tt + 1) * P], oh[:, tt].rearrange("p e s -> p (e s)").bitcast(F32), ident)
                                pe.transpose(ps[0:80, 7, 0:NP], ohg[:, :].bitcast(F32), ident).then_inc(sem("g_ready"), 1)
                            if n == 41:
                                pe.wait_ge(sem("g_copied"), 1).then_inc(sem("g_copied"), -1)
                                pe.wait_ge(sem("onehot_ready"), 1).then_inc(sem("onehot_ready"), -1)
                            if n > 40:
                                gather((n - 41,) if n < 47 else (6, 7))
                        gather_weights()
                        pe.wait_ge(sem("ys_copied"), 1).then_inc(sem("ys_copied"), -1)
                        scatter(0)
                        scatter(1)
                    pe.wait_ge(sem("xs_copied"), 1).then_inc(sem("xs_copied"), -1)
                    scatter_prompt()
                    for m in range(2, KC):
                        scatter(m)
                    pe.wait_ge(sem("y_read"), 2).then_inc(sem("y_read"), -2)
                    pe.wait_ge(sem("yp_read"), 1).then_inc(sem("yp_read"), -1)

                @block.scalar
                def _(act):

                    def copy_xs():
                        for n in range(3):
                            act.wait_ge(sem("xs_ready"), 1).then_inc(sem("xs_ready"), -1)
                            c0, w = 3 * n, 3 if n < 2 else 2
                            src = ps[:, (0, 1, 6)[n], 0:w * 160].rearrange("p (c s) -> p c s", c=w)
                            act.activation(xs0[:, 0, c0:c0 + w], src[:, :, 0:80], ACT.Copy).then_inc(act_done, 1)
                            act.activation(xs1[:, 0, c0:c0 + w, 0:CAPP], src[:, :, 80:96], ACT.Copy).then_inc(act_done, 1)
                            act.activation(xs1[:, 0, c0:c0 + w, P - CAPS:P], src[:, :, 96:160], ACT.Copy).then_inc(act_done, 1)
                            act.wait_ge(act_done, 3).then_inc(act_done, -3)
                            act.sem_inc(sem("xs_high"), 1)

                    def high(n):
                        if n % 2 == 0:
                            act.wait_ge(sem(f"slab{n // 2 % RAW}"), 16).then_inc(sem(f"slab{n // 2 % RAW}"), -16)
                        act.wait_ge(sem("split_free"), 1).then_inc(sem("split_free"), -1)
                        act.activation(wh[:, n % SPLIT], raw[:, n // 2 % RAW, n % 2], ACT.Copy).then_inc(sem("high_ready"), 1)

                    act.wait_ge(sem("zeroed_act"), 1).then_inc(sem("zeroed_act"), -1)
                    copy_xs()
                    with act.Fori(0, E // 2) as i:
                        for n in range(PIECES):
                            high(n)
                            if n in (21, 37):
                                ee = n // 37
                                act.wait_ge(sem("acc_ready"), 2).then_inc(sem("acc_ready"), -2)
                                act.activation(th[0:M[ee]], ps[0:M[ee], 4 * ee:4 * ee + 2].rearrange("p b n -> p (b n)"), ACT.Tanh, scale=0.5).then_inc(sem("tanh_ready"), 1)
                            if n in (31, 40):
                                ee = n // 40
                                act.wait_ge(sem("hidT_ready"), 1).then_inc(sem("hidT_ready"), -1)
                                act.activation(XS[ee][:, 0], ps[:, 0:2].rearrange("p b (c s) -> p (b c) s", c=4)[:, :, 0:M[ee]], ACT.Copy).then_inc(sem("hT_high"), 1)
                            if n == 40:
                                act.wait_ge(sem("g_ready"), 1).then_inc(sem("g_ready"), -1)
                                act.activation(gs[:, :], ps[:, 6], ACT.Copy).then_inc(act_done, 1)
                                act.activation(gp[:, :], ps[0:80, 7, 0:NP], ACT.Copy).then_inc(act_done, 1)
                                act.wait_ge(act_done, 2).then_inc(act_done, -2)
                                act.sem_inc(sem("g_copied"), 1)
                                act.sem_inc(sem("g_copied_dve"), 1)
                            if n in (45, 47):
                                ee = n // 46
                                act.wait_ge(sem("acc_ready"), 1).then_inc(sem("acc_ready"), -1)
                                (a, b), (pa, pb) = ROWS[ee]
                                src = ps[:, 2 + 2 * ee:4 + 2 * ee].rearrange("p b n -> p (b n)")
                                act.activation(ys[a:b, 0], src[a:b], ACT.Copy).then_inc(act_done, 1)
                                act.activation(yp[pa:pb, 0], src[pa:pb], ACT.Copy).then_inc(act_done, 1)
                                act.wait_ge(act_done, 2).then_inc(act_done, -2)
                                act.sem_inc(sem("ys_high"), 1)
                        copy_xs()
                    act.wait_ge(sem("split_free"), SPLIT).then_inc(sem("split_free"), -SPLIT)

                @block.vector
                def _(dve):

                    def onehot(i):
                        for dst, src in ((slp, slot), (afp, aff)):
                            v = src[:, :, :].rearrange("p t (q e) -> p q t e", e=2)
                            v = v[:, i] if isinstance(i, int) else v[:, bass.ds(i, 1)].rearrange("p a t e -> p (a t) e")
                            dve.tensor_scalar(dst, v, 0.0, None, ALU.add).then_inc(dve_done, 1)
                        dve.wait_ge(dve_done, 2).then_inc(dve_done, -2)
                        dve.tensor_tensor(oh[:, :, :, :], bcast(bcast(iota, 1, 2), 1, ST), bcast(slp[:, 0:ST], 3, CAPS), ALU.is_equal).then_inc(dve_done, 1)
                        dve.tensor_tensor(ohp[:, :, :], bcast(iota[:, 0:CAPP], 1, 2), bcast(slp[:, ST], 2, CAPP), ALU.is_equal).then_inc(dve_done, 1)
                        dve.tensor_scalar(ohg[:, CAPS:80], iota[:, 0:CAPP], slp[:, ST, 0:1], None, ALU.is_equal).then_inc(dve_done, 1)
                        dve.tensor_scalar(ohg[:, 0:CAPP], iota[:, 0:CAPP], slp[:, ST, 1:2], None, ALU.is_equal).then_inc(dve_done, 1)
                        dve.wait_ge(dve_done, 4).then_inc(dve_done, -4)
                        dve.sem_inc(sem("onehot_ready"), 1)

                    def low_xs():
                        for n in range(3):
                            dve.wait_ge(sem("xs_high"), 1).then_inc(sem("xs_high"), -1)
                            c0, w = 3 * n, 3 if n < 2 else 2
                            src = ps[:, (0, 1, 6)[n], 0:w * 160].rearrange("p (c s) -> p c s", c=w)
                            for dst, lo, a, b in ((xs0, 0, 0, 80), (xs1, 0, 80, 96), (xs1, P - CAPS, 96, 160)):
                                dve.tensor_tensor(dst[:, 1, c0:c0 + w, lo:lo + b - a], src[:, :, a:b], dst[:, 0, c0:c0 + w, lo:lo + b - a].bitcast(F32), ALU.subtract).then_inc(dve_done, 1)
                        dve.wait_ge(sem("weights_ready"), 1).then_inc(sem("weights_ready"), -1)
                        for ee in range(2):
                            for a, b in ROWS[ee]:
                                dve.tensor_scalar(half[a:b, ee:ee + 1], ps[a:b, 7, ee:ee + 1], 0.5, None, ALU.mult).then_inc(dve_done, 1)
                        dve.wait_ge(dve_done, 13).then_inc(dve_done, -13)
                        dve.sem_inc(sem("xs_copied"), 1)

                    def low(n):
                        dve.wait_ge(sem("high_ready"), 1).then_inc(sem("high_ready"), -1)
                        dve.tensor_tensor(wl[:, n % SPLIT], raw[:, n // 2 % RAW, n % 2], wh[:, n % SPLIT].bitcast(F32), ALU.subtract).then_inc(sem("low_ready"), 1)

                    dve.memset(half, 0.0).then_inc(dve_done, 1)
                    dve.wait_ge(dve_done, 1).then_inc(dve_done, -1)
                    dve.wait_ge(sem("zeroed_dve"), 1).then_inc(sem("zeroed_dve"), -1)
                    onehot(0)
                    low_xs()
                    with dve.Fori(0, E // 2) as i:
                        for n in range(PIECES):
                            low(n)
                            if n in (5, 9):
                                if n == 5:
                                    dve.wait_ge(sem("yp_ready"), 1).then_inc(sem("yp_ready"), -1)
                                for m in range(4 * (n // 9), 4 * (n // 9) + 4):
                                    dve.scalar_tensor_tensor(x[:, m, NS:T], ps[:, 6 + m // 4, (m % 4) * NP:(m % 4 + 1) * NP], mod[:, l, 5, m, 1:2],
                                                                x[:, m, NS:T], ALU.mult, ALU.add).then_inc(dve_done, 1)
                                dve.wait_ge(dve_done, 4).then_inc(dve_done, -4)
                                if n == 9:
                                    dve.sem_inc(sem("yp_read"), 1)
                            if n in (1, 3, 6, 8, 10, 12, 14, 16):
                                m = (1, 3, 6, 8, 10, 12, 14, 16).index(n)
                                dve.wait_ge(sem("y_ready"), 1).then_inc(sem("y_ready"), -1)
                                dve.scalar_tensor_tensor(x[:, m, 0:NS], ps[:, 4 + m % 2], mod[:, l, 5, m, 0:1], x[:, m, 0:NS], ALU.mult, ALU.add).then_inc(sem("y_read"), 1)
                            if n in (21, 37):
                                ee = n // 37
                                mm = M[ee]
                                dve.wait_ge(sem("tanh_ready"), 1).then_inc(sem("tanh_ready"), -1)
                                g = ps[0:mm, 4 * ee:4 * ee + 2].rearrange("p b n -> p (b n)")
                                u = ps[0:mm, 4 * ee + 2:4 * ee + 4].rearrange("p b n -> p (b n)")
                                dve.scalar_tensor_tensor(th[0:mm], th[0:mm], 1.0, g, ALU.add, ALU.mult).then_inc(dve_done, 1)
                                dve.wait_ge(dve_done, 1).then_inc(dve_done, -1)
                                dve.scalar_tensor_tensor(hid[0:mm], th[0:mm], half[0:mm, ee:ee + 1], u, ALU.mult, ALU.mult).then_inc(dve_done, 1)
                                dve.wait_ge(dve_done, 1).then_inc(dve_done, -1)
                                dve.sem_inc(sem("hid_ready"), 1)
                                if ee:
                                    dve.sem_inc(sem("hid_read"), 1)
                            if n in (31, 40):
                                ee = n // 40
                                mm, hT = M[ee], XS[ee]
                                dve.wait_ge(sem("hT_high"), 1).then_inc(sem("hT_high"), -1)
                                dve.tensor_tensor(hT[:, 1], ps[:, 0:2].rearrange("p b (c s) -> p (b c) s", c=4)[:, :, 0:mm], hT[:, 0].bitcast(F32), ALU.subtract).then_inc(sem("hT_ready"), 1)
                            if n in (45, 47):
                                ee = n // 46
                                dve.wait_ge(sem("ys_high"), 1).then_inc(sem("ys_high"), -1)
                                (a, b), (pa, pb) = ROWS[ee]
                                src = ps[:, 2 + 2 * ee:4 + 2 * ee].rearrange("p b n -> p (b n)")
                                dve.tensor_tensor(ys[a:b, 1], src[a:b], ys[a:b, 0].bitcast(F32), ALU.subtract).then_inc(dve_done, 1)
                                dve.tensor_tensor(yp[pa:pb, 1], src[pa:pb], yp[pa:pb, 0].bitcast(F32), ALU.subtract).then_inc(dve_done, 1)
                                dve.wait_ge(dve_done, 2).then_inc(dve_done, -2)
                                if ee:
                                    dve.sem_inc(sem("ys_copied"), 1)
                            if n == 40:
                                dve.wait_ge(sem("g_copied_dve"), 1).then_inc(sem("g_copied_dve"), -1)
                                onehot(i + 1)
                        low_xs()
                    dve.wait_ge(sem("yp_ready"), 1).then_inc(sem("yp_ready"), -1)
                    for m in range(KC):
                        dve.scalar_tensor_tensor(x[:, m, NS:T], ps[:, 6 + m // 4, (m % 4) * NP:(m % 4 + 1) * NP], mod[:, l, 5, m, 1:2],
                                                    x[:, m, NS:T], ALU.mult, ALU.add).then_inc(dve_done, 1)
                    dve.wait_ge(dve_done, 8).then_inc(dve_done, -8)
                    dve.sem_inc(sem("yp_read"), 1)
                    for m in range(KC):
                        dve.wait_ge(sem("y_ready"), 1).then_inc(sem("y_ready"), -1)
                        dve.scalar_tensor_tensor(x[:, m, 0:NS], ps[:, 4 + m % 2], mod[:, l, 5, m, 0:1], x[:, m, 0:NS], ALU.mult, ALU.add).then_inc(dve_done, 1)
                        dve.wait_ge(dve_done, 1).then_inc(dve_done, -1)
                        dve.sem_inc(sem("y_read"), 1)

        def odd_mixer():
            PADW = 15
            W = T + 4 * PADW
            WO = W - 2 * PADW
            OFF = NS + 2 * PADW
            mix = work["mix"]
            cv = Carve()
            win = cv(KC, 2048)
            xp = cv(4, W)
            acc = cv(4, WO)
            vn = cv(4, T)
            vtok = cv(NT, 512)
            ws = cv(4, P)
            bs = cv(4, P, parts=1)
            th = cv(2, T)
            sq = cv(2, T)
            root = cv(T)
            rp = root
            tho = th[:, 0]
            cw = V("conv_w").rearrange("p (c k) -> p c k", c=4)
            tiles = [m for c in range(4) for m in (4 + c, c)] + [12, 13, 14, 15, 8, 9, 10, 11]

            def seg(ap, off):
                return ap[:, 0:NS], ap[:, off:off + NP]

            with stage() as block:
                @block.sync
                def _(sp):
                    for k in range(4):
                        src = t["od_w_in"].rearrange("(c p) (k n) -> k p c n", p=P, k=4)
                        for q in ((1, 0, 3, 2)[k],):
                            sp.dma_start(win[:, :, q * 512:(q + 1) * 512], src[q]).then_inc(sem(f"win{q}"), 16)
                    sp.dma_start(ws, t["ws"].rearrange("p (h n) -> p h n", h=4)).then_inc(sem("ws_in"), 16)
                    sp.dma_start(bs, t["bs"].rearrange("a (h n) -> a h n", h=4)).then_inc(sem("ws_in"), 16)

                @block.tensor
                def _(pe):
                    for n, m in enumerate(tiles):
                        if n == 0:
                            pe.wait_ge(sem("win1"), 16).then_inc(sem("win1"), -16)
                            pe.wait_ge(sem("win0"), 16).then_inc(sem("win0"), -16)
                        if n == 8:
                            pe.wait_ge(sem("win3"), 16).then_inc(sem("win3"), -16)
                        if n == 12:
                            pe.wait_ge(sem("win2"), 16).then_inc(sem("win2"), -16)
                        if n >= 3:
                            pe.wait_ge(sem("tile_read_a" if n - 3 < 8 and (n - 3) % 2 else "tile_read"), 1).then_inc(sem("tile_read_a" if n - 3 < 8 and (n - 3) % 2 else "tile_read"), -1)
                        for a, b in ((0, NS), (NS, T)):
                            for c in range(KC):
                                last = pe.matmul(pair(n % 3)[:, a:b], win[:, c, m * P:(m + 1) * P], h[:, c, a:b], start=c == 0, stop=c == KC - 1)
                        last.then_inc(sem("tile_b" if n < 8 and n % 2 == 0 else "tile_a" if n < 8 else "tile_vu"), 1)
                    pe.wait_ge(sem("tile_read"), 3).then_inc(sem("tile_read"), -3)

                    def layer_mean(src, tag):
                        for c in range(4):
                            pe.wait_ge(sem(tag + "_in"), 1).then_inc(sem(tag + "_in"), -1)
                            for (a, b), s in zip(((0, NS), (NS, T)), src(c)):
                                last = pe.matmul(pair(3)[:, a:b], mean512[:, :], s, start=c == 0, stop=c == 3)
                            if tag.endswith("sq"):
                                last.then_inc(sem(tag + "_used"), 1)
                        pe.drain().then_inc(sem(tag + "_mean"), 1)

                    pe.wait_ge(sem("ws_in"), 32).then_inc(sem("ws_in"), -32)
                    layer_mean(lambda c: (vn[:, c, 0:NS], vn[:, c, NS:T]), "v")
                    pe.wait_ge(sem("v_mean_read"), 1).then_inc(sem("v_mean_read"), -1)
                    layer_mean(lambda c: (sq[:, c % 2, 0:NS], sq[:, c % 2, NS:T]), "vsq")
                    pe.wait_ge(sem("vsq_mean_read"), 1).then_inc(sem("vsq_mean_read"), -1)
                    pe.wait_ge(sem("vn_done"), 1).then_inc(sem("vn_done"), -1)
                    for tt in range(NT):
                        if tt >= 2:
                            pe.wait_ge(sem("vtok_copied"), 1).then_inc(sem("vtok_copied"), -1)
                        for c in range(4):
                            last = pe.transpose(ps[:, tt % 2, c * P:(c + 1) * P], vn[:, c, tt * P:(tt + 1) * P], ident)
                        last.then_inc(sem("vtok_ready"), 1)
                    pe.wait_ge(sem("vtok_copied"), 2).then_inc(sem("vtok_copied"), -2)
                    pe.wait_ge(sem("vtok_all"), 1).then_inc(sem("vtok_all"), -1)
                    for hd in range(4):
                        if hd >= 2:
                            pe.wait_ge(sem("mixed_read"), 1).then_inc(sem("mixed_read"), -1)
                        q = 1 + hd % 2
                        for tt in range(NT):
                            o = pair(q)[:, tt * P:(tt + 1) * P]
                            pe.matmul(o, vtok[:, tt, hd * P:(hd + 1) * P], ws[:, hd], start=True, stop=False)
                            last = pe.matmul(o, ones[0:1, :], bs[:, hd], start=False, stop=True)
                        last.then_inc(sem("mixed_ready"), 1)
                    pe.wait_ge(sem("mixed_read"), 2).then_inc(sem("mixed_read"), -2)
                    layer_mean(lambda c: seg(acc[:, c], OFF), "c")
                    pe.wait_ge(sem("c_mean_read"), 1).then_inc(sem("c_mean_read"), -1)
                    layer_mean(lambda c: (sq[:, c % 2, 0:NS], sq[:, c % 2, NS:T]), "csq")
                    pe.wait_ge(sem("csq_mean_read"), 1).then_inc(sem("csq_mean_read"), -1)

                @block.scalar
                def _(act):
                    for c in range(4):
                        act.wait_ge(sem("tile_b"), 1).then_inc(sem("tile_b"), -1)
                        if c >= 2:
                            act.wait_ge(sem("th_used"), 1).then_inc(sem("th_used"), -1)
                        act.activation(th[:, c % 2], pair(2 * c % 3), ACT.Tanh, scale=0.5).then_inc(act_done, 1)
                        act.wait_ge(act_done, 1).then_inc(act_done, -1)
                        act.sem_inc(sem("tile_read"), 1)
                        act.sem_inc(sem("th_ready"), 1)
                    act.wait_ge(sem("th_used"), 2).then_inc(sem("th_used"), -2)
                    for n in range(8, 16):
                        act.wait_ge(sem("tile_vu"), 1).then_inc(sem("tile_vu"), -1)
                        out = vn[:, n - 8] if n < 12 else mix[:, n - 8]
                        act.activation(out, pair(n % 3), ACT.Gelu_apprx_tanh).then_inc(act_done, 1)
                        act.wait_ge(act_done, 1).then_inc(act_done, -1)
                        act.sem_inc(sem("tile_read"), 1)
                        if n < 12:
                            act.sem_inc(sem("v_in"), 1)
                    act.sem_inc(sem("gelu_done"), 1)

                    def var(src, tag):
                        for c in range(4):
                            act.wait_ge(sem(tag + "_centred"), 1).then_inc(sem(tag + "_centred"), -1)
                            if c >= 2:
                                act.wait_ge(sem(tag + "sq_used"), 1).then_inc(sem(tag + "sq_used"), -1)
                            for (a, b), s in zip(((0, NS), (NS, T)), src(c)):
                                act.activation(sq[:, c % 2, a:b], s, ACT.Square).then_inc(act_done, 1)
                            act.wait_ge(act_done, 2).then_inc(act_done, -2)
                            act.sem_inc(sem(tag + "sq_in"), 1)
                        act.wait_ge(sem(tag + "sq_used"), 2).then_inc(sem(tag + "sq_used"), -2)
                        act.wait_ge(sem(tag + "sq_mean"), 1).then_inc(sem(tag + "sq_mean"), -1)
                        act.activation(root, pair(3), ACT.Sqrt, bias=eps[:, 1:2]).then_inc(act_done, 1)
                        act.wait_ge(act_done, 1).then_inc(act_done, -1)
                        act.sem_inc(sem(tag + "_root"), 1)
                        act.sem_inc(sem(tag + "sq_mean_read"), 1)

                    var(lambda c: (vn[:, c, 0:NS], vn[:, c, NS:T]), "v")
                    for c in range(4):
                        act.wait_ge(sem("v_scaled"), 1).then_inc(sem("v_scaled"), -1)
                        act.activation(vn[:, c], vn[:, c], ACT.Identity, scale=V("vln_g", c, c + 1), bias=V("vln_b", c, c + 1)).then_inc(act_done, 1)
                    act.wait_ge(act_done, 4).then_inc(act_done, -4)
                    act.sem_inc(sem("vn_done"), 1)
                    for tt in range(NT):
                        act.wait_ge(sem("vtok_ready"), 1).then_inc(sem("vtok_ready"), -1)
                        act.activation(vtok[:, tt], ps[:, tt % 2], ACT.Copy).then_inc(act_done, 1)
                        act.wait_ge(act_done, 1).then_inc(act_done, -1)
                        act.sem_inc(sem("vtok_copied"), 1)
                    act.sem_inc(sem("vtok_all"), 1)
                    var(lambda c: seg(acc[:, c], OFF), "c")
                    for c in range(4):
                        act.wait_ge(sem("c_scaled"), 1).then_inc(sem("c_scaled"), -1)
                        act.activation(acc[:, c], acc[:, c], ACT.Identity, scale=V("cln_g", c, c + 1), bias=V("cln_b", c, c + 1)).then_inc(act_done, 1)
                        act.wait_ge(act_done, 1).then_inc(act_done, -1)
                        if c:
                            act.wait_ge(sem("tho_used"), 1).then_inc(sem("tho_used"), -1)
                        for (a, b), s in zip(((0, NS), (NS, T)), seg(acc[:, c], OFF)):
                            act.activation(tho[:, a:b], s, ACT.Tanh, scale=0.5).then_inc(act_done, 1)
                        act.wait_ge(act_done, 2).then_inc(act_done, -2)
                        act.sem_inc(sem("tho_ready"), 1)
                    act.wait_ge(sem("tho_used"), 1).then_inc(sem("tho_used"), -1)

                @block.gpsimd
                def _(pool):
                    pool.memset(xp, 0.0).then_inc(pool_done, 1)
                    pool.wait_ge(pool_done, 1).then_inc(pool_done, -1)
                    pool.sem_inc(sem("xp_zero"), 1)

                @block.vector
                def _(dve):
                    dve.wait_ge(sem("xp_zero"), 1).then_inc(sem("xp_zero"), -1)
                    for c in range(4):
                        dve.wait_ge(sem("tile_a"), 1).then_inc(sem("tile_a"), -1)
                        dve.wait_ge(sem("th_ready"), 1).then_inc(sem("th_ready"), -1)
                        for (a, b), s in zip(((0, NS), (NS, T)), seg(xp[:, c, PADW:W - PADW], OFF)):
                            dve.scalar_tensor_tensor(s, th[:, c % 2, a:b], 1.0, pair((2 * c + 1) % 3)[:, a:b], ALU.add, ALU.mult).then_inc(dve_done, 1)
                        dve.wait_ge(dve_done, 2).then_inc(dve_done, -2)
                        dve.sem_inc(sem("tile_read_a"), 1)
                        dve.sem_inc(sem("th_used"), 1)
                    dve.tensor_scalar(xp, xp, 0.5, None, ALU.mult).then_inc(dve_done, 1)
                    dve.wait_ge(dve_done, 1).then_inc(dve_done, -1)
                    for k in range(TAPS):
                        for c in range(4):
                            src = xp[:, c, k:k + WO]
                            if k == 0:
                                dve.tensor_scalar(acc[:, c], src, cw[:, c, 0:1], V("conv_b", c, c + 1), ALU.mult, ALU.add).then_inc(dve_done, 1)
                            else:
                                dve.scalar_tensor_tensor(acc[:, c], src, cw[:, c, k:k + 1], acc[:, c], ALU.mult, ALU.add).then_inc(dve_done, 1)
                        dve.wait_ge(dve_done, 4).then_inc(dve_done, -4)

                    def centre(dst, tag):
                        dve.wait_ge(sem(tag + "_mean"), 1).then_inc(sem(tag + "_mean"), -1)
                        for c in range(4):
                            for (a, b), s in zip(((0, NS), (NS, T)), dst(c)):
                                dve.tensor_tensor(s, s, pair(3)[:, a:b], ALU.subtract).then_inc(dve_done, 1)
                            dve.wait_ge(dve_done, 2).then_inc(dve_done, -2)
                            dve.sem_inc(sem(tag + "_centred"), 1)
                        dve.sem_inc(sem(tag + "_mean_read"), 1)

                    def scale(dst, tag):
                        dve.wait_ge(sem(tag + "_root"), 1).then_inc(sem(tag + "_root"), -1)
                        dve.reciprocal(rp, root).then_inc(dve_done, 1)
                        dve.wait_ge(dve_done, 1).then_inc(dve_done, -1)
                        for c in range(4):
                            for (a, b), s in zip(((0, NS), (NS, T)), dst(c)):
                                dve.tensor_tensor(s, s, rp[:, a:b], ALU.mult).then_inc(dve_done, 1)
                            dve.wait_ge(dve_done, 2).then_inc(dve_done, -2)
                            dve.sem_inc(sem(tag + "_scaled"), 1)

                    vd = lambda c: (vn[:, c, 0:NS], vn[:, c, NS:T])
                    cd = lambda c: seg(acc[:, c], OFF)
                    centre(vd, "v")
                    scale(vd, "v")
                    dve.wait_ge(sem("gelu_done"), 1).then_inc(sem("gelu_done"), -1)
                    for hd in range(4):
                        dve.wait_ge(sem("mixed_ready"), 1).then_inc(sem("mixed_ready"), -1)
                        dve.tensor_tensor(mix[:, 4 + hd], mix[:, 4 + hd], pair(1 + hd % 2), ALU.mult).then_inc(dve_done, 1)
                        dve.wait_ge(dve_done, 1).then_inc(dve_done, -1)
                        dve.sem_inc(sem("mixed_read"), 1)
                    dve.sem_inc(sem("c_in"), 4)
                    centre(cd, "c")
                    scale(cd, "c")
                    for c in range(4):
                        dve.wait_ge(sem("tho_ready"), 1).then_inc(sem("tho_ready"), -1)
                        for (a, b), s in zip(((0, NS), (NS, T)), cd(c)):
                            dve.scalar_tensor_tensor(mix[:, c, a:b], tho[:, a:b], 1.0, s, ALU.add, ALU.mult).then_inc(dve_done, 1)
                        dve.wait_ge(dve_done, 2).then_inc(dve_done, -2)
                        dve.sem_inc(sem("tho_used"), 1)
                        dve.tensor_scalar(mix[:, c], mix[:, c], 0.5, None, ALU.mult).then_inc(dve_done, 1)
                        dve.wait_ge(dve_done, 1).then_inc(dve_done, -1)

        def fill(l):
            def go(sp):
                for n in range(RAW - 2):
                    load_raw(sp, l, 0, n)
            return go

        with mixer_memory(0):
            setup()
            norm(0, 0)
            even_front()
            even_heads()
            out_proj(0, t["ev_w_out"])
        with expert_memory(0):
            norm(0, 1, fill(0))
            route(0, lambda sp: None)
            experts(0)
        with mixer_memory(1):
            norm(1, 0)
            odd_mixer()
            out_proj(1, t["od_w_out"])
        with expert_memory(1):
            norm(1, 1, fill(1))
            route(1, lambda sp: None)
            experts(1)
            norm(None, None)


def _constants():
    p = np.arange(P)
    cst = np.zeros((P, NCST), np.float32)

    def put(name, a):
        lo, hi = CST[name]
        cst[:, lo:hi] = np.asarray(a, np.float32).reshape(P, hi - lo)

    put("ident", np.eye(P))
    put("headones", (p[:, None] // HD == p[None, :] // HD))
    put("iota", np.broadcast_to(np.arange(64), (P, 64)))
    m = np.arange(64)
    ang = 2 * np.pi * ((m[:, None] * m[None, :]) % 64) / 64
    two = np.eye(2)
    put("dft64", np.concatenate([np.kron(two, np.cos(ang)), np.kron(two, -np.sin(ang))], axis=1))
    freq = (1.0 / (np.float32(10000.0) ** (np.arange(256, dtype=np.float32) / np.float32(256)))).astype(np.float32)
    ar = (freq[:, None] * np.arange(8, dtype=np.float32)[None]).astype(np.float32)
    ac = (freq[:, None] * np.arange(64, dtype=np.float32)[None]).astype(np.float32)
    row = np.concatenate([np.sin(ar), np.cos(ar)]).reshape(4, P, 8).transpose(1, 0, 2)
    col = np.concatenate([np.sin(ac), np.cos(ac)]).reshape(4, P, 64).transpose(1, 0, 2)
    put("posrow", row)
    put("poscol", col)
    s, t = p[:, None], p[None, :]
    tri = np.stack([np.concatenate([s < t, s <= t] * 2, axis=1), np.concatenate([s > t, s >= t] * 2, axis=1)], axis=1)
    put("tri", tri)
    m8 = np.zeros((P, LEVELS + 1, 2, P), np.float32)
    for lev in range(LEVELS + 1):
        b = 2 ** lev
        same = (s // (2 * b) == t // (2 * b)) & (s // b != t // b)
        m8[:, lev, 0] = same & (s < t)
        m8[:, lev, 1] = same & (s > t)

    def dft(n):
        k = np.arange(n)
        a = 2 * np.pi * ((k[:, None] * k[None, :]) % n) / n
        both = np.stack([np.cos(a), np.sin(a)], axis=1) / np.sqrt(n * 64.0)
        return both.reshape(n // P, P, 2, n).transpose(1, 0, 2, 3).reshape(P, -1).astype(np.float32)

    return {"cst": cst, "m8": m8.reshape(P, -1), "dft_s": dft(NS), "dft_p": dft(NP)}


def kernel(**inputs):
    import concourse.bacc as _bacc
    from concourse.bass_utils import run_bass_kernel_spmd as _run

    a = {k: np.asarray(v) for k, v in inputs.items()}

    def cols(v):
        return v.reshape(-1, P).T

    vec = np.concatenate([
        cols(a["mod_b"]), cols(a["norm_mix"]), cols(a["norm_ffn"]), cols(a["final_norm"]), cols(a["ev_mu_wag"]),
        np.stack([cols(a["c"]), cols(a["c_ctx"])], axis=2).reshape(P, 16),
        a["od_conv_w"][0].T.reshape(4, P, TAPS).transpose(1, 0, 2).reshape(P, -1),
        cols(a["od_conv_b"]), cols(a["od_cln_g"]), cols(a["od_cln_b"]), cols(a["od_vln_g"]), cols(a["od_vln_b"]),
    ], axis=1)
    heads = [a["ev_mu_rkv"][0, 0], a["ev_mu_rkv"][0, 1], a["ev_mu_rkv"][0, 2], a["ev_w0"][0, 0], a["ev_w0"][0, 1],
             a["ev_a0"][0, 0], a["ev_a0"][0, 1], a["ev_k_k"][0], a["ev_k_a"][0], a["ev_r_k"][0].reshape(-1),
             a["ev_gn_w"][0], a["ev_gn_b"][0]]
    dirs = lambda w: w[0].transpose(1, 0, 2).reshape(D, P)
    arrays = {
        "xT": np.concatenate([a["x_sample"][0], a["x_prompt"][0]], axis=0).T,
        "vec": vec,
        "hpv": np.stack(heads, axis=1).reshape(HP, P, NHPV),
        "state": a["state_wkv"][0, 0].transpose(0, 1, 3, 2).reshape(2, HP, P, HD),
        "lora1": np.concatenate([dirs(a["ev_w1"]), dirs(a["ev_a1"]), a["ev_g1"][0]], axis=1),
        "lora2": np.stack([a["ev_w2"][0].reshape(P, -1), a["ev_a2"][0].reshape(P, -1), a["ev_g2"][0]]),
        "router": a["moe_router"], "router_b": a["moe_router_b"],
        "ws": a["od_w_s"][0].transpose(2, 0, 1).reshape(P, 512), "bs": a["od_b_s"].reshape(1, 512),
        "ev_w_in": a["ev_w_in"][0], "ev_w_out": a["ev_w_out"][0], "od_w_in": a["od_w_in"][0], "od_w_out": a["od_w_out"][0],
        "mod_w": a["mod_w"], "moe_w_gate": a["moe_w_gate"], "moe_w_up": a["moe_w_up"], "moe_w_down": a["moe_w_down"],
        **_constants(),
    }
    arrays = {k: np.ascontiguousarray(v) for k, v in arrays.items()}
    nc = _bacc.Bacc("TRN2", target_bir_lowering=False, num_devices=1)
    t = {k: nc.dram_tensor("in_" + k, v.shape, mybir.dt.from_np(v.dtype), kind="ExternalInput").ap() for k, v in arrays.items()}
    t["yT"] = nc.dram_tensor("out_y", (D, T), F32, kind="ExternalOutput").ap()
    t["st_out"] = nc.dram_tensor("out_state", (2, HP, P, HD), F32, kind="ExternalOutput").ap()
    build(nc, t)
    r = _run(nc, [{"in_" + k: v for k, v in arrays.items()}], core_ids=[0]).results[0]
    y = np.asarray(r["out_y"]).T
    state = np.asarray(r["out_state"]).reshape(2, 2 * HP, HD, HD).transpose(0, 1, 3, 2)
    return np.ascontiguousarray(y[NS:])[None], np.ascontiguousarray(y[:NS])[None], np.ascontiguousarray(state)[None, None]
```
